# Optimizing a Trainium2 kernel written in Bass

```python
import math
import jax, jax.numpy as jnp
from jax import lax
import numpy as np

D_MODEL = 1024
BATCH = 1
SEQ = 1024
DEPTH = 1
DEC_BATCH = 1
DEC_SEQ = 256
PAST_LEN = 128

HEAD_DIM = 64
N_HEADS = 8
N_KV_HEADS = 2
GQ = N_HEADS // N_KV_HEADS
Q_DIM = N_HEADS * HEAD_DIM
KV_DIM = N_KV_HEADS * HEAD_DIM
WINDOW = 128
BLK = 128
N_BUCKETS = 32
MAX_DISTANCE = 128
D_INNER = 1024
SSD_HEAD_DIM = 64
N_SSD_HEADS = D_INNER // SSD_HEAD_DIM
N_SSD_GROUPS = 2
HPG = N_SSD_HEADS // N_SSD_GROUPS
D_STATE = 64
CHUNK = 128
CONV_WIDTH = 5
CONV_PAD = CONV_WIDTH // 2
BC_DIM = N_SSD_GROUPS * D_STATE
CONV_DIM = D_INNER + 2 * BC_DIM
N_EGROUPS = 4
EXPERTS_PER_GROUP = 4
N_EXPERTS = N_EGROUPS * EXPERTS_PER_GROUP
TOP_K_INNER = 2
D_EXPERT = 256
PLE_DIM = 256
EPS = 1e-6

SPLIT_SIZES = [Q_DIM, KV_DIM, KV_DIM, D_INNER, CONV_DIM, N_SSD_HEADS, N_SSD_HEADS, D_MODEL, D_MODEL]
IN_COLS = int(sum(SPLIT_SIZES))
SPLITS = [int(s) for s in np.cumsum(SPLIT_SIZES)[:-1]]

kernel_name = "hybrid_swa_ssd_hmoe_encoder"

def rmsnorm(x, g):
    xf = x.astype(jnp.float32)
    y = xf * lax.rsqrt(jnp.mean(xf * xf, axis=-1, keepdims=True) + EPS)
    return (y * g.astype(jnp.float32)).astype(x.dtype)

def _t5_bucket_band():
    rel = (np.arange(3 * BLK)[None, :] - BLK) - np.arange(BLK)[:, None]
    nb = N_BUCKETS // 2
    max_exact = nb // 2
    ret = (rel > 0).astype(np.int32) * nb
    n = np.abs(rel)
    large = max_exact + (np.log(np.maximum(n, 1) / max_exact) / np.log(MAX_DISTANCE / max_exact)
                         * (nb - max_exact)).astype(np.int32)
    large = np.minimum(large, nb - 1)
    return (ret + np.where(n < max_exact, n, large)).astype(np.int32), rel

def band_bias(rel_bias):
    bucket, _ = _t5_bucket_band()
    b = rel_bias[jnp.asarray(bucket)]
    b = jnp.transpose(b, (2, 0, 1)).astype(jnp.float32)
    return b.reshape(N_KV_HEADS, GQ, BLK, 3 * BLK)

def windowed_gqa(q, k, v, sink, bias):
    b, l = q.shape[:2]
    nb = l // BLK
    qb = q.reshape(b, nb, BLK, N_KV_HEADS, GQ, HEAD_DIM).astype(jnp.float32)
    pad = ((0, 0), (BLK, BLK), (0, 0), (0, 0))
    kp = jnp.pad(k, pad).reshape(b, nb + 2, BLK, N_KV_HEADS, HEAD_DIM)
    vp = jnp.pad(v, pad).reshape(b, nb + 2, BLK, N_KV_HEADS, HEAD_DIM)
    kb = jnp.concatenate([kp[:, :-2], kp[:, 1:-1], kp[:, 2:]], axis=2).astype(jnp.float32)
    vb = jnp.concatenate([vp[:, :-2], vp[:, 1:-1], vp[:, 2:]], axis=2).astype(jnp.float32)
    _, rel = _t5_bucket_band()
    kpos = np.arange(nb)[:, None, None] * BLK - BLK + np.arange(3 * BLK)[None, None, :]
    valid = (np.abs(rel)[None] <= WINDOW) & (kpos >= 0) & (kpos < l)
    s = jnp.einsum('bnqhgd,bnjhd->bnhgqj', qb, kb) * (HEAD_DIM ** -0.5) + bias
    s = jnp.where(jnp.asarray(valid)[None, :, None, None], s, -1e30)
    sink6 = sink.astype(jnp.float32)[None, None, :, :, None, None]
    m = jnp.maximum(jnp.max(s, axis=-1, keepdims=True), sink6)
    pe = jnp.exp(s - m)
    den = jnp.sum(pe, axis=-1, keepdims=True) + jnp.exp(sink6 - m)
    o = jnp.einsum('bnhgqj,bnjhd->bnqhgd', pe / den, vb)
    return o.reshape(b, l, Q_DIM).astype(q.dtype)

def depthwise_conv(u, w, bconv):
    out = lax.conv_general_dilated(u, w[:, None, :], (1,), [(CONV_PAD, CONV_PAD)],
                                   dimension_numbers=('NWC', 'WIO', 'NWC'),
                                   feature_group_count=CONV_DIM)
    return out + bconv

def ssd_chunked(x, dt, A, B, C):
    b, l = x.shape[:2]
    nc = l // CHUNK
    x = x.astype(jnp.float32).reshape(b, nc, CHUNK, N_SSD_GROUPS, HPG, SSD_HEAD_DIM)
    dt = dt.reshape(b, nc, CHUNK, N_SSD_GROUPS, HPG)
    B = B.astype(jnp.float32).reshape(b, nc, CHUNK, N_SSD_GROUPS, D_STATE)
    C = C.astype(jnp.float32).reshape(b, nc, CHUNK, N_SSD_GROUPS, D_STATE)
    acs = jnp.cumsum(dt * A, axis=2)
    xdt = x * dt[..., None]
    tril = jnp.tril(jnp.ones((CHUNK, CHUNK), dtype=bool))
    seg = acs[:, :, :, None] - acs[:, :, None]
    Lmat = jnp.exp(jnp.where(tril[:, :, None, None], seg, -jnp.inf))
    cb = jnp.einsum('bcign,bcjgn->bcijg', C, B)
    y_diag = jnp.einsum('bcijg,bcijgh,bcjghp->bcighp', cb, Lmat, xdt)
    decay_states = jnp.exp(acs[:, :, -1:] - acs)
    states = jnp.einsum('bcjgn,bcjghp->bcghpn', B, xdt * decay_states[..., None])
    chunk_decay = jnp.exp(acs[:, :, -1])

    def step(h, inp):
        s, d = inp
        return h * d[..., None, None] + s, h

    h0 = jnp.zeros((b, N_SSD_GROUPS, HPG, SSD_HEAD_DIM, D_STATE), jnp.float32)
    _, h_prev = lax.scan(step, h0, (jnp.moveaxis(states, 1, 0), jnp.moveaxis(chunk_decay, 1, 0)))
    h_prev = jnp.moveaxis(h_prev, 0, 1)
    y_off = jnp.einsum('bcign,bcghpn->bcighp', C, h_prev) * jnp.exp(acs)[..., None]
    return (y_diag + y_off).reshape(b, l, N_SSD_GROUPS, HPG, SSD_HEAD_DIM)

def ssd_branch(z, xbc, dtf, dtb, conv_w, conv_b, a_log_f, a_log_b, dt_bias_f, dt_bias_b, d_skip, norm_g):
    b, l, _ = z.shape
    xbc = jax.nn.silu(depthwise_conv(xbc, conv_w, conv_b))
    xs, Bm, Cm = jnp.split(xbc, [D_INNER, D_INNER + BC_DIM], axis=-1)
    xs = xs.reshape(b, l, N_SSD_GROUPS, HPG, SSD_HEAD_DIM)
    Bm = Bm.reshape(b, l, N_SSD_GROUPS, D_STATE)
    Cm = Cm.reshape(b, l, N_SSD_GROUPS, D_STATE)
    dt_f = jax.nn.softplus((dtf + dt_bias_f).astype(jnp.float32)).reshape(b, l, N_SSD_GROUPS, HPG)
    dt_b = jax.nn.softplus((dtb + dt_bias_b).astype(jnp.float32)).reshape(b, l, N_SSD_GROUPS, HPG)
    A_f = -jnp.exp(a_log_f.astype(jnp.float32)).reshape(N_SSD_GROUPS, HPG)
    A_b = -jnp.exp(a_log_b.astype(jnp.float32)).reshape(N_SSD_GROUPS, HPG)
    fl = lambda t: jnp.flip(t, axis=1)
    y = ssd_chunked(xs, dt_f, A_f, Bm, Cm) + fl(ssd_chunked(fl(xs), fl(dt_b), A_b, fl(Bm), fl(Cm)))
    y = y + d_skip.astype(jnp.float32).reshape(N_SSD_GROUPS, HPG)[:, :, None] * xs.astype(jnp.float32)
    gsz = D_INNER // N_SSD_GROUPS
    y = y.reshape(b, l, N_SSD_GROUPS, gsz) * jax.nn.silu(z.astype(jnp.float32)).reshape(b, l, N_SSD_GROUPS, gsz)
    y = y * lax.rsqrt(jnp.mean(y * y, axis=-1, keepdims=True) + EPS)
    y = y * norm_g.astype(jnp.float32).reshape(N_SSD_GROUPS, gsz)
    return y.reshape(b, l, D_INNER).astype(z.dtype)

def hier_moe(h, router_g, router_g_b, router_e, router_e_b, w_gate_up, w_down):
    b, l, _ = h.shape
    lg = (h @ router_g + router_g_b).astype(jnp.float32)
    pg = jax.nn.softmax(lg, axis=-1)
    p_sel, g_sel = lax.top_k(pg, 1)
    le = (h @ router_e + router_e_b).astype(jnp.float32).reshape(b, l, N_EGROUPS, EXPERTS_PER_GROUP)
    le_sel = jnp.take_along_axis(le, g_sel[..., None], axis=2)[:, :, 0]
    pe = jax.nn.softmax(le_sel, axis=-1)
    vals, idx = lax.top_k(pe, TOP_K_INNER)
    vals = vals / jnp.sum(vals, axis=-1, keepdims=True)
    w_inner = jnp.sum(jax.nn.one_hot(idx, EXPERTS_PER_GROUP, dtype=jnp.float32) * vals[..., None], axis=-2)
    gates = (jax.nn.one_hot(g_sel[..., 0], N_EGROUPS, dtype=jnp.float32)[..., None]
             * w_inner[:, :, None, :] * p_sel[..., None]).reshape(b, l, N_EXPERTS).astype(h.dtype)

    def per_seq(args):
        hs, gs = args
        gu = jnp.einsum('ld,edf->lef', hs, w_gate_up)
        g, u = jnp.split(gu, 2, axis=-1)
        a = jax.nn.silu(g) * u * gs[..., None]
        return jnp.einsum('lef,efd->ld', a, w_down)

    return lax.map(per_seq, (h, gates))

def trunk(x, p, P):
    b, l, _ = x.shape
    bias = band_bias(P['rel_bias'])
    for i in range(DEPTH):
        h = rmsnorm(x, P['g_mix'][i])
        proj = h @ P['w_in'][i]
        q, k, v, z, xbc, dtf, dtb, ga, gs = jnp.split(proj, SPLITS, axis=-1)
        att = windowed_gqa(q.reshape(b, l, N_KV_HEADS, GQ, HEAD_DIM),
                           k.reshape(b, l, N_KV_HEADS, HEAD_DIM),
                           v.reshape(b, l, N_KV_HEADS, HEAD_DIM),
                           P['attn_sink'][i].reshape(N_KV_HEADS, GQ), bias)
        ya = att @ P['w_attn_out'][i]
        ys = ssd_branch(z, xbc, dtf, dtb, P['conv_w'][i], P['conv_b'][i], P['a_log_f'][i], P['a_log_b'][i],
                        P['dt_bias_f'][i], P['dt_bias_b'][i], P['d_skip'][i], P['ssd_norm_g'][i]) @ P['w_ssd_out'][i]
        mixed = jax.nn.sigmoid(ga) * ya + jax.nn.sigmoid(gs) * ys
        x = x + mixed @ P['w_out'][i]
        x = x + hier_moe(rmsnorm(x, P['g_ffn'][i]), P['router_g'][i], P['router_g_b'][i],
                         P['router_e'][i], P['router_e_b'][i], P['w_gate_up'][i], P['w_down'][i])
        x = x + jax.nn.sigmoid(rmsnorm(x, P['g_ple'][i]) @ P['w_ple_gate'][i]) * (p[i] @ P['w_ple_proj'][i])
    return rmsnorm(x, P['g_final'])

def setup_inputs(seed: int = 0) -> dict:
    key = jax.random.key(seed)
    ks = iter(jax.random.split(key, 40))
    nrm = lambda shape, scale: jax.random.normal(next(ks), shape, jnp.float32) * scale

    def dt_bias(shape):
        dt = jnp.exp(jax.random.uniform(next(ks), shape, jnp.float32, math.log(1e-3), math.log(1e-1)))
        return dt + jnp.log(-jnp.expm1(-dt))

    def a_log(shape):
        return jnp.log(jax.random.uniform(next(ks), shape, jnp.float32, 1.0, 16.0))

    return {
        "x_prompt": nrm((BATCH, SEQ, D_MODEL), 1.0),
        "x_sample": nrm((DEC_BATCH, DEC_SEQ, D_MODEL), 1.0),
        "p_prompt": nrm((DEPTH, BATCH, SEQ, PLE_DIM), 1.0),
        "p_sample": nrm((DEPTH, DEC_BATCH, DEC_SEQ, PLE_DIM), 1.0),
        "g_mix": 1.0 + nrm((DEPTH, D_MODEL), 0.02),
        "w_in": nrm((DEPTH, D_MODEL, IN_COLS), D_MODEL ** -0.5),
        "rel_bias": nrm((N_BUCKETS, N_HEADS), 0.5),
        "attn_sink": nrm((DEPTH, N_HEADS), 0.5),
        "w_attn_out": nrm((DEPTH, Q_DIM, D_MODEL), Q_DIM ** -0.5),
        "conv_w": nrm((DEPTH, CONV_WIDTH, CONV_DIM), CONV_WIDTH ** -0.5),
        "conv_b": nrm((DEPTH, CONV_DIM), 0.02),
        "a_log_f": a_log((DEPTH, N_SSD_HEADS)),
        "a_log_b": a_log((DEPTH, N_SSD_HEADS)),
        "dt_bias_f": dt_bias((DEPTH, N_SSD_HEADS)),
        "dt_bias_b": dt_bias((DEPTH, N_SSD_HEADS)),
        "d_skip": 1.0 + nrm((DEPTH, N_SSD_HEADS), 0.02),
        "ssd_norm_g": 1.0 + nrm((DEPTH, D_INNER), 0.02),
        "w_ssd_out": nrm((DEPTH, D_INNER, D_MODEL), D_INNER ** -0.5),
        "w_out": nrm((DEPTH, D_MODEL, D_MODEL), D_MODEL ** -0.5),
        "g_ffn": 1.0 + nrm((DEPTH, D_MODEL), 0.02),
        "router_g": nrm((DEPTH, D_MODEL, N_EGROUPS), D_MODEL ** -0.5),
        "router_g_b": nrm((DEPTH, N_EGROUPS), 0.01),
        "router_e": nrm((DEPTH, D_MODEL, N_EXPERTS), D_MODEL ** -0.5),
        "router_e_b": nrm((DEPTH, N_EXPERTS), 0.01),
        "w_gate_up": nrm((DEPTH, N_EXPERTS, D_MODEL, 2 * D_EXPERT), D_MODEL ** -0.5),
        "w_down": nrm((DEPTH, N_EXPERTS, D_EXPERT, D_MODEL), D_EXPERT ** -0.5),
        "g_ple": 1.0 + nrm((DEPTH, D_MODEL), 0.02),
        "w_ple_gate": nrm((DEPTH, D_MODEL, D_MODEL), D_MODEL ** -0.5),
        "w_ple_proj": nrm((DEPTH, PLE_DIM, D_MODEL), PLE_DIM ** -0.5),
        "g_final": 1.0 + nrm((D_MODEL,), 0.02),
    }

def reference(x_prompt, x_sample, p_prompt, p_sample, g_mix, w_in, rel_bias, attn_sink, w_attn_out,
              conv_w, conv_b, a_log_f, a_log_b, dt_bias_f, dt_bias_b, d_skip, ssd_norm_g, w_ssd_out,
              w_out, g_ffn, router_g, router_g_b, router_e, router_e_b, w_gate_up, w_down,
              g_ple, w_ple_gate, w_ple_proj, g_final):
    P = dict(g_mix=g_mix, w_in=w_in, rel_bias=rel_bias, attn_sink=attn_sink, w_attn_out=w_attn_out,
             conv_w=conv_w, conv_b=conv_b, a_log_f=a_log_f, a_log_b=a_log_b, dt_bias_f=dt_bias_f,
             dt_bias_b=dt_bias_b, d_skip=d_skip, ssd_norm_g=ssd_norm_g, w_ssd_out=w_ssd_out,
             w_out=w_out, g_ffn=g_ffn, router_g=router_g, router_g_b=router_g_b, router_e=router_e,
             router_e_b=router_e_b, w_gate_up=w_gate_up, w_down=w_down, g_ple=g_ple,
             w_ple_gate=w_ple_gate, w_ple_proj=w_ple_proj, g_final=g_final)
    y_prompt = trunk(x_prompt, p_prompt, P)
    y_sample = trunk(x_sample, p_sample, P)
    return (y_prompt, y_sample)


_drawn_inputs = setup_inputs


def setup_inputs(seed=0):
    import zlib

    import numpy as np

    out = dict(_drawn_inputs(seed))
    spreads = {}
    factors = {'g_mix': 2.951,
     'attn_sink': 64.0,
     'conv_b': 2.841,
     'd_skip': 12.558,
     'ssd_norm_g': 4.025,
     'g_ffn': 2.702,
     'router_g_b': 8.0,
     'router_e_b': 8.0,
     'g_ple': 64.0,
     'g_final': 8.559}
    for name, (base, spread) in spreads.items():
        noise = np.random.default_rng([zlib.crc32(name.encode()), seed]).standard_normal(out[name].shape)
        drawn = base * np.exp(spread * noise) if base else spread * noise
        out[name] = __import__('jax').numpy.asarray(drawn.astype(out[name].dtype))
    for name, factor in factors.items():
        out[name] = (out[name] * factor).astype(out[name].dtype)
    return out
```

```python
from contextlib import ExitStack

import numpy as np

import concourse.bass as bass
from concourse import mybir

F32 = mybir.dt.float32
F32R = mybir.dt.float32r
I32 = mybir.dt.int32
U32 = mybir.dt.uint32
ALU = mybir.AluOpType
ACT = mybir.ActivationFunctionType
AX = mybir.AxisListType
ds = bass.ds

P = 128
D = 1024
SEQS = (1024, 256)
T = sum(SEQS)
NT = T // P
KT = D // P
EPS = 1e-6
NEG = -1e30

HEAD = 64
N_HEADS = 8
N_KV = 2
GQ = N_HEADS // N_KV
BAND = 3 * P
N_BUCKETS = 32
QB = SEQS[0] // P

N_SSD = 16
SSD_HEAD = 64
N_STATE = 64
HPG = 8
XBC = D + 2 * 128
CONV = 5
PADDED = T + 8
CONV_LEN = T + 4
SEQ2_AT = SEQS[0] + 4

N_GROUPS = 4
PER_GROUP = 4
N_EXP = 16
F = 256
NB = (2 * T - N_EXP) // P + N_EXP
NBLK = NB + NB % 2
PLE = 256

U_XBC = 0
U_REST = U_XBC + 10
U_Z = U_REST + 22
U_AO = U_Z + 8
U_SO = U_AO + 4
U_OUT = U_SO + 8
U_PG = U_OUT + 8
U_PP = U_PG + 8
N_UNITS = U_PP + 2

C_ID, C_REV, C_INCU, C_INCL, C_GT, C_LT, C_ONE = (P * n for n in range(7))
C_TH = 7 * P
C_IOTA = C_TH + NT
C_E16 = C_IOTA + NBLK
C_RANK = C_E16 + N_EXP
N_CONST = C_RANK + 4


def host_constants():
    c = np.zeros((P, N_CONST), np.float32)
    r = np.arange(P)
    c[:, C_ID:C_ID + P] = np.eye(P)
    c[:, C_REV:C_REV + P] = np.eye(P)[::-1]
    c[:, C_INCU:C_INCU + P] = r[:, None] <= r[None]
    c[:, C_INCL:C_INCL + P] = r[:, None] >= r[None]
    c[:, C_GT:C_GT + P] = r[:, None] > r[None]
    c[:, C_LT:C_LT + P] = r[:, None] < r[None]
    c[:, C_ONE:C_ONE + P] = 1.0
    c[:, C_TH:C_TH + NT] = P * np.arange(NT)
    c[:, C_IOTA:C_IOTA + NBLK] = np.arange(NBLK)
    c[:, C_E16:C_E16 + N_EXP] = np.arange(N_EXP)
    c[:, C_RANK:C_RANK + 4] = 4 - np.arange(4)
    ids = (np.arange(NT)[None] * P + r[:, None]).astype(np.int32)
    rel = np.arange(512) - 255
    half, exact = N_BUCKETS // 2, N_BUCKETS // 4
    n = np.abs(rel)
    large = exact + (np.log(np.maximum(n, 1) / exact) / np.log(128 / exact) * (half - exact)).astype(np.int32)
    bucket = (rel > 0) * half + np.where(n < exact, n, np.minimum(large, half - 1))
    hot = np.zeros((N_BUCKETS + 1, 512), np.float32)
    hot[bucket, np.arange(512)] = n <= 128
    hot[N_BUCKETS] = np.where(n <= 128, 0.0, NEG)
    return c, ids, hot


class Core:

    def __init__(self, nc, dram):
        self.nc = nc
        self.d = dram
        self.used = []
        self.const = self.at("const", [P, N_CONST], F32, O_CONST)

    def at(self, name, shape, dtype, offset):
        return self.nc.alloc_sbuf_tensor_at(name, shape, dtype, offset=offset)

    def sems(self, ctx, *names):
        made = [self.nc.alloc_semaphore(n) for n in names]
        self.used.extend(made)
        return made

    def clear_semaphores(self):
        self.nc.all_engine_barrier()
        self.nc.clear_and_free_semaphores(self.used)
        self.nc.all_engine_barrier()
        self.used = []


O_CONST = 16512
O_KEEP = O_CONST + 3872
O_W = O_KEEP + 4256
O_R1 = O_W + 12 * 4096
O_R2 = O_R1 + 20 * 4096
O_ST = O_R2 + 11 * 4096


def weight_ring(k, tag, slots=4):
    raw = k.at(f"wraw_{tag}", [P, slots, 1024], F32, O_W)
    hi = k.at(f"whi_{tag}", [P, slots, 1024], F32R, O_W + 4 * 4096)
    lo = k.at(f"wlo_{tag}", [P, slots, 1024], F32R, O_W + 8 * 4096)
    return raw, hi, lo


def split_pair(k, tag, ktiles=KT, offset=O_R1):
    hi = k.at(f"hi_{tag}", [P, ktiles, T], F32R, offset)
    lo = k.at(f"lo_{tag}", [P, ktiles, T], F32R, offset + ktiles * T * 4)
    return hi, lo



def stage_load_constants(k):
    nc, d = k.nc, k.d
    with ExitStack() as ctx:
        (loaded,) = k.sems(ctx, "const_loaded")
        block = ctx.enter_context(nc.Block())

        @block.sync
        def _(sp):
            sp.dma_start(k.const[:, :], d["consts"]).then_inc(loaded, 16)
            sp.wait_ge(loaded, 16)



def stage_norm_transpose(k, tag, gain, hi, lo, x_dram=None, x_sbuf=None):
    nc, d = k.nc, k.d
    with ExitStack() as ctx:
        o = O_ST
        gb = k.at(f"{tag}_g", [P, D], F32, O_W)
        neg_half = k.at(f"{tag}_nh", [P, 1], F32, O_KEEP + 3008)
        eps = k.at(f"{tag}_st", [P, 2, 4], F32, O_KEEP + 3072)
        xin = k.at(f"{tag}_x", [P, 2, D], F32, O_W + 4096)
        xn = k.at(f"{tag}_xn", [P, 2, D], F32, O_W + 3 * 4096)
        junk = k.at(f"{tag}_j", [P, 2, D], F32, O_W + 5 * 4096)
        tp = [ctx.enter_context(nc.psum_tensor(f"{tag}_tp{s}", [P, KT, P], F32)) for s in range(2)]
        g_in, half_set, squared, scaled, rstd_ready, normed, turned, hi_ready, lo_ready, x_used = k.sems(
            ctx, *(f"{tag}_{n}" for n in ("g_in", "half_set", "squared", "scaled", "rstd_ready", "normed", "turned",
                                          "hi_ready", "lo_ready", "x_used")))
        x_in = k.sems(ctx, f"{tag}_x_in0", f"{tag}_x_in1")
        ident = k.const[:, C_ID:C_ID + P]

        def x_of(s, t):
            return xin[:, s, :] if x_dram is not None else x_sbuf[:, t, :]

        block = ctx.enter_context(nc.Block())

        @block.sync
        def _(sp):
            sp.dma_start(gb[:, :], gain.partition_broadcast(P)).then_inc(g_in, 16)
            if x_dram is not None:
                with sp.Fori(0, NT // 2) as i:
                    for s in range(2):
                        sp.wait_ge(x_used, 2 * i + s + 1)
                        sp.dma_start(xin[:, s, :], x_dram[ds((2 * i + s) * P, P), :]).then_inc(x_in[s], 16)

        @block.gpsimd
        def _(pool):
            pool.memset(neg_half[:, :], -0.5).then_inc(half_set, 1)
            pool.wait_ge(half_set, 1)
            with pool.Fori(0, NT // 2) as i:
                for s in range(2):
                    pool.wait_ge(scaled, 2 * i + s + 1)
                    pool.tensor_tensor(eps[:, s, 2:3], eps[:, s, 1:2], neg_half[:, :], ALU.pow).then_inc(rstd_ready, 1)

        @block.scalar
        def _(act):
            act.preload_act_table(ACT.Square)

            def square(t, s, n):
                if x_dram is not None:
                    act.wait_ge(x_in[s], 16 * n)
                act.wait_ge(x_used, t + 1)
                act.activation(junk[:, s, :], x_of(s, t), ACT.Square, accum_out=eps[:, s, 0:1]).then_inc(squared, 1)

            def split(t, s):
                act.wait_ge(turned, t + 1)
                act.activation(hi[:, :, ds(t * P, P)], tp[s][:, :, :], ACT.Copy).then_inc(hi_ready, 1)

            square(0, 0, 1)
            with act.Fori(0, NT // 2 - 1) as i:
                square(2 * i + 1, 1, i + 1)
                split(2 * i, 0)
                square(2 * i + 2, 0, i + 2)
                split(2 * i + 1, 1)
            square(NT - 1, 1, NT // 2)
            split(NT - 2, 0)
            split(NT - 1, 1)

        @block.vector
        def _(dve):
            dve.sem_inc(x_used, 2)
            dve.sem_inc(lo_ready, 2)
            dve.wait_ge(g_in, 16)

            def norm(t, s):
                dve.wait_ge(squared, t + 1)
                dve.tensor_scalar(eps[:, s, 1:2], eps[:, s, 0:1], 1.0 / D, EPS, ALU.mult, ALU.add).then_inc(scaled, 1)
                dve.wait_ge(rstd_ready, t + 1)
                dve.scalar_tensor_tensor(out=xn[:, s, :], in0=x_of(s, t), scalar=eps[:, s, 2:3],
                                         in1=gb[:, :], op0=ALU.mult, op1=ALU.mult).then_inc(normed, 1)
                dve.wait_ge(normed, t + 1)
                dve.sem_inc(x_used, 1)

            def rest(t, s):
                dve.wait_ge(hi_ready, t + 1)
                dve.tensor_tensor(lo[:, :, ds(t * P, P)], tp[s][:, :, :],
                                  hi[:, :, ds(t * P, P)].bitcast(F32), ALU.subtract).then_inc(lo_ready, 1)

            norm(0, 0)
            with dve.Fori(0, NT // 2 - 1) as i:
                norm(2 * i + 1, 1)
                rest(2 * i, 0)
                norm(2 * i + 2, 0)
                rest(2 * i + 1, 1)
            norm(NT - 1, 1)
            rest(NT - 2, 0)
            rest(NT - 1, 1)

        @block.tensor
        def _(pe):
            with pe.Fori(0, NT // 2) as i:
                for s in range(2):
                    pe.wait_ge(normed, 2 * i + s + 1)
                    pe.wait_ge(lo_ready, 2 * i + s + 1)
                    for c in range(KT):
                        mm = pe.transpose(tp[s][:, c, :], xn[:, s, c * P:(c + 1) * P], ident)
                    mm.then_inc(turned, 1)



def pe_channel_tile(pe, out, whi, wlo, hi, lo, ktiles):
    cols = [(0, 512), (512, 512), (1024, 256)]
    for kk in range(ktiles):
        for w, h in ((whi, hi), (whi, lo), (wlo, hi)):
            for n, (c, size) in enumerate(cols):
                mm = pe.matmul(out[:, n, 0:size], w[:, kk, :], h[:, kk, c:c + size],
                               start=(kk == 0 and w is whi and h is hi), stop=(kk == ktiles - 1 and w is wlo))
    return mm


def stage_project_conv(k, hi, lo):
    nc, d = k.nc, k.d
    with ExitStack() as ctx:
        raw, whi, wlo = weight_ring(k, "xbc")
        xpad = k.at("xpad", [P, 2, PADDED], F32, O_R2)
        cv = k.at("conv_acc", [P, 2, CONV_LEN], F32, O_R2 + 2 * PADDED * 4)
        xc = k.at("conv_out", [P, 2, T], F32, O_R2 + 4 * PADDED * 4)
        xt = k.at("conv_tok", [P, 2, NT, P], F32, O_R2 + 6 * PADDED * 4)
        cw = k.at("conv_w", [P, 10, CONV + 1], F32, O_KEEP)
        gp = [ctx.enter_context(nc.psum_tensor(f"xbc_p{s}", [P, 3, 512], F32)) for s in range(2)]
        tb = [ctx.enter_context(nc.psum_tensor(f"xbc_t{s}", [P, 4, P], F32)) for s in range(2)]
        w_in = k.sems(ctx, "xbc_w_in0", "xbc_w_in1")
        w_hi, w_lo, mm_done, padded, conv_step, conv_read, silu_done, turned, tok_copied = k.sems(
            ctx, "xbc_w_hi", "xbc_w_lo", "xbc_mm", "xbc_padded", "xbc_conv_step", "xbc_conv_read", "xbc_silu",
            "xbc_turned", "xbc_tok")
        cw_in, pads = k.sems(ctx, "cw_in", "xbc_pads")
        stored = k.sems(ctx, "xbc_stored0", "xbc_stored1")
        ch_stored, = k.sems(ctx, "xbc_ch_stored")
        ident = k.const[:, C_ID:C_ID + P]
        GROUPS = [(0, 4), (4, 4), (8, 2)]
        block = ctx.enter_context(nc.Block())

        @block.sync
        def _(sp):
            sp.dma_start(cw[:, :, :], d["conv"]).then_inc(cw_in, 16)
            sp.sem_inc(stored[0], 16)
            sp.sem_inc(stored[1], 16)
            xtok = d["xtok"].rearrange("(t p) c -> p t c", p=P)

            def load(c, s):
                sp.wait_ge(w_lo, c + 1)
                sp.dma_start(raw[:, s, :], d["units"][ds(U_XBC + c, 1), :, :].rearrange("u p n -> (u p) n")
                             ).then_inc(w_in[s], 16)

            def store(c, s):
                sp.wait_ge(tok_copied, 3 * c + 5)
                sp.dma_start(xtok[:, :, ds(c * P, P)], xt[:, s, :, :]).then_inc(stored[s], 16)

            for c in range(4):
                load(c, c % 2)
            with sp.Fori(0, 3) as i:
                for s in range(2):
                    load(2 * i + s + 4, s)
                    store(2 * i + s, s)
            for c in range(6, 10):
                store(c, c % 2)
            sp.wait_ge(stored[0], 96)
            sp.wait_ge(stored[1], 96)

        @block.scalar
        def _(act):
            act.preload_act_table(ACT.Silu)

            def split(c, s, n):
                act.wait_ge(w_in[s], 16 * n)
                act.wait_ge(mm_done, c + 1)
                act.activation(whi[:, s, :], raw[:, s, :], ACT.Copy).then_inc(w_hi, 1)

            def pad(c, s):
                act.wait_ge(mm_done, c + 3)
                act.wait_ge(conv_read, c + 1)
                act.activation(xpad[:, s, 2:2 + SEQS[0]].rearrange("p (a n) -> p a n", a=2), gp[s][:, 0:2, :], ACT.Copy)
                act.activation(xpad[:, s, SEQ2_AT + 2:SEQ2_AT + 2 + SEQS[1]], gp[s][:, 2, 0:SEQS[1]],
                               ACT.Copy).then_inc(padded, 1)

            def silu(c, s):
                act.wait_ge(conv_read, c + 3)
                act.wait_ge(turned, 3 * c + 1)
                act.activation(xc[:, s, 0:SEQS[0]], cv[:, s, 0:SEQS[0]], ACT.Silu)
                act.activation(xc[:, s, SEQS[0]:T], cv[:, s, SEQ2_AT:SEQ2_AT + SEQS[1]], ACT.Silu).then_inc(silu_done, 1)

            split(0, 0, 1)
            split(1, 1, 1)
            act.wait_ge(pads, 1)
            with act.Fori(0, 4) as i:
                for s in range(2):
                    pad(2 * i + s, s)
                    split(2 * i + s + 2, s, i + 2)
                    silu(2 * i + s, s)
            for s in range(2):
                pad(8 + s, s)
                silu(8 + s, s)
            act.wait_ge(silu_done, 12)
            act.dma_start(d["bc"].rearrange("(s p) t -> p s t", p=P), xc[:, :, :]).then_inc(ch_stored, 16)
            act.wait_ge(ch_stored, 16)

        @block.gpsimd
        def _(pool):
            pool.memset(xpad[:, :, :], 0.0).then_inc(pads, 1)
            pool.sem_inc(w_lo, 2)
            with pool.Fori(0, 5) as i:
                for s in range(2):
                    pool.wait_ge(w_hi, 2 * i + s + 1)
                    pool.tensor_tensor(wlo[:, s, :], raw[:, s, :], whi[:, s, :].bitcast(F32), ALU.subtract).then_inc(w_lo, 1)

        @block.tensor
        def _(pe):
            def product(c, s):
                pe.wait_ge(w_lo, c + 3)
                pe.wait_ge(padded, c + 1)
                w = whi[:, s, :].rearrange("p (k c) -> p k c", k=KT)
                wl = wlo[:, s, :].rearrange("p (k c) -> p k c", k=KT)
                pe_channel_tile(pe, gp[s], w, wl, hi, lo, KT).then_inc(mm_done, 1)

            def turn(c, s):
                pe.wait_ge(silu_done, c + 3)
                for n, (a, m) in enumerate(GROUPS):
                    pe.wait_ge(tok_copied, 3 * c + n + 1)
                    for j in range(m):
                        mm = pe.transpose(tb[(s + n) % 2][:, j, :], xc[:, s, (a + j) * P:(a + j + 1) * P], ident)
                    mm.then_inc(turned, 1)

            pe.sem_inc(mm_done, 2)
            pe.sem_inc(turned, 6)
            product(0, 0)
            with pe.Fori(0, 4) as i:
                product(2 * i + 1, 1)
                turn(2 * i, 0)
                product(2 * i + 2, 0)
                turn(2 * i + 1, 1)
            product(9, 1)
            turn(8, 0)
            turn(9, 1)

        @block.vector
        def _(dve):
            dve.sem_inc(padded, 2)
            dve.sem_inc(conv_read, 2)
            dve.sem_inc(silu_done, 2)
            dve.sem_inc(tok_copied, 2)
            dve.wait_ge(cw_in, 16)

            def conv(c, s):
                dve.wait_ge(padded, c + 3)
                dve.wait_ge(silu_done, c + 1)
                dve.tensor_scalar(cv[:, s, :], xpad[:, s, 0:CONV_LEN], cw[:, ds(c, 1), 0:1], cw[:, ds(c, 1), CONV:CONV + 1],
                                  ALU.mult, ALU.add).then_inc(conv_step, 1)
                for w in range(1, CONV):
                    dve.wait_ge(conv_step, 4 * c + w)
                    mm = dve.scalar_tensor_tensor(out=cv[:, s, :], in0=xpad[:, s, w:w + CONV_LEN],
                                                  scalar=cw[:, ds(c, 1), w:w + 1], in1=cv[:, s, :], op0=ALU.mult, op1=ALU.add)
                    mm.then_inc(conv_step if w < CONV - 1 else conv_read, 1)

            def tokens(c, s, i):
                dve.wait_ge(stored[s], 16 * (i + 1))
                for n, (a, m) in enumerate(GROUPS):
                    dve.wait_ge(turned, 3 * c + n + 7)
                    dve.tensor_copy(xt[:, s, a:a + m, :], tb[(s + n) % 2][:, 0:m, :]).then_inc(tok_copied, 1)

            conv(0, 0)
            with dve.Fori(0, 4) as i:
                tokens(2 * i, 0, i)
                conv(2 * i + 1, 1)
                tokens(2 * i + 1, 1, i)
                conv(2 * i + 2, 0)
            tokens(8, 0, 4)
            conv(9, 1)
            tokens(9, 1, 4)


def stage_project_rest(k, hi, lo):
    nc, d = k.nc, k.d
    n_tiles = 22
    with ExitStack() as ctx:
        raw, whi, wlo = weight_ring(k, "rest")
        got = k.at("rest_out", [P, 2, T], F32, O_R2)
        gp = [ctx.enter_context(nc.psum_tensor(f"rest_p{s}", [P, 3, 512], F32)) for s in range(2)]
        w_in = k.sems(ctx, "rest_w_in0", "rest_w_in1")
        stored = k.sems(ctx, "rest_stored0", "rest_stored1")
        w_hi, w_lo, mm_done, copied = k.sems(ctx, "rest_w_hi", "rest_w_lo", "rest_mm", "rest_copied")
        block = ctx.enter_context(nc.Block())

        @block.sync
        def _(sp):
            sp.sem_inc(stored[0], 16)
            sp.sem_inc(stored[1], 16)

            def load(c, s):
                sp.wait_ge(w_lo, c + 1)
                sp.dma_start(raw[:, s, :], d["units"][ds(U_REST + c, 1), :, :].rearrange("u p n -> (u p) n")
                             ).then_inc(w_in[s], 16)

            def store(c, s):
                sp.wait_ge(copied, c + 3)
                sp.dma_start(d["rest"][ds(c * P, P), :], got[:, s, :]).then_inc(stored[s], 16)

            for c in range(4):
                load(c, c % 2)
            with sp.Fori(0, (n_tiles - 4) // 2) as i:
                for s in range(2):
                    load(2 * i + s + 4, s)
                    store(2 * i + s, s)
            for c in range(n_tiles - 4, n_tiles):
                store(c, c % 2)
            for s in range(2):
                sp.wait_ge(stored[s], 16 * (n_tiles // 2 + 1))

        @block.scalar
        def _(act):
            act.sem_inc(copied, 2)

            def split(c, s, n):
                act.wait_ge(w_in[s], 16 * n)
                act.wait_ge(mm_done, c + 1)
                act.activation(whi[:, s, :], raw[:, s, :], ACT.Copy).then_inc(w_hi, 1)

            def copy(c, s, n):
                act.wait_ge(mm_done, c + 3)
                act.wait_ge(stored[s], 16 * n)
                act.activation(got[:, s, 0:1024].rearrange("p (a n) -> p a n", a=2), gp[s][:, 0:2, :], ACT.Copy)
                act.activation(got[:, s, 1024:T], gp[s][:, 2, 0:256], ACT.Copy).then_inc(copied, 1)

            split(0, 0, 1)
            split(1, 1, 1)
            with act.Fori(0, n_tiles // 2 - 1) as i:
                for s in range(2):
                    copy(2 * i + s, s, i + 1)
                    split(2 * i + s + 2, s, i + 2)
            for s in range(2):
                copy(n_tiles - 2 + s, s, n_tiles // 2)

        @block.gpsimd
        def _(pool):
            pool.sem_inc(w_lo, 2)
            with pool.Fori(0, n_tiles // 2) as i:
                for s in range(2):
                    pool.wait_ge(w_hi, 2 * i + s + 1)
                    pool.tensor_tensor(wlo[:, s, :], raw[:, s, :], whi[:, s, :].bitcast(F32), ALU.subtract).then_inc(w_lo, 1)

        @block.tensor
        def _(pe):
            pe.sem_inc(mm_done, 2)
            with pe.Fori(0, n_tiles // 2) as i:
                for s in range(2):
                    pe.wait_ge(w_lo, 2 * i + s + 3)
                    pe.wait_ge(copied, 2 * i + s + 1)
                    pe_channel_tile(pe, gp[s], whi[:, s, :].rearrange("p (k c) -> p k c", k=KT),
                                    wlo[:, s, :].rearrange("p (k c) -> p k c", k=KT), hi, lo, KT).then_inc(mm_done, 1)



def pe_token_tile(pe, out, hi, lo, t, whi, wlo, ktiles, unit_done=None):
    for kk in range(ktiles):
        c = slice((kk % 2) * 512, (kk % 2) * 512 + 512)
        tok = slice(t * P, (t + 1) * P)
        pe.matmul(out, hi[:, kk, tok], whi[:, kk // 2, c], start=(kk == 0), stop=False)
        pe.matmul(out, hi[:, kk, tok], wlo[:, kk // 2, c], start=False, stop=False)
        mm = pe.matmul(out, lo[:, kk, tok], whi[:, kk // 2, c], start=False, stop=(kk == ktiles - 1))
        if unit_done is not None and kk % 2 == 1 and kk < ktiles - 1:
            mm.then_inc(unit_done, 1)
    return mm


def stage_project_z(k, hi, lo):
    nc, d = k.nc, k.d
    with ExitStack() as ctx:
        raw, whi, wlo = weight_ring(k, "z")
        zt = k.at("z_out", [P, 2, 512], F32, O_R2)
        wd_raw = k.at("wd_raw", [P, KT, 32], F32, O_R2 + 4096)
        wd_hi = k.at("wd_hi", [P, KT, 32], F32R, O_R2 + 5120)
        wd_lo = k.at("wd_lo", [P, KT, 32], F32R, O_R2 + 6144)
        zp = [ctx.enter_context(nc.psum_tensor(f"z_p{b}", [P, 512], F32)) for b in range(5)]
        dp = ctx.enter_context(nc.psum_tensor("dt_p", [P, NT, 32], F32))
        w_in = k.sems(ctx, *(f"z_w_in{s}" for s in range(4)))
        stored = k.sems(ctx, "z_stored0", "z_stored1")
        w_hi, w_lo, unit_done, tile_done, silued, wd_in, wd_h, wd_l, dt_done = k.sems(
            ctx, "z_w_hi", "z_w_lo", "z_unit", "z_tile", "z_silu", "wd_in", "wd_h", "wd_l", "dt_done")
        block = ctx.enter_context(nc.Block())

        @block.sync
        def _(sp):
            sp.sem_inc(stored[0], 16)
            sp.sem_inc(stored[1], 16)
            for n in range(4):
                sp.dma_start(raw[:, n, :], d["units"][U_Z + n]).then_inc(w_in[n], 16)
            sp.dma_start(wd_raw[:, :, :], d["w_dt"]).then_inc(wd_in, 16)
            for c in range(2):
                for t in range(NT):
                    if c == 0 and t == 0:
                        for n in range(4):
                            sp.wait_ge(w_lo, n + 1)
                            sp.dma_start(raw[:, n, :], d["units"][U_Z + 4 + n]).then_inc(w_in[n], 16)
                    sp.wait_ge(silued, NT * c + t + 6)
                    sp.dma_start(d["ztok"][t * P:(t + 1) * P, c * 512:(c + 1) * 512], zt[:, t % 2, :]).then_inc(stored[t % 2], 16)
            sp.wait_ge(stored[0], 176)
            sp.wait_ge(stored[1], 176)

        @block.scalar
        def _(act):
            act.preload_act_table(ACT.Silu)
            act.sem_inc(silued, 5)
            for c in range(2):
                if c == 0:
                    for n in range(4):
                        act.wait_ge(w_in[n], 16)
                        act.activation(whi[:, n, :], raw[:, n, :], ACT.Copy).then_inc(w_hi, 1)
                    act.wait_ge(wd_in, 16)
                    act.activation(wd_hi[:, :, :], wd_raw[:, :, :], ACT.Copy).then_inc(wd_h, 1)
                for t in range(NT):
                    if c == 0 and t == NT - 1:
                        for n in range(4):
                            act.wait_ge(w_in[n], 32)
                            if n < 3:
                                act.wait_ge(unit_done, n + 1)
                            else:
                                act.wait_ge(tile_done, NT)
                            act.activation(whi[:, n, :], raw[:, n, :], ACT.Copy).then_inc(w_hi, 1)
                    act.wait_ge(tile_done, NT * c + t + 1)
                    act.wait_ge(stored[t % 2], 16 * (5 * c + t // 2 + 1))
                    act.activation(zt[:, t % 2, :], zp[t % 5][:, :], ACT.Silu).then_inc(silued, 1)

        @block.gpsimd
        def _(pool):
            for c in range(2):
                for n in range(4):
                    pool.wait_ge(w_hi, 4 * c + n + 1)
                    pool.tensor_tensor(wlo[:, n, :], raw[:, n, :], whi[:, n, :].bitcast(F32), ALU.subtract).then_inc(w_lo, 1)
                if c == 0:
                    pool.wait_ge(wd_h, 1)
                    pool.tensor_tensor(wd_lo[:, :, :], wd_raw[:, :, :], wd_hi[:, :, :].bitcast(F32),
                                       ALU.subtract).then_inc(wd_l, 1)

        @block.tensor
        def _(pe):
            for c in range(2):
                for t in range(NT):
                    if t == 0:
                        pe.wait_ge(w_lo, 4 * c + 4)
                    pe.wait_ge(silued, NT * c + t + 1)
                    last = c == 0 and t == NT - 1
                    mm = pe_token_tile(pe, zp[t % 5][:, :], hi, lo, t, whi, wlo, KT, unit_done if last else None)
                    mm.then_inc(tile_done, 1)
            pe.wait_ge(wd_l, 1)
            for t in range(NT):
                tok = slice(t * P, (t + 1) * P)
                for kk in range(KT):
                    pe.matmul(dp[:, t, :], hi[:, kk, tok], wd_hi[:, kk, :], start=(kk == 0), stop=False)
                    pe.matmul(dp[:, t, :], hi[:, kk, tok], wd_lo[:, kk, :], start=False, stop=False)
                    mm = pe.matmul(dp[:, t, :], lo[:, kk, tok], wd_hi[:, kk, :], start=False, stop=(kk == KT - 1))
            mm.then_inc(dt_done, 1)

        @block.vector
        def _(dve):
            dve.wait_ge(dt_done, 1)
            dve.tensor_copy(k.dt_raw[:, :, :], dp[:, :, :])



O_BIAS = O_W


def stage_bias_tables(k):
    nc, d = k.nc, k.d
    with ExitStack() as ctx:
        hot = k.at("hot", [N_BUCKETS + 1, 512], F32, O_R2)
        rel = k.at("rel", [N_BUCKETS + 1, N_HEADS], F32, O_R2 + 2048)
        line = k.at("line", [N_HEADS, 512], F32, O_R2 + 4096)
        slid = k.at("slid", [P, N_HEADS, BAND], F32, O_R2 + 8192)
        lp = ctx.enter_context(nc.psum_tensor("line_p", [P, 512], F32))
        bp = [ctx.enter_context(nc.psum_tensor(f"bias_p{s}", [P, 512], F32)) for s in range(2)]
        ones_set, tab_in, line_done, line_copied, line_stored, slid_in, flipped, copied, firsts = k.sems(
            ctx, "ones_set", "tab_in", "line_done", "line_copied", "line_stored", "slid_in", "flipped", "bias_copied",
            "bias_first")
        block = ctx.enter_context(nc.Block())

        @block.sync
        def _(sp):
            sp.dma_start(hot[:, :], d["hot"]).then_inc(tab_in, 16)
            sp.wait_ge(ones_set, 1)
            sp.dma_start(rel[0:N_BUCKETS, :], d["rel_bias"]).then_inc(tab_in, 16)
            sp.wait_ge(line_copied, 1)
            sp.dma_start(d["bias_line"], line[:, :]).then_inc(line_stored, 16)
            sp.wait_ge(line_stored, 16)
            src = bass.AP(tensor=d["bias_line"].tensor, offset=0, ap=[[1, P], [512, N_HEADS], [1, BAND]])
            sp.dma_start(slid[:, :, :], src).then_inc(slid_in, 16)

        @block.tensor
        def _(pe):
            pe.wait_ge(tab_in, 32)
            pe.matmul(lp[0:N_HEADS, :], rel[:, :], hot[:, :], start=True, stop=True).then_inc(line_done, 1)
            pe.wait_ge(slid_in, 16)
            for h in range(N_HEADS):
                if h >= 2:
                    pe.wait_ge(copied, h - 1)
                pe.matmul(bp[h % 2][:, 0:BAND], k.const[:, C_REV:C_REV + P], slid[:, h, :], start=True,
                          stop=True).then_inc(flipped, 1)

        @block.vector
        def _(dve):
            dve.memset(rel[:, :], 1.0).then_inc(ones_set, 1)
            dve.wait_ge(line_done, 1)
            dve.tensor_copy(line[:, :], lp[0:N_HEADS, :]).then_inc(line_copied, 1)
            for h in range(N_HEADS):
                dve.wait_ge(flipped, h + 1)
                dve.tensor_copy(k.bias[:, 0, h, :], bp[h % 2][:, 0:BAND]).then_inc(copied, 1)
            dve.wait_ge(copied, N_HEADS)
            for v in (1, 2):
                dve.tensor_copy(k.bias[:, v, :, :], k.bias[:, 0, :, :]).then_inc(firsts, 1)
            dve.wait_ge(firsts, 2)
            dve.memset(k.bias[:, 1, :, 0:P], NEG)
            dve.memset(k.bias[:, 2, :, 2 * P:], NEG)


def stage_attention(k, att_hi, att_lo):
    nc, d = k.nc, k.d
    with ExitStack() as ctx:
        o = O_R2
        qs = k.at("q_blk", [P, 2, 4, P], F32, o)
        ks = k.at("k_win", [P, 2, BAND], F32, o + 4096)
        vt = k.at("v_ch", [P, T], F32, o + 7168)
        vn = k.at("v_tok", [P, NT + 4, P], F32, o + 12288)
        sc = k.at("scores", [P, 2, GQ, BAND], F32, o + 19456)
        pt = k.at("probs_t", [P, 2, BAND], F32, o + 31744)
        att = k.at("att_tok", [P, 2, N_HEADS * HEAD], F32, o + 34816)
        sink = k.at("sink", [P, N_HEADS], F32, o + 38912)
        nsink = k.at("nsink", [P, N_HEADS], F32, o + 38944)
        st = k.at("att_stat", [P, 2, 6, GQ], F32, o + 38976)
        rden = k.at("att_rden", [P, 2, N_HEADS], F32, o + 39168)
        sp_ = ctx.enter_context(nc.psum_tensor("score_p", [P, GQ, 512], F32))
        tp = [ctx.enter_context(nc.psum_tensor(f"att_tp{s}", [P, 512], F32)) for s in range(2)]
        pv = ctx.enter_context(nc.psum_tensor("pv_p", [P, N_HEADS * HEAD], F32))
        ap_ = ctx.enter_context(nc.psum_tensor("att_t", [P, 4, P], F32))
        qk_in = k.sems(ctx, "qk_in0", "qk_in1")
        names = ("v_in", "v_zero", "v_turned", "v_copied", "sink_in", "sink_neg", "score_done", "scored", "step",
                 "probs", "turned", "pt_even", "pt_odd", "pv_done", "att_done", "att_turned", "att_hi_s",
                 "att_lo_s", "ready", "pv_step")
        (v_in, v_zero, v_turned, v_copied, sink_in, sink_neg, score_done, scored, step, probs,
         turned, pt_even, pt_odd, pv_done, att_done, att_turned, att_hi_s, att_lo_s, ready, pv_step) = k.sems(
             ctx, *(f"att_{n}" for n in names))
        ident = k.const[:, C_ID:C_ID + P]
        MID = (0, 0)
        block = ctx.enter_context(nc.Block())

        def pairs(eng, body):
            body(0, (1, 0), 0)
            with eng.Fori(1, QB // 2 - 1) as i:
                body(2 * i, MID, 0)
            body(QB - 2, (0, 2), 0)
            body(QB, (1, 2), 1)

        @block.sync
        def _(sp):
            sp.dma_start(vt[:, :], d["rest"][5 * P:6 * P, :]).then_inc(v_in, 16)
            sp.dma_start(sink[:, :], d["sink"].partition_broadcast(P)).then_inc(sink_in, 16)
            sp.wait_ge(v_zero, 2)

            def body(n0, tables, seq):
                for s in range(2):
                    n = n0 + s
                    sp.wait_ge(score_done, 2 * n + 2)
                    sp.dma_start(qs[:, s, :, :], d["rest"][0:4 * P, ds(n * P, P)].rearrange("(m p) t -> p m t", p=P)
                                 ).then_inc(qk_in[s], 16)
                    a = 1 if tables[s] == 1 else 0
                    b = 2 if tables[s] == 2 else 3
                    sp.dma_start(ks[:, s, a * P:b * P], d["rest"][4 * P:5 * P, ds((n - 1 + a) * P, (b - a) * P)]
                                 ).then_inc(qk_in[s], 16)

            pairs(sp, body)

        @block.gpsimd
        def _(pool):
            pool.memset(vn[:, :, :], 0.0).then_inc(v_zero, 1)
            pool.memset(ks[:, :, :], 0.0).then_inc(v_zero, 1)

        @block.tensor
        def _(pe):
            pe.sem_inc(score_done, 4)
            pe.sem_inc(turned, 8)
            pe.sem_inc(pv_done, 2)
            pe.wait_ge(v_in, 16)
            for t in range(NT):
                if t >= 2:
                    pe.wait_ge(v_copied, t - 1)
                pe.transpose(tp[t % 2][:, 0:P], vt[:, t * P:(t + 1) * P], ident).then_inc(v_turned, 1)
            pe.wait_ge(v_copied, NT)

            def score(n, s, g):
                u = 2 * n + g
                if g == 0:
                    pe.wait_ge(qk_in[s], 16 * (n - s) + 32)
                pe.wait_ge(scored, u + 1)
                for m in range(GQ):
                    mm = pe.matmul(sp_[:, m, 0:BAND], qs[g * HEAD:(g + 1) * HEAD, s, m, :],
                                   ks[g * HEAD:(g + 1) * HEAD, s, :], start=True, stop=True)
                mm.then_inc(score_done, 1)

            def turn(n, s, g, m):
                if m == 0:
                    pe.wait_ge(probs, 2 * n + g + 1)
                pe.wait_ge(pt_even if m % 2 == 0 else pt_odd, 2 * (2 * n + g) + m // 2 + 1)
                for b in range(3):
                    mm = pe.transpose(tp[m % 2][:, b * P:(b + 1) * P], sc[:, g, m, b * P:(b + 1) * P], ident)
                mm.then_inc(turned, 1)

            def weigh(n, s, g, m, seq):
                pe.wait_ge(pt_even if m % 2 == 0 else pt_odd, 2 * (2 * n + g) + m // 2 + 2)
                if g == 0 and m == 0:
                    pe.wait_ge(att_done, n + 1)
                hd = (4 * g + m) * HEAD
                for b in range(3):
                    mm = pe.matmul(pv[:, hd:hd + HEAD], pt[:, m % 2, b * P:(b + 1) * P],
                                   vn[:, ds(n + seq + b, 1), g * HEAD:(g + 1) * HEAD].rearrange("p a n -> p (a n)"),
                                   start=(b == 0), stop=(b == 2))
                mm.then_inc(pv_done, 1)

            def values(n, s, g, seq):
                turn(n, s, g, 0)
                for m in range(1, GQ):
                    turn(n, s, g, m)
                    weigh(n, s, g, m - 1, seq)
                weigh(n, s, g, GQ - 1, seq)

            def out(n, s):
                pe.wait_ge(att_done, n + 2)
                pe.wait_ge(att_lo_s, n + 1)
                for m in range(4):
                    mm = pe.transpose(ap_[:, m, :], att[:, s, m * P:(m + 1) * P], ident)
                mm.then_inc(att_turned, 1)

            def body(n, tables, seq):
                score(n, 0, 0)
                score(n, 0, 1)
                values(n, 0, 0, seq)
                score(n + 1, 1, 0)
                values(n, 0, 1, seq)
                score(n + 1, 1, 1)
                out(n, 0)
                values(n + 1, 1, 0, seq)
                values(n + 1, 1, 1, seq)
                out(n + 1, 1)

            pairs(pe, body)

        @block.scalar
        def _(act):
            act.preload_act_table(ACT.Exp)
            act.sem_inc(pt_odd, 1)

            def exps(n, g):
                u = 2 * n + g
                act.wait_ge(ready, u + 1)
                for m in range(GQ):
                    act.activation(sc[:, g, m, :], sc[:, g, m, :], ACT.Exp, bias=st[:, g, 1, m:m + 1],
                                   accum_out=st[:, g, 4, m:m + 1])
                act.activation(st[:, g, 3, :], st[:, g, 2, :], ACT.Exp).then_inc(probs, 1)

            def odd(n, g):
                for m in (1, 3):
                    act.wait_ge(turned, 4 * (2 * n + g) + m + 9)
                    act.wait_ge(pv_done, 4 * (2 * n + g) + m + 1)
                    act.activation(pt[:, 1, :], tp[1][:, 0:BAND], ACT.Copy).then_inc(pt_odd, 1)

            def split(n):
                act.wait_ge(att_turned, n + 1)
                act.activation(att_hi[:, :, ds(n * P, P)], ap_[:, :, :], ACT.Copy).then_inc(att_hi_s, 1)

            def body(n, tables, seq):
                exps(n, 0)
                exps(n, 1)
                odd(n, 0)
                exps(n + 1, 0)
                odd(n, 1)
                exps(n + 1, 1)
                split(n)
                odd(n + 1, 0)
                odd(n + 1, 1)
                split(n + 1)

            pairs(act, body)

        @block.vector
        def _(dve):
            dve.sem_inc(scored, 1)
            dve.sem_inc(pt_even, 1)
            dve.sem_inc(att_done, 1)
            dve.sem_inc(att_lo_s, 1)
            dve.wait_ge(sink_in, 16)
            dve.tensor_scalar(nsink[:, :], sink[:, :], -1.0, None, ALU.mult).then_inc(sink_neg, 1)
            dve.wait_ge(v_zero, 2)
            for t in range(NT):
                dve.wait_ge(v_turned, t + 1)
                at = t + 1 if t < QB else t + 2
                dve.tensor_copy(vn[:, at, :], tp[t % 2][:, 0:P]).then_inc(v_copied, 1)
            dve.wait_ge(sink_neg, 1)

            def stats(n, g, table):
                u = 2 * n + g
                dve.wait_ge(score_done, u + 5)
                dve.wait_ge(turned, 4 * u + 4)
                dve.scalar_tensor_tensor(out=sc[:, g, :, :], in0=sp_[:, :, 0:BAND], scalar=HEAD ** -0.5,
                                         in1=k.bias[:, table, g * GQ:(g + 1) * GQ, :], op0=ALU.mult,
                                         op1=ALU.add).then_inc(scored, 1)
                dve.wait_ge(scored, u + 2)
                dve.tensor_reduce(st[:, g, 0, :], sc[:, g, :, :], AX.X, ALU.max).then_inc(step, 1)
                dve.wait_ge(step, 2 * u + 1)
                dve.scalar_tensor_tensor(out=st[:, g, 1, :], in0=st[:, g, 0, :], scalar=-1.0,
                                         in1=nsink[:, g * GQ:(g + 1) * GQ], op0=ALU.mult, op1=ALU.min).then_inc(step, 1)
                dve.wait_ge(step, 2 * u + 2)
                dve.tensor_tensor(st[:, g, 2, :], st[:, g, 1, :], sink[:, g * GQ:(g + 1) * GQ], ALU.add).then_inc(ready, 1)

            def even(n, s, g):
                u = 2 * n + g
                dve.wait_ge(probs, u + 1)
                dve.tensor_tensor(st[:, g, 5, :], st[:, g, 4, :], st[:, g, 3, :], ALU.add).then_inc(pv_step, 1)
                for m in (0, 2):
                    dve.wait_ge(turned, 4 * u + m + 9)
                    dve.wait_ge(pv_done, 4 * u + m + 1)
                    dve.tensor_copy(pt[:, 0, :], tp[0][:, 0:BAND]).then_inc(pt_even, 1)
                dve.wait_ge(pv_step, 2 * u + 1)
                dve.reciprocal(rden[:, s, g * GQ:(g + 1) * GQ], st[:, g, 5, :]).then_inc(pv_step, 1)

            def scale(n, s):
                dve.wait_ge(pv_done, 8 * n + 10)
                dve.wait_ge(pv_step, 4 * n + 4)
                dve.tensor_tensor(att[:, s, :].rearrange("p (h e) -> p h e", e=HEAD),
                                  pv[:, :].rearrange("p (h e) -> p h e", e=HEAD),
                                  rden[:, s, :].unsqueeze(2).to_broadcast([P, N_HEADS, HEAD]), ALU.mult).then_inc(att_done, 1)

            def rest(n):
                dve.wait_ge(att_hi_s, n + 1)
                dve.tensor_tensor(att_lo[:, :, ds(n * P, P)], ap_[:, :, :], att_hi[:, :, ds(n * P, P)].bitcast(F32),
                                  ALU.subtract).then_inc(att_lo_s, 1)

            def body(n, tables, seq):
                stats(n, 0, tables[0])
                stats(n, 1, tables[0])
                even(n, 0, 0)
                stats(n + 1, 0, tables[1])
                even(n, 0, 1)
                scale(n, 0)
                stats(n + 1, 1, tables[1])
                rest(n)
                even(n + 1, 1, 0)
                even(n + 1, 1, 1)
                scale(n + 1, 1)
                rest(n + 1)

            pairs(dve, body)



def stage_gated(k, tag, hi, lo, ktiles, unit0, gate0, add, out_sbuf=None):
    nc, d = k.nc, k.d
    per_unit = KT // ktiles
    n_units = KT // per_unit
    with ExitStack() as ctx:
        raw, whi, wlo = weight_ring(k, tag)
        gate = [k.at(f"{tag}_gate{s}", [P, T], F32, O_ST + s * 5120) for s in range(2)]
        other = [k.at(f"{tag}_other{s}", [P, T], F32, O_ST + 2 * 5120 + s * 5120) for s in range(2)] if add else None
        prod = [k.at(f"{tag}_prod{s}", [P, T], F32, O_W + 2 * 4096 + s * 16384) for s in range(2)]
        gp = [ctx.enter_context(nc.psum_tensor(f"{tag}_p{s}", [P, 3, 512], F32)) for s in range(2)]
        w_in = k.sems(ctx, f"{tag}_w_in0", f"{tag}_w_in1")
        g_in = k.sems(ctx, f"{tag}_g_in0", f"{tag}_g_in1")
        stored = k.sems(ctx, f"{tag}_stored0", f"{tag}_stored1")
        w_hi, w_lo, mm_done, sig, used, prod_done = k.sems(
            ctx, *(f"{tag}_{n}" for n in ("w_hi", "w_lo", "mm", "sig", "used", "prod")))
        loads = 2 if add else 1
        block = ctx.enter_context(nc.Block())

        @block.sync
        def _(sp):
            if not add:
                sp.sem_inc(stored[0], 16)
                sp.sem_inc(stored[1], 16)

            def load_unit(u, s):
                sp.wait_ge(w_lo, u + 1)
                sp.dma_start(raw[:, s, :], d["units"][ds(unit0 + u, 1), :, :].rearrange("u p n -> (u p) n")
                             ).then_inc(w_in[s], 16)

            def load_gate(c, s):
                sp.wait_ge(used, c + 1)
                sp.dma_start(gate[s][:, :], d["rest"][ds((gate0 + c) * P, P), :]).then_inc(g_in[s], 16)
                if add:
                    sp.dma_start(other[s][:, :], d["mix_a"][ds(c * P, P), :]).then_inc(g_in[s], 16)

            def store(c, s):
                sp.wait_ge(used, c + 3)
                sp.dma_start(d["mix_a"][ds(c * P, P), :], prod[s][:, :]).then_inc(stored[s], 16)

            load_unit(0, 0)
            load_unit(1, 1)
            load_gate(0, 0)
            load_gate(1, 1)
            with sp.Fori(0, n_units // 2 - 1) as i:
                for s in range(2):
                    load_unit(2 * i + s + 2, s)
                    for c in range(per_unit):
                        if not add:
                            store((2 * i + s) * per_unit + c, (s * per_unit + c) % 2)
                        load_gate((2 * i + s) * per_unit + c + 2, (s * per_unit + c) % 2)
            for c in range(KT - 2 * per_unit, KT):
                if not add:
                    store(c, c % 2)
                if c < KT - 2:
                    load_gate(c + 2, c % 2)
            if not add:
                sp.wait_ge(stored[0], 16 * (KT // 2 + 1))
                sp.wait_ge(stored[1], 16 * (KT // 2 + 1))

        @block.scalar
        def _(act):
            act.preload_act_table(ACT.Sigmoid)

            def split(u, s, n):
                act.wait_ge(w_in[s], 16 * n)
                act.wait_ge(mm_done, per_unit * (u + 1))
                act.activation(whi[:, s, :], raw[:, s, :], ACT.Copy).then_inc(w_hi, 1)

            def gates(c, s, n):
                act.wait_ge(g_in[s], 16 * loads * n)
                act.activation(gate[s][:, :], gate[s][:, :], ACT.Sigmoid).then_inc(sig, 1)

            split(0, 0, 1)
            split(1, 1, 1)
            with act.Fori(0, n_units // 2 - 1) as i:
                for s in range(2):
                    for c in range(per_unit):
                        gates((2 * i + s) * per_unit + c, (s * per_unit + c) % 2, i * per_unit + (s * per_unit + c) // 2 + 1)
                    split(2 * i + s + 2, s, i + 2)
            for c in range(KT - 2 * per_unit, KT):
                gates(c, c % 2, c // 2 + 1)

        @block.gpsimd
        def _(pool):
            pool.sem_inc(w_lo, 2)
            with pool.Fori(0, n_units // 2) as i:
                for s in range(2):
                    pool.wait_ge(w_hi, 2 * i + s + 1)
                    pool.tensor_tensor(wlo[:, s, :], raw[:, s, :], whi[:, s, :].bitcast(F32), ALU.subtract).then_inc(w_lo, 1)

        @block.tensor
        def _(pe):
            pe.sem_inc(mm_done, 2 * per_unit)
            with pe.Fori(0, n_units // 2) as i:
                for s in range(2):
                    pe.wait_ge(w_lo, 2 * i + s + 3)
                    for c in range(per_unit):
                        pe.wait_ge(used, (2 * i + s) * per_unit + c + 1)
                        w = (x[:, s, c * ktiles * P:(c + 1) * ktiles * P].rearrange("p (k c) -> p k c", k=ktiles)
                             for x in (whi, wlo))
                        pe_channel_tile(pe, gp[(s * per_unit + c) % 2], *w, hi, lo, ktiles).then_inc(mm_done, 1)

        @block.vector
        def _(dve):
            dve.sem_inc(used, 2)
            with dve.Fori(0, KT // 2) as i:
                for s in range(2):
                    c = 2 * i + s
                    dve.wait_ge(sig, c + 1)
                    dve.wait_ge(mm_done, c + 2 * per_unit + 1)
                    if not add:
                        dve.wait_ge(stored[s], 16 * (i + 1))
                    dve.tensor_tensor(prod[s][:, 0:1024].rearrange("p (a n) -> p a n", a=2), gp[s][:, 0:2, :],
                                      gate[s][:, 0:1024].rearrange("p (a n) -> p a n", a=2), ALU.mult).then_inc(prod_done, 1)
                    mm = dve.tensor_tensor(prod[s][:, 1024:T], gp[s][:, 2, 0:256], gate[s][:, 1024:T], ALU.mult)
                    if not add:
                        mm.then_inc(used, 1)
                    else:
                        mm.then_inc(prod_done, 1)
                        dve.wait_ge(prod_done, 2 * c + 2)
                        dve.tensor_tensor(out_sbuf[:, ds(c, 1), :].rearrange("p a t -> p (a t)"), prod[s][:, :],
                                          other[s][:, :], ALU.add).then_inc(used, 1)



class SsdTiles:

    def __init__(self, k):
        o = O_W
        self.dt = k.at("ssd_dt", [P, NT, 32], F32, o)
        self.dta = k.at("ssd_dta", [P, NT, 32], F32, o + 1280)
        self.e0 = k.at("ssd_e0", [P, 3, NT, N_SSD], F32, o + 2560)
        self.e1 = k.at("ssd_e1", [P, NT * 16 * 3], F32, o + 2560 + 1920)
        self.inc_f = self.e0[:, 2, :, :]
        self.inc_b = self.e1[:, 0:160].rearrange("p (t h) -> p t h", t=NT)
        self.tot = self.e1[:, 160:480].rearrange("p (t h) -> p t h", t=NT)
        self.cf = k.at("ssd_cf", [P, 2, NT, N_SSD], F32, o + 6400)
        self.et = k.at("ssd_et", [P, 2, NT, HPG], F32, o + 7680)
        self.st = [k.at(f"ssd_state{n}", [P, NT + 1, 512], F32, O_R2 + n * (NT + 1) * 2048) for n in range(2)]


def of_chunk(x, t):
    return x[:, ds(t, 1), :].rearrange("p a h -> p (a h)")


def per_head(x, width=SSD_HEAD):
    return x.unsqueeze(2).to_broadcast([P, x.shape[1], width])


def stage_ssd_decays(k, q):
    nc, d = k.nc, k.d
    with ExitStack() as ctx:
        w = k.at("dec_w", [P, 8, NT, 32], F32, O_R2)
        bias = k.at("dec_bias", [P, 32], F32, O_ST)
        alog = k.at("dec_alog", [P, 32], F32, O_ST + 128)
        sums = [ctx.enter_context(nc.psum_tensor(f"dec_p{n}", [P, 512], F32)) for n in range(2)]
        par_in, chain, exp_a, exp_v, ln_u, dta_ready, summed, exped = k.sems(
            ctx, *(f"dec_{n}" for n in ("par_in", "chain", "exp_a", "exp_v", "ln_u", "dta", "summed", "exped")))
        v, neg, mag, e, u, lnu, d0, z = (w[:, n, :, :] for n in range(8))
        block = ctx.enter_context(nc.Block())

        @block.sync
        def _(sp):
            sp.dma_start(bias[:, :], d["dt_bias"].partition_broadcast(P)).then_inc(par_in, 16)
            sp.dma_start(alog[:, :], d["a_log"].partition_broadcast(P)).then_inc(par_in, 16)

        @block.vector
        def _(dve):
            steps = [0]

            def step(ins):
                steps[0] += 1
                ins.then_inc(chain, 1)
                dve.wait_ge(chain, steps[0])

            dve.wait_ge(par_in, 32)
            step(dve.tensor_tensor(v, k.dt_raw[:, :, :], bias[:, :].unsqueeze(1).to_broadcast([P, NT, 32]), ALU.add))
            step(dve.tensor_scalar(neg, v, -1.0, None, ALU.mult))
            step(dve.tensor_tensor(mag, v, neg, ALU.max))
            dve.wait_ge(exp_v, 1)
            step(dve.tensor_scalar(u, e, 1.0, None, ALU.add))
            step(dve.tensor_scalar(d0, u, -1.0, None, ALU.add))
            step(dve.tensor_scalar(z, d0, 0.0, None, ALU.is_equal))
            step(dve.tensor_tensor(d0, d0, z, ALU.add))
            step(dve.reciprocal(mag, d0))
            step(dve.tensor_tensor(mag, mag, e, ALU.mult))
            step(dve.tensor_tensor(z, z, e, ALU.mult))
            dve.wait_ge(ln_u, 1)
            step(dve.tensor_tensor(mag, mag, lnu, ALU.mult))
            step(dve.tensor_tensor(mag, mag, z, ALU.add))
            step(dve.scalar_tensor_tensor(out=q.dt[:, :, :], in0=v, scalar=0.0, in1=mag, op0=ALU.max, op1=ALU.add))
            dve.wait_ge(exp_a, 1)
            dve.scalar_tensor_tensor(out=q.dta[:, :, :], in0=q.dt[:, :, :], scalar=-1.0,
                                     in1=alog[:, :].unsqueeze(1).to_broadcast([P, NT, 32]), op0=ALU.mult,
                                     op1=ALU.mult).then_inc(dta_ready, 1)
            dve.wait_ge(exped, 2)
            for n in range(2):
                dve.tensor_tensor(q.cf[:, n, :, :], q.dt[:, :, n * 16:(n + 1) * 16], q.e0[:, n, :, :], ALU.mult)
                for g in range(2):
                    rows = slice(g * 64, (g + 1) * 64)
                    dve.tensor_copy(q.et[rows, n, :, :], q.tot[rows, :, n * 16 + g * HPG:n * 16 + (g + 1) * HPG])

        @block.scalar
        def _(act):
            act.preload_act_table_set("natural_log_exp_and_others")
            act.wait_ge(par_in, 32)
            act.activation(alog[:, :], alog[:, :], ACT.Exp).then_inc(exp_a, 1)
            act.wait_ge(chain, 3)
            act.activation(e, mag, ACT.Exp, scale=-1.0).then_inc(exp_v, 1)
            act.wait_ge(chain, 4)
            act.activation(lnu, u, ACT.Ln).then_inc(ln_u, 1)
            act.wait_ge(summed, 1)
            act.activation(q.e0[:, :, :, :].rearrange("p a t h -> p (a t h)"), sums[0][:, 0:480], ACT.Exp).then_inc(exped, 1)
            act.activation(q.e1[:, :], sums[1][:, 0:480], ACT.Exp).then_inc(exped, 1)

        @block.tensor
        def _(pe):
            pe.wait_ge(dta_ready, 1)
            f, b = q.dta[:, :, 0:16], q.dta[:, :, 16:32]
            for bank, at, mask, rhs in ((0, 0, C_GT, f), (0, 160, C_LT, b), (0, 320, C_INCU, f), (1, 0, C_INCL, b),
                                        (1, 160, C_ONE, q.dta[:, :, :])):
                n = NT * rhs.shape[2]
                mm = pe.matmul(sums[bank][:, at:at + n].rearrange("p (t h) -> p t h", t=NT), k.const[:, mask:mask + P], rhs,
                               start=True, stop=True)
            mm.then_inc(summed, 1)


def stage_ssd_states(k, q):
    nc, d = k.nc, k.d
    sf, sb = q.st
    with ExitStack() as ctx:
        o = O_W + 9 * 1024
        xb = [k.at(f"sst_x{s}", [P, D + P], F32, o + s * 4608) for s in range(2)]
        xd = [[k.at(f"sst_xd{n}{s}", [P, D], F32, o + 9216 + (2 * n + s) * 4096) for s in range(2)] for n in range(2)]
        tmp = [k.at(f"sst_tmp{n}", [P, 512], F32, O_ST + 2048 * n) for n in range(2)]
        pp = [[ctx.enter_context(nc.psum_tensor(f"sst_p{n}{s}", [P, 512], F32)) for s in range(2)] for n in range(2)]
        x_in = k.sems(ctx, "sst_x_in0", "sst_x_in1")
        scaled_f, scaled_b, state_mm, saved, zeroed, chain_f, chain_b = k.sems(
            ctx, *(f"sst_{n}" for n in ("scaled_f", "scaled_b", "mm", "saved", "zeroed", "chain_f", "chain_b")))
        block = ctx.enter_context(nc.Block())

        @block.sync
        def _(sp):
            with sp.Fori(0, NT // 2) as i:
                for s in range(2):
                    sp.wait_ge(state_mm, 2 * i + s + 1)
                    sp.dma_start(xb[s][:, :], d["xtok"][ds((2 * i + s) * P, P), 0:D + P]).then_inc(x_in[s], 16)

        def scale(eng, n, i, s, done):
            t = 2 * i + s
            eng.wait_ge(x_in[s], 16 * (i + 1))
            eng.wait_ge(state_mm, t + 1)
            eng.tensor_tensor(xd[n][s][:, :].rearrange("p (h e) -> p h e", e=SSD_HEAD),
                              xb[s][:, 0:D].rearrange("p (h e) -> p h e", e=SSD_HEAD),
                              per_head(of_chunk(q.cf[:, n, :, :], t)), ALU.mult).then_inc(done, 1)

        @block.tensor
        def _(pe):
            pe.sem_inc(state_mm, 2)
            with pe.Fori(0, NT // 2) as i:
                for s in range(2):
                    t = 2 * i + s
                    pe.wait_ge(scaled_f, t + 1)
                    pe.wait_ge(scaled_b, t + 1)
                    pe.wait_ge(saved, t + 1)
                    for n in range(2):
                        for g in range(2):
                            mm = pe.matmul(pp[n][s][g * 64:(g + 1) * 64, :], xb[s][:, D + g * 64:D + (g + 1) * 64],
                                           xd[n][s][:, g * 512:(g + 1) * 512], start=True, stop=True)
                    mm.then_inc(state_mm, 1)

        @block.scalar
        def _(act):
            act.sem_inc(saved, 2)
            with act.Fori(0, NT // 2) as i:
                for s in range(2):
                    t = 2 * i + s
                    act.wait_ge(state_mm, t + 3)
                    act.activation(of_chunk(sf, t + 1), pp[0][s][:, :], ACT.Copy)
                    act.activation(of_chunk(sb, t), pp[1][s][:, :], ACT.Copy).then_inc(saved, 1)

        def carry(eng, n, to, frm, at, done, m):
            st = q.st[n]
            eng.tensor_tensor(tmp[n][:, :].rearrange("p (h e) -> p h e", e=SSD_HEAD),
                              st[:, frm, :].rearrange("p (h e) -> p h e", e=SSD_HEAD),
                              per_head(q.et[:, n, at, :]), ALU.mult).then_inc(done, 1)
            eng.wait_ge(done, 2 * m + 1)
            eng.tensor_tensor(st[:, to, :], st[:, to, :], tmp[n][:, :], ALU.add).then_inc(done, 1)
            eng.wait_ge(done, 2 * m + 2)

        @block.vector
        def _(dve):
            with dve.Fori(0, NT // 2) as i:
                for s in range(2):
                    scale(dve, 0, i, s, scaled_f)
            dve.wait_ge(saved, NT + 2)
            for x, slot in ((sf, 0), (sf, QB), (sb, QB), (sb, NT)):
                dve.memset(x[:, slot, :], 0.0).then_inc(zeroed, 1)
            for m, t in enumerate(range(1, QB - 1)):
                carry(dve, 0, t + 1, t, t, chain_f, m)

        @block.gpsimd
        def _(pool):
            with pool.Fori(0, NT // 2) as i:
                for s in range(2):
                    scale(pool, 1, i, s, scaled_b)
            pool.wait_ge(saved, NT + 2)
            for m, p in enumerate(range(QB - 2, 0, -1)):
                carry(pool, 1, p, p + 1, p, chain_b, m)


def stage_ssd_scan(k, q, y_hi, y_lo):
    nc, d = k.nc, k.d
    sf, sb = q.st
    with ExitStack() as ctx:
        at = [O_W + 9 * 1024]

        def tile(name, shape, dtype=F32):
            size = 4 * int(np.prod(shape[1:]))
            if at[0] < O_R1 and at[0] + size > O_R1:
                at[0] = O_ST
            x = k.at("scan_" + name, shape, dtype, at[0])
            at[0] += -(-size // 32) * 32
            return x

        xs = [tile(f"x{s}", [P, D]) for s in range(2)]
        zs = [tile(f"z{s}", [P, D]) for s in range(2)]
        hs = [tile(f"h{s}", [P, 2, 512]) for s in range(2)]
        bc = [tile(f"bc{s}", [P, 2, P]) for s in range(2)]
        xw = tile("xw", [P, 3, D])
        rf = [tile(f"rf{s}", [P, 4, P]) for s in range(2)]
        rb = [tile(f"rb{s}", [P, 4, P]) for s in range(2)]
        mu = [tile(f"mu{s}", [P, 4, P]) for s in range(2)]
        ml = [tile(f"ml{s}", [P, 4, P]) for s in range(2)]
        cbm = tile("cbm", [P, 2, 2, P])
        y = tile("y", [P, D])
        t2 = tile("t2", [P, D])
        gain = k.at("scan_gain", [P, D], F32, O_KEEP)
        dsk = tile("dsk", [P, N_SSD])
        stat = tile("stat", [P, 3, 2])
        nh = tile("nh", [P, 2])
        assert at[0] <= 229368, at[0]
        seg = [ctx.enter_context(nc.psum_tensor(f"scan_seg{s}", [P, 4, P], F32)) for s in range(2)]
        cbp = ctx.enter_context(nc.psum_tensor("scan_cb", [P, 2, P], F32))
        yp = ctx.enter_context(nc.psum_tensor("scan_y", [P, D], F32))
        yo = ctx.enter_context(nc.psum_tensor("scan_yo", [P, 2, 512], F32))
        tr = ctx.enter_context(nc.psum_tensor("scan_tr", [P, 4, P], F32))
        ld = k.sems(ctx, "scan_ld0", "scan_ld1")
        names = ("par_in", "nh_set", "x_dt", "x_skip", "r_ready", "seg_done", "exped", "m_ready", "m_used", "cb_done",
                 "cb_masked", "yo_done", "yo_read", "y_mm", "y_read", "turned", "hi_done", "lo_done", "y_step", "gated",
                 "squared", "var", "rstd", "ydone", "cb_half")
        (par_in, nh_set, x_dt, x_skip, r_ready, seg_done, exped, m_ready, m_used, cb_done, cb_masked, yo_done, yo_read,
         y_mm, y_read, turned, hi_done, lo_done, y_step, gated, squared, var, rstd, ydone, cb_half) = k.sems(
             ctx, *(f"scan_{n}" for n in names))
        ident = k.const[:, C_ID:C_ID + P]

        def heads(x, width=SSD_HEAD):
            return x.rearrange("p (h e) -> p h e", e=width)

        def chunks(eng, body):
            body(0, 0, True, False)
            with eng.Fori(0, NT // 2 - 1) as i:
                body(2 * i + 1, 1, False, False)
                body(2 * i + 2, 0, False, False)
            body(NT - 1, 1, False, True)

        block = ctx.enter_context(nc.Block())

        @block.sync
        def _(sp):
            sp.dma_start(gain[:, :], d["norm_g"].partition_broadcast(P)).then_inc(par_in, 16)
            sp.dma_start(dsk[:, :], d["d_skip"].partition_broadcast(P)).then_inc(par_in, 16)

            def body(t, s, first, last):
                sp.wait_ge(ydone, t + 1)
                sp.dma_start(xs[s][:, :], d["xtok"][ds(t * P, P), 0:D]).then_inc(ld[s], 16)
                sp.dma_start(zs[s][:, :], d["ztok"][ds(t * P, P), :]).then_inc(ld[s], 16)
                sp.dma_start(bc[s][:, :, :], d["bc"][:, ds(t * P, P)].rearrange("(m p) t -> p m t", p=P)).then_inc(ld[s], 16)
                sp.dma_start(hs[s][:, 0, :], of_chunk(sf, t)).then_inc(ld[s], 16)
                sp.dma_start(hs[s][:, 1, :], of_chunk(sb, t + 1)).then_inc(ld[s], 16)

            chunks(sp, body)

        def loaded(t, s):
            return 40 * (t - s) + 80

        @block.gpsimd
        def _(pool):
            pool.memset(nh[:, :], -0.5).then_inc(nh_set, 1)

            def spans(t, quad):
                n = 4 * t + quad
                pool.wait_ge(seg_done, n + 1)
                for r, mask, first in ((rf, C_INCU, 0), (rb, C_INCL, 16)):
                    m = k.const[:, mask:mask + P].unsqueeze(1).to_broadcast([P, 4, P])
                    h = of_chunk(q.dta[:, :, first + 4 * quad:first + 4 * quad + 4], t)
                    ins = pool.tensor_tensor(r[quad % 2][:, :, :], m, per_head(h, P), ALU.mult)
                ins.then_inc(r_ready, 1)

            def body(t, s, first, last):
                pool.wait_ge(ld[s], loaded(t, s))
                pool.wait_ge(y_mm, t + 1)
                pool.tensor_tensor(heads(xw[:, 2, :]), heads(xs[s][:, :]), per_head(dsk[:, :]), ALU.mult).then_inc(x_skip, 1)
                spans(t, 2)
                spans(t, 3)
                if not last:
                    spans(t + 1, 0)
                    spans(t + 1, 1)
                pool.wait_ge(var, t + 1)
                pool.tensor_tensor(stat[:, 2, :], stat[:, 1, :], nh[:, :], ALU.pow).then_inc(rstd, 1)

            pool.wait_ge(par_in, 32)
            pool.wait_ge(nh_set, 1)
            spans(0, 0)
            spans(0, 1)
            chunks(pool, body)

        @block.tensor
        def _(pe):
            def sums(t, quad):
                n = 4 * t + quad
                pe.wait_ge(r_ready, n + 1)
                pe.wait_ge(exped, n + 1)
                out = seg[quad % 2][:, :, :]
                pe.matmul(out, k.const[:, C_GT:C_GT + P], rf[quad % 2][:, :, :], start=True, stop=False)
                pe.matmul(out, k.const[:, C_LT:C_LT + P], rb[quad % 2][:, :, :], start=False, stop=True).then_inc(seg_done, 1)

            def apply(t, quad):
                pe.wait_ge(m_ready, 4 * t + quad + 3)
                for m in range(4):
                    c = slice((4 * quad + m) * SSD_HEAD, (4 * quad + m + 1) * SSD_HEAD)
                    pe.matmul(yp[:, c], mu[quad % 2][:, m, :], xw[:, 0, c], start=False, stop=False)
                    mm = pe.matmul(yp[:, c], ml[quad % 2][:, m, :], xw[:, 1, c], start=False, stop=(m == 3 and quad % 2 == 1))
                mm.then_inc(m_used, 1)

            def carried(t, s, n):
                pe.wait_ge(yo_read, 2 * t + n + 1)
                for g in range(2):
                    mm = pe.matmul(yo[:, g, :], bc[s][g * 64:(g + 1) * 64, 1, :], hs[s][g * 64:(g + 1) * 64, n, :],
                                   start=True, stop=True)
                mm.then_inc(yo_done, 1)

            def turn(t, r):
                pe.wait_ge(ydone, t + 3)
                pe.wait_ge(lo_done, 2 * t + r + 1)
                for m in range(4):
                    c = 4 * r + m
                    mm = pe.transpose(tr[:, m, :], y[:, c * P:(c + 1) * P], ident)
                mm.then_inc(turned, 1)

            def body(t, s, first, last):
                pe.wait_ge(ld[s], loaded(t, s))
                pe.wait_ge(cb_masked, t + 1)
                for g in range(2):
                    mm = pe.matmul(cbp[:, g, :], bc[s][g * 64:(g + 1) * 64, 0, :], bc[s][g * 64:(g + 1) * 64, 1, :],
                                   start=True, stop=True)
                    if g == 0:
                        mm.then_inc(cb_half, 1)
                        pe.wait_ge(cb_half, t + 1)
                mm.then_inc(cb_done, 1)
                sums(t, 0)
                sums(t, 1)
                pe.wait_ge(x_skip, t + 1)
                pe.wait_ge(y_read, t + 1)
                for g in range(2):
                    pe.matmul(yp[:, g * 512:(g + 1) * 512], ident, xw[:, 2, g * 512:(g + 1) * 512], start=True, stop=False)
                carried(t, s, 0)
                pe.wait_ge(x_dt, t + 1)
                apply(t, 0)
                sums(t, 2)
                if not first:
                    turn(t - 1, 0)
                apply(t, 1)
                sums(t, 3)
                apply(t, 2)
                if not first:
                    turn(t - 1, 1)
                apply(t, 3)
                carried(t, s, 1)

            pe.sem_inc(seg_done, 2)
            pe.sem_inc(m_used, 2)
            chunks(pe, body)
            turn(NT - 1, 0)
            turn(NT - 1, 1)

        @block.scalar
        def _(act):
            act.sem_inc(exped, 2)

            def exp(t, quad):
                n = 4 * t + quad
                act.wait_ge(seg_done, n + 3)
                act.wait_ge(m_used, n + 1)
                act.activation(mu[quad % 2][:, :, :], seg[quad % 2][:, :, :], ACT.Exp).then_inc(exped, 1)

            def split(t, r):
                act.wait_ge(turned, 2 * t + r + 1)
                act.activation(y_hi[:, 4 * r:4 * r + 4, ds(t * P, P)], tr[:, :, :], ACT.Copy).then_inc(hi_done, 1)

            def body(t, s, first, last):
                exp(t, 0)
                exp(t, 1)
                exp(t, 2)
                if not first:
                    split(t - 1, 0)
                exp(t, 3)
                if not first:
                    split(t - 1, 1)
                act.wait_ge(gated, t + 1)
                for g in range(2):
                    ins = act.activation(t2[:, g * 512:(g + 1) * 512], y[:, g * 512:(g + 1) * 512], ACT.Square,
                                         accum_out=stat[:, 0, g:g + 1])
                ins.then_inc(squared, 1)

            chunks(act, body)
            split(NT - 1, 0)
            split(NT - 1, 1)

        @block.vector
        def _(dve):
            dve.sem_inc(m_ready, 2)
            dve.sem_inc(cb_masked, 1)
            dve.sem_inc(yo_read, 1)
            dve.sem_inc(y_read, 1)
            dve.sem_inc(y_mm, 1)
            dve.sem_inc(ydone, 2)
            dve.sem_inc(lo_done, 1)
            dve.wait_ge(par_in, 32)

            def weigh(t, quad):
                n = 4 * t + quad
                dve.wait_ge(exped, n + 3)
                dve.wait_ge(m_used, n + 1)
                for out, half in ((ml, 1), (mu, 0)):
                    ins = dve.tensor_tensor(out[quad % 2][:, :, :], mu[quad % 2][:, :, :],
                                            cbm[:, half, quad // 2, :].unsqueeze(1).to_broadcast([P, 4, P]), ALU.mult)
                ins.then_inc(m_ready, 1)

            def rest(t, r):
                dve.wait_ge(hi_done, 2 * t + r + 1)
                dve.tensor_tensor(y_lo[:, 4 * r:4 * r + 4, ds(t * P, P)], tr[:, :, :],
                                  y_hi[:, 4 * r:4 * r + 4, ds(t * P, P)].bitcast(F32), ALU.subtract).then_inc(lo_done, 1)

            def body(t, s, first, last):
                dve.wait_ge(ld[s], loaded(t, s))
                for n in range(2):
                    ins = dve.tensor_tensor(heads(xw[:, n, :]), heads(xs[s][:, :]),
                                            per_head(of_chunk(q.dt[:, :, n * 16:(n + 1) * 16], t)), ALU.mult)
                ins.then_inc(x_dt, 1)
                dve.wait_ge(cb_done, t + 1)
                for half, mask in ((0, C_INCU), (1, C_INCL)):
                    ins = dve.tensor_tensor(cbm[:, half, :, :], cbp[:, :, :],
                                            k.const[:, mask:mask + P].unsqueeze(1).to_broadcast([P, 2, P]), ALU.mult)
                ins.then_inc(cb_masked, 1)
                dve.wait_ge(cb_masked, t + 2)
                weigh(t, 0)
                weigh(t, 1)
                if not first:
                    rest(t - 1, 0)
                weigh(t, 2)
                if not first:
                    rest(t - 1, 1)
                weigh(t, 3)
                dve.wait_ge(yo_done, 2 * t + 1)
                dve.tensor_tensor(heads(y[:, :]), yo[:, :, :].rearrange("p g (h e) -> p (g h) e", e=SSD_HEAD),
                                  per_head(of_chunk(q.inc_f, t)), ALU.mult).then_inc(yo_read, 1)
                dve.wait_ge(m_used, 4 * t + 6)
                dve.wait_ge(yo_read, 2 * t + 2)
                dve.tensor_tensor(y[:, :], yp[:, :], y[:, :], ALU.add).then_inc(y_read, 1)
                dve.wait_ge(yo_done, 2 * t + 2)
                dve.tensor_tensor(heads(t2[:, :]), yo[:, :, :].rearrange("p g (h e) -> p (g h) e", e=SSD_HEAD),
                                  per_head(of_chunk(q.inc_b, t)), ALU.mult).then_inc(yo_read, 1)
                dve.wait_ge(yo_read, 2 * t + 3)
                dve.sem_inc(y_mm, 1)
                dve.tensor_tensor(y[:, :], y[:, :], t2[:, :], ALU.add).then_inc(y_step, 1)
                dve.wait_ge(y_step, 2 * t + 1)
                dve.tensor_tensor(y[:, :], y[:, :], zs[s][:, :], ALU.mult).then_inc(gated, 1)
                dve.wait_ge(squared, t + 1)
                dve.tensor_scalar(stat[:, 1, :], stat[:, 0, :], 1.0 / 512, EPS, ALU.mult, ALU.add).then_inc(var, 1)
                dve.wait_ge(rstd, t + 1)
                for g in range(2):
                    ins = dve.scalar_tensor_tensor(out=y[:, g * 512:(g + 1) * 512], in0=y[:, g * 512:(g + 1) * 512],
                                                   scalar=stat[:, 2, g:g + 1], in1=gain[:, g * 512:(g + 1) * 512],
                                                   op0=ALU.mult, op1=ALU.mult)
                    ins.then_inc(ydone if g else y_step, 1)

            chunks(dve, body)
            rest(NT - 1, 0)
            rest(NT - 1, 1)



def stage_residual_out(k, mixed, hi, lo, x1):
    nc, d = k.nc, k.d
    with ExitStack() as ctx:
        raw, whi, wlo = weight_ring(k, "out")
        xin = [k.at(f"out_x{s}", [P, 512], F32, O_ST + 2048 * s) for s in range(2)]
        zp = [ctx.enter_context(nc.psum_tensor(f"out_p{b}", [P, 512], F32)) for b in range(5)]
        w_in = k.sems(ctx, *(f"out_w_in{s}" for s in range(4)))
        x_in = k.sems(ctx, "out_x_in0", "out_x_in1")
        w_hi, w_lo, unit_done, tile_done, added, m_hi, m_lo = k.sems(
            ctx, "out_w_hi", "out_w_lo", "out_unit", "out_tile", "out_added", "out_m_hi", "out_m_lo")
        block = ctx.enter_context(nc.Block())

        @block.sync
        def _(sp):
            for n in range(4):
                sp.dma_start(raw[:, n, :], d["units"][U_OUT + n]).then_inc(w_in[n], 16)
            for n in range(4):
                sp.wait_ge(w_lo, n + 1)
                sp.dma_start(raw[:, n, :], d["units"][U_OUT + 4 + n]).then_inc(w_in[n], 16)
            for c in range(2):
                with sp.Fori(0, NT // 2) as i:
                    for s in range(2):
                        t = 2 * i + s
                        sp.wait_ge(added, t + (NT * c + 4))
                        sp.dma_start(xin[s][:, :], d["x"][ds(t * P, P), c * 512:(c + 1) * 512]).then_inc(x_in[s], 16)

        @block.scalar
        def _(act):
            for n in range(4):
                act.wait_ge(w_in[n], 16)
                act.activation(whi[:, n, :], raw[:, n, :], ACT.Copy).then_inc(w_hi, 1)
            with act.Fori(0, KT) as i:
                act.activation(of_chunk(hi, i), of_chunk(mixed, i), ACT.Copy).then_inc(m_hi, 1)
            for n in range(4):
                act.wait_ge(w_in[n], 32)
                if n < 3:
                    act.wait_ge(unit_done, n + 1)
                else:
                    act.wait_ge(tile_done, NT)
                act.activation(whi[:, n, :], raw[:, n, :], ACT.Copy).then_inc(w_hi, 1)

        @block.gpsimd
        def _(pool):
            for c in range(2):
                for n in range(4):
                    pool.wait_ge(w_hi, 4 * c + n + 1)
                    pool.tensor_tensor(wlo[:, n, :], raw[:, n, :], whi[:, n, :].bitcast(F32), ALU.subtract).then_inc(w_lo, 1)

        @block.tensor
        def _(pe):
            pe.wait_ge(m_lo, KT)
            for c in range(2):
                pe.wait_ge(w_lo, 4 * c + 4)
                for t in range(NT):
                    pe.wait_ge(added, NT * c + t + 1)
                    last = c == 0 and t == NT - 1
                    pe_token_tile(pe, zp[t % 5][:, :], hi, lo, t, whi, wlo, KT, unit_done if last else None
                                  ).then_inc(tile_done, 1)

        @block.vector
        def _(dve):
            dve.sem_inc(added, 5)
            with dve.Fori(0, KT) as i:
                dve.wait_ge(m_hi, i + 1)
                dve.tensor_tensor(of_chunk(lo, i), of_chunk(mixed, i), of_chunk(hi, i).bitcast(F32),
                                  ALU.subtract).then_inc(m_lo, 1)
            dve.wait_ge(m_lo, KT)
            for c in range(2):
                for t in range(NT):
                    dve.wait_ge(x_in[t % 2], 16 * (5 * c + t // 2 + 1))
                    dve.wait_ge(tile_done, NT * c + t + 1)
                    dve.tensor_tensor(x1[:, t, c * 512:(c + 1) * 512], zp[t % 5][:, :], xin[t % 2][:, :],
                                      ALU.add).then_inc(added, 1)



class Routing:

    def __init__(self, k):
        o = O_KEEP
        self.logits = k.at("logits", [P, NT, 20], F32, o)
        self.weight = k.at("pair_weight", [P, 2, NT], F32, o + 800)
        self.slot = k.at("pair_slot", [P, 2, NT], I32, o + 896)
        self.expert = k.at("block_expert", [P, NBLK], I32, o + 992)
        self.ids = k.at("token_ids", [P, NT], I32, o + 1152)


def stage_norm_route(k, x1, r):
    nc, d = k.nc, k.d
    with ExitStack() as ctx:
        gb = k.at("nr_g", [P, D], F32, O_W)
        nh = k.at("nr_nh", [P, 1], F32, O_W + 4096)
        st = k.at("nr_st", [P, 2, 4], F32, O_W + 4128)
        rw = k.at("nr_rw", [P, KT, 20], F32, O_W + 4160)
        rb = k.at("nr_rb", [P, 20], F32, O_W + 4800)
        xn = k.at("nr_xn", [P, 2, D], F32, O_W + 8192)
        junk = k.at("nr_j", [P, 2, D], F32, O_W + 16384)
        ht = k.at("nr_ht", [P, 2, KT, P], F32, O_W + 24576)
        tp = [ctx.enter_context(nc.psum_tensor(f"nr_tp{s}", [P, KT, P], F32)) for s in range(2)]
        lp = ctx.enter_context(nc.psum_tensor("nr_lg", [P, NT, 20], F32))
        stored = k.sems(ctx, "nr_stored0", "nr_stored1")
        par_in, half_set, squared, scaled, rstd, normed, turned, copied, routed = k.sems(
            ctx, *(f"nr_{n}" for n in ("par_in", "half_set", "squared", "scaled", "rstd", "normed", "turned", "copied",
                                       "routed")))
        ident = k.const[:, C_ID:C_ID + P]
        block = ctx.enter_context(nc.Block())

        @block.sync
        def _(sp):
            sp.sem_inc(stored[0], 16)
            sp.sem_inc(stored[1], 16)
            sp.dma_start(gb[:, :], d["g_ffn"].partition_broadcast(P)).then_inc(par_in, 16)
            sp.dma_start(rw[:, :, :], d["router"]).then_inc(par_in, 16)
            sp.dma_start(rb[:, :], d["router_b"].partition_broadcast(P)).then_inc(par_in, 16)
            sp.dma_start(r.ids[:, :], d["ids"]).then_inc(par_in, 16)
            with sp.Fori(0, NT // 2) as i:
                for s in range(2):
                    sp.wait_ge(normed, 2 * i + s + 3)
                    sp.dma_start(d["h2"][ds((2 * i + s) * P, P), :], xn[:, s, :]).then_inc(stored[s], 16)
            sp.wait_ge(stored[0], 96)
            sp.wait_ge(stored[1], 96)

        @block.gpsimd
        def _(pool):
            pool.memset(nh[:, :], -0.5).then_inc(half_set, 1)
            pool.wait_ge(half_set, 1)
            with pool.Fori(0, NT // 2) as i:
                for s in range(2):
                    pool.wait_ge(scaled, 2 * i + s + 1)
                    pool.tensor_tensor(st[:, s, 2:3], st[:, s, 1:2], nh[:, :], ALU.pow).then_inc(rstd, 1)

        @block.scalar
        def _(act):
            act.sem_inc(copied, 2)

            def square(t, s):
                act.wait_ge(normed, t + 1)
                act.activation(junk[:, s, :], of_chunk(x1, t), ACT.Square,
                               accum_out=st[:, s, 0:1]).then_inc(squared, 1)

            def copy(t, s):
                act.wait_ge(turned, t + 3)
                act.wait_ge(routed, t + 1)
                act.activation(ht[:, s, :, :], tp[s][:, :, :], ACT.Copy).then_inc(copied, 1)

            square(0, 0)
            with act.Fori(0, NT // 2 - 1) as i:
                square(2 * i + 1, 1)
                copy(2 * i, 0)
                square(2 * i + 2, 0)
                copy(2 * i + 1, 1)
            square(NT - 1, 1)
            copy(NT - 2, 0)
            copy(NT - 1, 1)

        @block.vector
        def _(dve):
            dve.sem_inc(normed, 2)
            dve.wait_ge(par_in, 64)
            with dve.Fori(0, NT // 2) as i:
                for s in range(2):
                    t = 2 * i + s
                    dve.wait_ge(squared, t + 1)
                    dve.tensor_scalar(st[:, s, 1:2], st[:, s, 0:1], 1.0 / D, EPS, ALU.mult, ALU.add).then_inc(scaled, 1)
                    dve.wait_ge(rstd, t + 1)
                    dve.wait_ge(stored[s], 16 * (i + 1))
                    dve.wait_ge(turned, t + 1)
                    dve.scalar_tensor_tensor(out=xn[:, s, :], in0=of_chunk(x1, t), scalar=st[:, s, 2:3], in1=gb[:, :],
                                             op0=ALU.mult, op1=ALU.mult).then_inc(normed, 1)
            dve.wait_ge(routed, NT + 2)
            dve.tensor_tensor(r.logits[:, :, :], lp[:, :, :], rb[:, :].unsqueeze(1).to_broadcast([P, NT, 20]), ALU.add)

        @block.tensor
        def _(pe):
            pe.sem_inc(routed, 2)
            pe.sem_inc(turned, 2)

            def turn(t, s):
                pe.wait_ge(normed, t + 3)
                pe.wait_ge(copied, t + 1)
                for c in range(KT):
                    mm = pe.transpose(tp[s][:, c, :], xn[:, s, c * P:(c + 1) * P], ident)
                mm.then_inc(turned, 1)

            def logits(t, s):
                pe.wait_ge(copied, t + 3)
                for c in range(KT):
                    mm = pe.matmul(lp[:, ds(t, 1), :].rearrange("p a n -> p (a n)"), ht[:, s, c, :], rw[:, c, :],
                                   start=(c == 0), stop=(c == KT - 1))
                mm.then_inc(routed, 1)

            pe.wait_ge(par_in, 64)
            turn(0, 0)
            with pe.Fori(0, NT // 2 - 1) as i:
                turn(2 * i + 1, 1)
                logits(2 * i, 0)
                turn(2 * i + 2, 0)
                logits(2 * i + 1, 1)
            turn(NT - 1, 1)
            logits(NT - 2, 0)
            logits(NT - 1, 1)


def stage_route(k, r):
    nc, d = k.nc, k.d
    with ExitStack() as ctx:
        at = [O_W]

        def tile(name, shape, dtype=F32):
            x = k.at("rt_" + name, shape, dtype, at[0])
            at[0] += -(-4 * int(np.prod(shape[1:])) // 32) * 32
            return x

        gmax, gsum, psel = (tile(n, [P, NT]) for n in ("gmax", "gsum", "psel"))
        gexp, geq, goh, sel, sel2, eeq, o1, o2 = (tile(n, [P, NT, 4]) for n in (
            "gexp", "geq", "goh", "sel", "sel2", "eeq", "o1", "o2"))
        m1, m2, e2, mr = (tile(n, [P, NT]) for n in ("m1", "m2", "e2", "mr"))
        wide = tile("wide", [P, NT, 4, 4])
        a1, a2, both, off, w16 = (tile(n, [P, NT, N_EXP]) for n in ("a1", "a2", "both", "off", "w16"))
        base = tile("base", [P, NT + 1, N_EXP])
        over = tile("over", [P, N_EXP, NT])
        nb, upto, first, ones = (tile(n, [P, N_EXP]) for n in ("nb", "upto", "first", "ones"))
        past = tile("past", [P, NBLK, N_EXP])
        bex = tile("bex", [P, NBLK])
        slot = tile("slot", [P, 2, NT])
        zero = tile("zero", [P, NBLK], I32)
        pp = [ctx.enter_context(nc.psum_tensor(f"rt_p{n}", [P, 512], F32)) for n in range(2)]
        chain, exps, counted, table_zero, slots_ready, zero_set = k.sems(
            ctx, "rt_chain", "rt_exps", "rt_counted", "rt_table_zero", "rt_slots", "rt_zero")
        scattered = k.sems(ctx, "rt_scattered0", "rt_scattered1")
        pair_done, exp_in = k.sems(ctx, "rt_pairs", "rt_exp_in")
        rank = k.const[:, C_RANK:C_RANK + 4].unsqueeze(1).to_broadcast([P, NT, 4])
        block = ctx.enter_context(nc.Block())

        @block.vector
        def _(dve):
            steps = [0]

            def step(ins):
                steps[0] += 1
                ins.then_inc(chain, 1)
                dve.wait_ge(chain, steps[0])

            def over4(x):
                return x.unsqueeze(2).to_broadcast([P, NT, 4])

            def first_max(x, top, hot):
                step(dve.tensor_reduce(top, x, AX.X, ALU.max))
                step(dve.tensor_tensor(hot, x, over4(top), ALU.is_equal))
                step(dve.tensor_tensor(hot, hot, rank, ALU.mult))
                step(dve.tensor_reduce(mr[:, :], hot, AX.X, ALU.max))
                step(dve.tensor_tensor(hot, hot, over4(mr[:, :]), ALU.is_equal))

            dve.memset(zero[:, :], 0).then_inc(zero_set, 1)
            dve.memset(base[:, 0, :], 0.0)
            dve.memset(ones[:, :], 1.0)
            lg, le = r.logits[:, :, 0:4], r.logits[:, :, 4:20].rearrange("p t (g e) -> p t g e", g=4)
            first_max(lg, gmax[:, :], goh[:, :, :])
            dve.tensor_tensor(gexp[:, :, :], lg, over4(gmax[:, :]), ALU.subtract).then_inc(exp_in, 1)
            step(dve.tensor_tensor(wide[:, :, :, :], le, goh[:, :, :].unsqueeze(3).to_broadcast([P, NT, 4, 4]), ALU.mult))
            step(dve.tensor_reduce(sel[:, :, :], wide[:, :, :, :].rearrange("p t g e -> p t e g"), AX.X, ALU.add))
            first_max(sel[:, :, :], m1[:, :], o1[:, :, :])
            step(dve.scalar_tensor_tensor(out=sel2[:, :, :], in0=o1[:, :, :], scalar=NEG, in1=sel[:, :, :], op0=ALU.mult,
                                          op1=ALU.add))
            first_max(sel2[:, :, :], m2[:, :], o2[:, :, :])
            dve.tensor_tensor(e2[:, :], m2[:, :], m1[:, :], ALU.subtract).then_inc(exp_in, 1)
            for a, o in ((a1, o1), (a2, o2)):
                step(dve.tensor_tensor(a[:, :, :].rearrange("p t (g e) -> p t g e", g=4),
                                       goh[:, :, :].unsqueeze(3).to_broadcast([P, NT, 4, 4]),
                                       o[:, :, :].unsqueeze(2).to_broadcast([P, NT, 4, 4]), ALU.mult))
            dve.tensor_tensor(both[:, :, :], a1[:, :, :], a2[:, :, :], ALU.add).then_inc(pair_done, 1)
            dve.wait_ge(exps, 1)
            step(dve.tensor_reduce(gsum[:, :], gexp[:, :, :], AX.X, ALU.add))
            step(dve.reciprocal(psel[:, :], gsum[:, :]))
            dve.wait_ge(exps, 2)
            step(dve.tensor_scalar(m1[:, :], e2[:, :], 1.0, None, ALU.add))
            step(dve.reciprocal(m2[:, :], m1[:, :]))
            step(dve.tensor_tensor(r.weight[:, 0, :], m2[:, :], psel[:, :], ALU.mult))
            step(dve.tensor_tensor(r.weight[:, 1, :], e2[:, :], r.weight[:, 0, :], ALU.mult))
            dve.wait_ge(counted, 1)
            tot = pp[1][:, 0:160].rearrange("p (t e) -> p t e", t=NT)
            for t in range(NT):
                step(dve.tensor_tensor(base[:, t + 1, :], tot[:, t, :], base[:, t, :], ALU.add))
            step(dve.tensor_tensor(over[:, :, :], base[:, NT, :].unsqueeze(2).to_broadcast([P, N_EXP, NT]),
                                   k.const[:, C_TH:C_TH + NT].unsqueeze(1).to_broadcast([P, N_EXP, NT]), ALU.is_gt))
            step(dve.tensor_reduce(nb[:, :], over[:, :, :], AX.X, ALU.add))
            step(dve.tensor_tensor_scan(upto[:, :], ones[:, :], nb[:, :], 0.0, ALU.mult, ALU.add))
            step(dve.tensor_tensor(first[:, :], upto[:, :], nb[:, :], ALU.subtract))
            step(dve.tensor_tensor(off[:, :, :], pp[0][:, 0:160].rearrange("p (t e) -> p t e", t=NT), base[:, 0:NT, :], ALU.add))
            step(dve.scalar_tensor_tensor(out=off[:, :, :], in0=first[:, :].unsqueeze(1).to_broadcast([P, NT, N_EXP]),
                                          scalar=float(P), in1=off[:, :, :], op0=ALU.mult, op1=ALU.add))
            for n, a in enumerate((a1, a2)):
                step(dve.tensor_tensor(w16[:, :, :], a[:, :, :], off[:, :, :], ALU.mult))
                step(dve.tensor_reduce(slot[:, n, :], w16[:, :, :], AX.X, ALU.add))
            dve.tensor_copy(r.slot[:, :, :], slot[:, :, :]).then_inc(slots_ready, 1)
            step(dve.tensor_tensor(past[:, :, :], upto[:, :].unsqueeze(1).to_broadcast([P, NBLK, N_EXP]),
                                   k.const[:, C_IOTA:C_IOTA + NBLK].unsqueeze(2).to_broadcast([P, NBLK, N_EXP]), ALU.is_le))
            step(dve.tensor_reduce(bex[:, :], past[:, :, :], AX.X, ALU.add))
            dve.tensor_scalar(r.expert[:, :], bex[:, :], float(N_EXP - 1), None, ALU.min)

        @block.scalar
        def _(act):
            act.preload_act_table(ACT.Exp)
            act.wait_ge(exp_in, 1)
            act.activation(gexp[:, :, :], gexp[:, :, :], ACT.Exp).then_inc(exps, 1)
            act.wait_ge(exp_in, 2)
            act.activation(e2[:, :], e2[:, :], ACT.Exp).then_inc(exps, 1)

        @block.tensor
        def _(pe):
            pe.wait_ge(pair_done, 1)
            rhs = both[:, :, :]
            for n, mask in ((0, C_LT), (1, C_ONE)):
                mm = pe.matmul(pp[n][:, 0:160].rearrange("p (t e) -> p t e", t=NT), k.const[:, mask:mask + P], rhs,
                               start=True, stop=True)
            mm.then_inc(counted, 1)

        @block.gpsimd
        def _(pool):
            pool.wait_ge(zero_set, 1)
            pool.dma_start(d["slots"].rearrange("(p n) o -> p (n o)", p=P), zero[:, :]).then_inc(table_zero, 16)
            pool.wait_ge(table_zero, 16)
            pool.wait_ge(slots_ready, 1)
            for n in range(2):
                for t in range(NT):
                    pool.indirect_dma_start(
                        out=d["slots"], out_offset=bass.IndirectOffsetOnAxis(ap=r.slot[:, n, t:t + 1].bitcast(U32), axis=0),
                        in_=r.ids[:, t:t + 1], in_offset=None).then_inc(scattered[n], 16)
            pool.wait_ge(scattered[0], 16 * NT)
            pool.wait_ge(scattered[1], 16 * NT)



def stage_experts(k, r):
    nc, d = k.nc, k.d
    with ExitStack() as ctx:
        raw = k.at("ex_raw", [P, 6, 1024], F32, O_W)
        whi = k.at("ex_whi", [P, 6, 1024], F32R, O_W + 6 * 4096)
        wlo = k.at("ex_wlo", [P, 6, 1024], F32R, O_W + 12 * 4096)
        o = O_W + 18 * 4096
        idx = [k.at(f"ex_idx{s}", [P, 1], I32, o + 32 * s) for s in range(2)]
        xg = [k.at(f"ex_x{s}", [P, D], F32, o + 64 + 4096 * s) for s in range(2)]
        xh = k.at("ex_xh", [P, KT, P], F32R, o + 64 + 8192)
        xl = k.at("ex_xl", [P, KT, P], F32R, o + 64 + 12288)
        act_t = k.at("ex_silu", [P, F], F32, o + 64 + 16384)
        hid = k.at("ex_hid", [P, F], F32, o + 64 + 17408)
        ah = k.at("ex_ah", [P, 2, P], F32R, o + 64 + 18432)
        al = k.at("ex_al", [P, 2, P], F32R, o + 64 + 19456)
        ys = [k.at(f"ex_y{s}", [P, D], F32, o + 64 + 20480 + 4096 * s) for s in range(2)]
        tx = ctx.enter_context(nc.psum_tensor("ex_tx", [P, KT, P], F32))
        gu = [ctx.enter_context(nc.psum_tensor(f"ex_gu{s}", [P, 2 * F], F32)) for s in range(2)]
        ta = ctx.enter_context(nc.psum_tensor("ex_ta", [P, 2, P], F32))
        yp = ctx.enter_context(nc.psum_tensor("ex_yp", [P, D], F32))
        w_in = k.sems(ctx, *(f"ex_w_in{n}" for n in range(6)))
        w_hi = k.sems(ctx, *(f"ex_w_hi{n}" for n in range(6)))
        w_lo = k.sems(ctx, *(f"ex_w_lo{n}" for n in range(6)))
        w_used = k.sems(ctx, *(f"ex_w_used{n}" for n in range(6)))
        idx_in = k.sems(ctx, "ex_idx_in0", "ex_idx_in1")
        x_in = k.sems(ctx, "ex_x_in0", "ex_x_in1")
        stored = k.sems(ctx, "ex_stored0", "ex_stored1")
        names = ("x_turned", "x_hi", "x_lo", "silu", "hid", "a_turned", "a_hi", "a_lo", "y_copied")
        (x_turned, x_hi, x_lo, silu, hid_done, a_turned, a_hi, a_lo, y_copied) = k.sems(
            ctx, *(f"ex_{n}" for n in names))
        ident = k.const[:, C_ID:C_ID + P]
        block = ctx.enter_context(nc.Block())

        def blocks(eng, body):
            body(0, 0, True, False)
            with eng.Fori(0, NBLK // 2 - 1) as i:
                body(2 * i + 1, 1, False, False)
                body(2 * i + 2, 0, False, False)
            body(NBLK - 1, 1, False, True)

        @block.sync
        def _(sp):
            sp.sem_inc(stored[0], 16)
            sp.sem_inc(stored[1], 16)

            def weights(b, units):
                e = sp.value_load(r.expert[0:1, ds(b, 1)], min_val=0, max_val=N_EXP - 1)
                for n in units:
                    sp.wait_ge(w_lo[n], b + 1)
                    sp.dma_start(raw[:, n, :], d["experts"][ds(e * (6 * P) + n * P, P), :]).then_inc(w_in[n], 16)

            def index(b, s):
                sp.wait_ge(x_turned, b + 1)
                sp.dma_start(idx[s][:, :], d["slots"][ds(b * P, P), :]).then_inc(idx_in[s], 16)

            def store(b, s):
                sp.wait_ge(y_copied, b + 2)
                sp.dma_start(d["y_slots"][ds(b * P, P), :], ys[s][:, :]).then_inc(stored[s], 16)

            index(0, 0)
            index(1, 1)
            weights(0, range(6))

            def body(b, s, first, last):
                if not last:
                    weights(b + 1, range(4))
                    index(b + 2, s)
                if not first:
                    store(b - 1, 1 - s)
                if not last:
                    weights(b + 1, (4, 5))

            body(0, 0, True, False)
            with sp.Fori(0, NBLK // 2 - 2) as i:
                body(2 * i + 1, 1, False, False)
                body(2 * i + 2, 0, False, False)
            for b in (NBLK - 3, NBLK - 2):
                weights(b + 1, range(4))
                if b == NBLK - 3:
                    index(b + 2, b % 2)
                store(b - 1, (b - 1) % 2)
                weights(b + 1, (4, 5))
            store(NBLK - 2, 0)
            store(NBLK - 1, 1)
            sp.wait_ge(stored[0], 16 * (NBLK // 2 + 1))
            sp.wait_ge(stored[1], 16 * (NBLK // 2 + 1))

        def split_hi(eng, b, n):
            eng.wait_ge(w_in[n], 16 * b + 16)
            eng.wait_ge(w_used[n], b + 1)
            if eng is nc.scalar:
                eng.activation(whi[:, n, :], raw[:, n, :], ACT.Copy).then_inc(w_hi[n], 1)
            else:
                eng.tensor_copy(whi[:, n, :], raw[:, n, :]).then_inc(w_hi[n], 1)

        def split_lo(eng, b, n):
            eng.wait_ge(w_hi[n], b + 1)
            eng.tensor_tensor(wlo[:, n, :], raw[:, n, :], whi[:, n, :].bitcast(F32), ALU.subtract).then_inc(w_lo[n], 1)

        @block.gpsimd
        def _(pool):
            for n in (1, 3, 5):
                pool.sem_inc(w_lo[n], 1)

            def may_gather(b, s):
                pool.wait_ge(idx_in[s], 8 * (b - s) + 16)
                pool.wait_ge(x_turned, b + 1)

            def gather(b, s):
                pool.indirect_dma_start(out=xg[s][:, :], out_offset=None, in_=d["h2"],
                                        in_offset=bass.IndirectOffsetOnAxis(ap=idx[s][:, 0:1].bitcast(U32), axis=0)
                                        ).then_inc(x_in[s], 16)

            for b in range(2):
                may_gather(b, b)
                gather(b, b)
            split_lo(pool, 0, 1)
            split_lo(pool, 0, 3)

            def body(b, s, first, last, more=True):
                if not last:
                    split_lo(pool, b + 1, 1)
                    split_lo(pool, b + 1, 3)
                if more:
                    may_gather(b + 2, s)
                split_lo(pool, b, 5)
                if more:
                    gather(b + 2, s)

            body(0, 0, True, False)
            with pool.Fori(0, NBLK // 2 - 2) as i:
                body(2 * i + 1, 1, False, False)
                body(2 * i + 2, 0, False, False)
            body(NBLK - 3, 1, False, False)
            body(NBLK - 2, 0, False, False, more=False)
            body(NBLK - 1, 1, False, True, more=False)

        @block.tensor
        def _(pe):
            def turn_x(b, s):
                pe.wait_ge(x_in[s], 8 * (b - s) + 16)
                pe.wait_ge(x_lo, b + 1)
                for c in range(KT):
                    mm = pe.transpose(tx[:, c, :], xg[s][:, c * P:(c + 1) * P], ident)
                mm.then_inc(x_turned, 1)

            def gate_up(b, s):
                pe.wait_ge(x_lo, b + 2)
                pe.wait_ge(hid_done, b + 1)
                for n in range(4):
                    pe.wait_ge(w_lo[n], b + 2)
                    for j in range(2):
                        kk, c = 2 * n + j, slice(512 * j, 512 * j + 512)
                        pe.matmul(gu[s][:, :], xh[:, kk, :], whi[:, n, c], start=(kk == 0), stop=False)
                        pe.matmul(gu[s][:, :], xh[:, kk, :], wlo[:, n, c], start=False, stop=False)
                        mm = pe.matmul(gu[s][:, :], xl[:, kk, :], whi[:, n, c], start=False, stop=(kk == KT - 1))
                    mm.then_inc(w_used[n], 1)

            def down(b):
                pe.wait_ge(a_lo, b + 2)
                pe.wait_ge(y_copied, b + 1)
                for n in range(2):
                    pe.wait_ge(w_lo[4 + n], b + 2)
                    for h in range(2):
                        c = slice(512 * h, 512 * h + 512)
                        pe.matmul(yp[:, c], ah[:, n, :], whi[:, 4 + n, c], start=(n == 0), stop=False)
                        pe.matmul(yp[:, c], ah[:, n, :], wlo[:, 4 + n, c], start=False, stop=False)
                        mm = pe.matmul(yp[:, c], al[:, n, :], whi[:, 4 + n, c], start=False, stop=(n == 1))
                    mm.then_inc(w_used[4 + n], 1)

            def turn_a(b):
                pe.wait_ge(hid_done, b + 3)
                pe.wait_ge(a_lo, b + 1)
                for c in range(2):
                    mm = pe.transpose(ta[:, c, :], hid[:, c * P:(c + 1) * P], ident)
                mm.then_inc(a_turned, 1)

            def body(b, s, first, last):
                gate_up(b, s)
                if not last:
                    turn_x(b + 1, 1 - s)
                if not first:
                    down(b - 1)
                turn_a(b)

            for n in range(6):
                pe.sem_inc(w_used[n], 1)
            pe.sem_inc(x_turned, 2)
            turn_x(0, 0)
            blocks(pe, body)
            down(NBLK - 1)

        @block.scalar
        def _(act):
            act.preload_act_table(ACT.Silu)
            act.sem_inc(y_copied, 1)

            def x_split(b):
                act.wait_ge(x_turned, b + 3)
                act.wait_ge(w_used[3], b + 1)
                act.activation(xh[:, :, :], tx[:, :, :], ACT.Copy).then_inc(x_hi, 1)

            def gate(b, s):
                act.wait_ge(w_used[3], b + 2)
                act.activation(act_t[:, :], gu[s][:, 0:F], ACT.Silu).then_inc(silu, 1)

            def y_copy(b, s):
                act.wait_ge(w_used[5], b + 2)
                act.wait_ge(stored[s], 8 * (b - s) + 16)
                act.activation(ys[s][:, :], yp[:, :], ACT.Copy).then_inc(y_copied, 1)

            def a_split(b):
                act.wait_ge(a_turned, b + 1)
                act.wait_ge(w_used[5], b + 1)
                act.activation(ah[:, :, :], ta[:, :, :], ACT.Copy).then_inc(a_hi, 1)

            def body(b, s, first, last):
                if not last:
                    for n in (0, 1, 2):
                        split_hi(act, b + 1, n)
                gate(b, s)
                if not last:
                    x_split(b + 1)
                    split_hi(act, b + 1, 3)
                if not first:
                    y_copy(b - 1, 1 - s)
                a_split(b)
                split_hi(act, b, 4)

            for n in range(4):
                split_hi(act, 0, n)
            x_split(0)
            blocks(act, body)
            y_copy(NBLK - 1, 1)

        @block.vector
        def _(dve):
            for n in (0, 2, 4):
                dve.sem_inc(w_lo[n], 1)
            dve.sem_inc(x_lo, 1)
            dve.sem_inc(a_lo, 1)
            dve.sem_inc(hid_done, 2)

            def x_rest(b):
                dve.wait_ge(x_hi, b + 1)
                dve.tensor_tensor(xl[:, :, :], tx[:, :, :], xh[:, :, :].bitcast(F32), ALU.subtract).then_inc(x_lo, 1)

            def hidden(b, s):
                dve.wait_ge(silu, b + 1)
                dve.wait_ge(a_lo, b + 1)
                dve.tensor_tensor(hid[:, :], gu[s][:, F:2 * F], act_t[:, :], ALU.mult).then_inc(hid_done, 1)

            def a_rest(b):
                dve.wait_ge(a_hi, b + 1)
                dve.tensor_tensor(al[:, :, :], ta[:, :, :], ah[:, :, :].bitcast(F32), ALU.subtract).then_inc(a_lo, 1)

            def body(b, s, first, last):
                if not last:
                    split_lo(dve, b + 1, 0)
                    split_lo(dve, b + 1, 2)
                hidden(b, s)
                if not last:
                    x_rest(b + 1)
                a_rest(b)
                split_hi(dve, b, 5)
                split_lo(dve, b, 4)

            split_lo(dve, 0, 0)
            split_lo(dve, 0, 2)
            x_rest(0)
            blocks(dve, body)


def stage_combine(k, r, x1):
    nc, d = k.nc, k.d
    with ExitStack() as ctx:
        yg = [[k.at(f"cm_y{n}{s}", [P, D], F32, O_W + (2 * n + s) * 4096) for s in range(2)] for n in range(2)]
        y_in = [k.sems(ctx, f"cm_in{n}0", f"cm_in{n}1") for n in range(2)]
        added, part = k.sems(ctx, "cm_added", "cm_part")
        block = ctx.enter_context(nc.Block())

        @block.gpsimd
        def _(pool):
            for t in range(NT):
                if t >= 2:
                    pool.wait_ge(added, t - 1)
                for n in range(2):
                    pool.indirect_dma_start(out=yg[n][t % 2][:, :], out_offset=None, in_=d["y_slots"],
                                            in_offset=bass.IndirectOffsetOnAxis(ap=r.slot[:, n, t:t + 1].bitcast(U32), axis=0)
                                            ).then_inc(y_in[n][t % 2], 16)

        @block.vector
        def _(dve):
            for t in range(NT):
                for n in range(2):
                    dve.wait_ge(y_in[n][t % 2], 16 * (t // 2 + 1))
                    if n:
                        dve.wait_ge(part, t + 1)
                    dve.scalar_tensor_tensor(out=x1[:, t, :], in0=yg[n][t % 2][:, :], scalar=r.weight[:, n, t:t + 1],
                                             in1=x1[:, t, :], op0=ALU.mult, op1=ALU.add).then_inc(added if n else part, 1)



def stage_ple_project(k):
    nc, d = k.nc, k.d
    kt = PLE // P
    with ExitStack() as ctx:
        raw, whi, wlo = weight_ring(k, "pp")
        p_hi, p_lo = split_pair(k, "p", kt)
        pin = k.at("p_in", [P, NT, PLE], F32, O_R1 + 24 * 1024)
        out = [k.at(f"pp_out{s}", [P, 512], F32, O_ST + 2048 * s) for s in range(2)]
        tp = [ctx.enter_context(nc.psum_tensor(f"pp_tp{s}", [P, kt, P], F32)) for s in range(2)]
        pp = [ctx.enter_context(nc.psum_tensor(f"pp_p{s}", [P, 512], F32)) for s in range(2)]
        stored = k.sems(ctx, "pp_stored0", "pp_stored1")
        p_in, w_in, w_hi, w_lo, turned, hi_s, lo_s, done, copied = k.sems(
            ctx, *(f"pp_{n}" for n in ("p_in", "w_in", "w_hi", "w_lo", "turned", "hi", "lo", "done", "copied")))
        ident = k.const[:, C_ID:C_ID + P]
        block = ctx.enter_context(nc.Block())

        @block.sync
        def _(sp):
            sp.sem_inc(stored[0], 16)
            sp.sem_inc(stored[1], 16)
            sp.dma_start(pin[:, :, :], d["p"].rearrange("(t p) c -> p t c", p=P)).then_inc(p_in, 16)
            sp.dma_start(raw[:, 0:2, :], d["units"][U_PP:U_PP + 2].rearrange("u p n -> p u n")).then_inc(w_in, 16)
            for t in range(NT):
                for c in range(2):
                    sp.wait_ge(copied, 2 * t + c + 3)
                    sp.dma_start(d["pp"][t * P:(t + 1) * P, c * 512:(c + 1) * 512], out[c][:, :]).then_inc(stored[c], 16)
            sp.wait_ge(stored[0], 16 * (NT + 1))
            sp.wait_ge(stored[1], 16 * (NT + 1))

        @block.gpsimd
        def _(pool):
            pool.wait_ge(w_hi, 1)
            pool.tensor_tensor(wlo[:, 0:2, :], raw[:, 0:2, :], whi[:, 0:2, :].bitcast(F32), ALU.subtract).then_inc(w_lo, 1)

        @block.scalar
        def _(act):
            act.wait_ge(w_in, 16)
            act.activation(whi[:, 0:2, :], raw[:, 0:2, :], ACT.Copy).then_inc(w_hi, 1)
            for t in range(NT):
                act.wait_ge(turned, t + 1)
                act.activation(p_hi[:, :, t * P:(t + 1) * P], tp[t % 2][:, :, :], ACT.Copy).then_inc(hi_s, 1)

        @block.tensor
        def _(pe):
            pe.wait_ge(p_in, 16)
            for t in range(NT):
                if t >= 2:
                    pe.wait_ge(lo_s, t - 1)
                for c in range(kt):
                    mm = pe.transpose(tp[t % 2][:, c, :], pin[:, t, c * P:(c + 1) * P], ident)
                mm.then_inc(turned, 1)
            pe.wait_ge(w_lo, 1)
            for t in range(NT):
                pe.wait_ge(lo_s, t + 1)
                for c in range(2):
                    pe.wait_ge(copied, 2 * t + c + 1)
                    pe_token_tile(pe, pp[c][:, :], p_hi, p_lo, t, whi[:, c:c + 1, :], wlo[:, c:c + 1, :], kt).then_inc(done, 1)

        @block.vector
        def _(dve):
            dve.sem_inc(copied, 2)
            for t in range(NT):
                dve.wait_ge(hi_s, t + 1)
                tok = slice(t * P, (t + 1) * P)
                dve.tensor_tensor(p_lo[:, :, tok], tp[t % 2][:, :, :], p_hi[:, :, tok].bitcast(F32), ALU.subtract
                                  ).then_inc(lo_s, 1)
            for t in range(NT):
                for c in range(2):
                    dve.wait_ge(done, 2 * t + c + 1)
                    dve.wait_ge(stored[c], 16 * (t + 1))
                    dve.tensor_copy(out[c][:, :], pp[c][:, :]).then_inc(copied, 1)


def stage_ple(k, hi, lo, x2):
    nc, d = k.nc, k.d
    with ExitStack() as ctx:
        raw, whi, wlo = weight_ring(k, "pg")
        pin = [k.at(f"pg_p{s}", [P, 512], F32, O_ST + 2048 * s) for s in range(2)]
        sg = [k.at(f"pg_s{s}", [P, 512], F32, O_ST + 4096 + 2048 * s) for s in range(2)]
        zp = [ctx.enter_context(nc.psum_tensor(f"pg_z{b}", [P, 512], F32)) for b in range(5)]
        w_in = k.sems(ctx, *(f"pg_w_in{s}" for s in range(4)))
        p_in = k.sems(ctx, "pg_p_in0", "pg_p_in1")
        w_hi, w_lo, unit_done, tile_done, sig, part, added = k.sems(
            ctx, "pg_w_hi", "pg_w_lo", "pg_unit", "pg_tile", "pg_sig", "pg_part", "pg_added")
        block = ctx.enter_context(nc.Block())

        @block.sync
        def _(sp):
            for n in range(4):
                sp.dma_start(raw[:, n, :], d["units"][U_PG + n]).then_inc(w_in[n], 16)
            for n in range(4):
                sp.wait_ge(w_lo, n + 1)
                sp.dma_start(raw[:, n, :], d["units"][U_PG + 4 + n]).then_inc(w_in[n], 16)
            for c in range(2):
                with sp.Fori(0, NT // 2) as i:
                    for s in range(2):
                        t = 2 * i + s
                        sp.wait_ge(added, t + (NT * c + 1))
                        sp.dma_start(pin[s][:, :], d["pp"][ds(t * P, P), c * 512:(c + 1) * 512]).then_inc(p_in[s], 16)

        @block.scalar
        def _(act):
            act.preload_act_table(ACT.Sigmoid)
            act.sem_inc(sig, 5)
            for c in range(2):
                if c == 0:
                    for n in range(4):
                        act.wait_ge(w_in[n], 16)
                        act.activation(whi[:, n, :], raw[:, n, :], ACT.Copy).then_inc(w_hi, 1)
                for t in range(NT):
                    if c == 0 and t == NT - 1:
                        for n in range(4):
                            act.wait_ge(w_in[n], 32)
                            if n < 3:
                                act.wait_ge(unit_done, n + 1)
                            else:
                                act.wait_ge(tile_done, NT)
                            act.activation(whi[:, n, :], raw[:, n, :], ACT.Copy).then_inc(w_hi, 1)
                    act.wait_ge(tile_done, NT * c + t + 1)
                    act.wait_ge(added, NT * c + t + 1)
                    act.activation(sg[t % 2][:, :], zp[t % 5][:, :], ACT.Sigmoid).then_inc(sig, 1)

        @block.gpsimd
        def _(pool):
            for c in range(2):
                for n in range(4):
                    pool.wait_ge(w_hi, 4 * c + n + 1)
                    pool.tensor_tensor(wlo[:, n, :], raw[:, n, :], whi[:, n, :].bitcast(F32), ALU.subtract).then_inc(w_lo, 1)

        @block.tensor
        def _(pe):
            for c in range(2):
                pe.wait_ge(w_lo, 4 * c + 4)
                for t in range(NT):
                    pe.wait_ge(sig, NT * c + t + 1)
                    last = c == 0 and t == NT - 1
                    pe_token_tile(pe, zp[t % 5][:, :], hi, lo, t, whi, wlo, KT, unit_done if last else None
                                  ).then_inc(tile_done, 1)

        @block.vector
        def _(dve):
            dve.sem_inc(added, 2)
            for c in range(2):
                for t in range(NT):
                    n = NT * c + t
                    dve.wait_ge(p_in[t % 2], 16 * (5 * c + t // 2 + 1))
                    dve.wait_ge(sig, n + 6)
                    dve.tensor_tensor(sg[t % 2][:, :], sg[t % 2][:, :], pin[t % 2][:, :], ALU.mult).then_inc(part, 1)
                    dve.wait_ge(part, n + 1)
                    x = x2[:, t, c * 512:(c + 1) * 512]
                    dve.tensor_tensor(x, x, sg[t % 2][:, :], ALU.add).then_inc(added, 1)


def stage_final_norm(k, x3):
    nc, d = k.nc, k.d
    with ExitStack() as ctx:
        gb = k.at("fn_g", [P, D], F32, O_W)
        nh = k.at("fn_nh", [P, 1], F32, O_W + 4096)
        st = k.at("fn_st", [P, NT, 4], F32, O_W + 4128)
        junk = k.at("fn_j", [P, 2, D], F32, O_W + 8192)
        y = k.at("fn_y", [P, NT, D], F32, O_R1)
        g_in, half_set, squared, scaled, rstd, normed, stored = k.sems(
            ctx, *(f"fn_{n}" for n in ("g_in", "half_set", "squared", "scaled", "rstd", "normed", "stored")))
        block = ctx.enter_context(nc.Block())

        @block.sync
        def _(sp):
            sp.dma_start(gb[:, :], d["g_final"].partition_broadcast(P)).then_inc(g_in, 16)
            for t in range(NT):
                out = d["y_prompt"][0, t * P:(t + 1) * P, :] if t < QB else d["y_sample"][0, (t - QB) * P:(t - QB + 1) * P, :]
                sp.wait_ge(normed, t + 1)
                sp.dma_start(out, y[:, t, :]).then_inc(stored, 16)
            sp.wait_ge(stored, 16 * NT)

        @block.gpsimd
        def _(pool):
            pool.memset(nh[:, :], -0.5).then_inc(half_set, 1)
            pool.wait_ge(half_set, 1)
            for t in range(NT):
                pool.wait_ge(scaled, t + 1)
                pool.tensor_tensor(st[:, t, 2:3], st[:, t, 1:2], nh[:, :], ALU.pow).then_inc(rstd, 1)

        @block.scalar
        def _(act):
            for t in range(NT):
                if t >= 2:
                    act.wait_ge(squared, t - 1)
                act.activation(junk[:, t % 2, :], x3[:, t, :], ACT.Square, accum_out=st[:, t, 0:1]).then_inc(squared, 1)

        @block.vector
        def _(dve):
            dve.wait_ge(g_in, 16)

            def variance(t):
                dve.wait_ge(squared, t + 1)
                dve.tensor_scalar(st[:, t, 1:2], st[:, t, 0:1], 1.0 / D, EPS, ALU.mult, ALU.add).then_inc(scaled, 1)

            variance(0)
            for t in range(NT):
                if t + 1 < NT:
                    variance(t + 1)
                dve.wait_ge(rstd, t + 1)
                dve.scalar_tensor_tensor(out=y[:, t, :], in0=x3[:, t, :], scalar=st[:, t, 2:3], in1=gb[:, :], op0=ALU.mult,
                                         op1=ALU.mult).then_inc(normed, 1)

def build(nc, dram, upto=99):
    scratch = {
        "bc": ([2 * P, T], F32), "xtok": ([T, D + 256], F32), "rest": ([22 * P, T], F32),
        "ztok": ([T, D], F32), "mix_a": ([D, T], F32), "bias_line": ([N_HEADS, 512], F32),
        "h2": ([T, D], F32), "slots": ([NBLK * P, 1], I32), "y_slots": ([NBLK * P, D], F32),
        "pp": ([T, D], F32),
    }
    for name, (shape, dtype) in scratch.items():
        dram[name] = nc.dram_tensor(name, shape, dtype, kind="Internal").ap()
    k = Core(nc, dram)
    k.dt_raw = k.at("dt_raw", [P, NT, 32], F32, O_KEEP + 256)
    k.bias = k.at("bias", [P, 3, N_HEADS, BAND], F32, O_BIAS)
    stage_load_constants(k)
    hi, lo = split_pair(k, "h")
    stage_norm_transpose(k, "norm_in", dram["g_mix"], hi, lo, x_dram=dram["x"])
    stage_project_conv(k, hi, lo)
    stage_project_rest(k, hi, lo)
    stage_project_z(k, hi, lo)
    stage_bias_tables(k)
    att_hi, att_lo = split_pair(k, "att", 4)
    stage_attention(k, att_hi, att_lo)
    stage_gated(k, "ao", att_hi, att_lo, 4, U_AO, 6, add=False)
    k.clear_semaphores()
    q = SsdTiles(k)
    stage_ssd_decays(k, q)
    stage_ssd_states(k, q)
    y_hi, y_lo = split_pair(k, "y")
    stage_ssd_scan(k, q, y_hi, y_lo)
    mixed = k.at("mixed", [P, KT, T], F32, O_R2)
    stage_gated(k, "so", y_hi, y_lo, KT, U_SO, 14, add=True, out_sbuf=mixed)
    m_hi, m_lo = split_pair(k, "m")
    x1 = k.at("x1", [P, NT, D], F32, O_R2)
    stage_residual_out(k, mixed, m_hi, m_lo, x1)
    k.clear_semaphores()
    r = Routing(k)
    stage_norm_route(k, x1, r)
    stage_route(k, r)
    stage_experts(k, r)
    stage_combine(k, r, x1)
    stage_ple_project(k)
    g_hi, g_lo = split_pair(k, "g")
    stage_norm_transpose(k, "norm_ple", dram["g_ple"], g_hi, g_lo, x_sbuf=x1)
    stage_ple(k, g_hi, g_lo, x1)
    stage_final_norm(k, x1)


def _units(w_in, w_attn_out, w_ssd_out, w_out, w_ple_gate, w_ple_proj):
    def by_channel(w):
        kt, cols = w.shape[0] // P, w.shape[1]
        return w.reshape(kt, P, cols // P, P).transpose(2, 1, 0, 3).reshape(cols // P, P, kt * P)

    def by_token(w):
        kt, cols = w.shape[0] // P, w.shape[1]
        return w.reshape(kt // 2, 2, P, cols // 512, 512).transpose(3, 0, 2, 1, 4).reshape(-1, P, 1024)

    q, kk, v, z, xbc, dt, ga, gs = np.split(w_in, np.cumsum([512, 128, 128, 1024, 1280, 32, 1024]), axis=1)
    q = q.reshape(D, N_KV, GQ, HEAD).transpose(0, 2, 1, 3).reshape(D, N_HEADS * HEAD)
    ao = by_channel(w_attn_out).reshape(4, 2, P, 512).transpose(0, 2, 1, 3).reshape(4, P, 1024)
    units = [by_channel(xbc), by_channel(q), by_channel(kk), by_channel(v), by_channel(ga), by_channel(gs),
             by_token(z), ao, by_channel(w_ssd_out), by_token(w_out), by_token(w_ple_gate), by_token(w_ple_proj)]
    return np.ascontiguousarray(np.concatenate(units)), dt.reshape(KT, P, 32).transpose(1, 0, 2)


def kernel(**inputs):
    import concourse.bacc as _bacc
    from concourse.bass_utils import run_bass_kernel_spmd as _run

    a = {n: np.asarray(v) for n, v in inputs.items()}
    consts, ids, hot = host_constants()
    units, w_dt = _units(a["w_in"][0], a["w_attn_out"][0], a["w_ssd_out"][0], a["w_out"][0], a["w_ple_gate"][0],
                         a["w_ple_proj"][0])
    conv = np.concatenate([a["conv_w"][0], a["conv_b"]]).reshape(CONV + 1, 10, P).transpose(2, 1, 0)
    gu = a["w_gate_up"][0].reshape(N_EXP, 4, 2, P, 512).transpose(0, 1, 3, 2, 4).reshape(N_EXP, 4, P, 1024)
    down = a["w_down"][0].reshape(N_EXP, 2, P, D)
    arrays = {
        "x": np.concatenate([a["x_prompt"][0], a["x_sample"][0]]),
        "p": np.concatenate([a["p_prompt"][0, 0], a["p_sample"][0, 0]]),
        "units": units, "w_dt": w_dt, "conv": conv, "consts": consts, "ids": ids, "hot": hot,
        "experts": np.concatenate([gu, down], axis=1).reshape(N_EXP * 6 * P, 1024),
        "g_mix": a["g_mix"][0], "g_ffn": a["g_ffn"][0], "g_ple": a["g_ple"][0], "g_final": a["g_final"],
        "norm_g": a["ssd_norm_g"][0], "rel_bias": a["rel_bias"], "sink": a["attn_sink"][0],
        "dt_bias": np.concatenate([a["dt_bias_f"][0], a["dt_bias_b"][0]]),
        "a_log": np.concatenate([a["a_log_f"][0], a["a_log_b"][0]]), "d_skip": a["d_skip"][0],
        "router": np.concatenate([a["router_g"][0], a["router_e"][0]], axis=1).reshape(KT, P, 20).transpose(1, 0, 2),
        "router_b": np.concatenate([a["router_g_b"][0], a["router_e_b"][0]]),
    }
    arrays = {n: np.ascontiguousarray(v) for n, v in arrays.items()}
    nc = _bacc.Bacc("TRN2", target_bir_lowering=False, num_devices=1)
    dram = {n: nc.dram_tensor(n, v.shape, mybir.dt.from_np(v.dtype), kind="ExternalInput").ap() for n, v in arrays.items()}
    outs = [((1, s, D), "y_prompt" if n == 0 else "y_sample") for n, s in enumerate(SEQS)]
    for shape, name in outs:
        dram[name] = nc.dram_tensor(name, shape, F32, kind="ExternalOutput").ap()
    build(nc, dram)
    r = _run(nc, [arrays], core_ids=[0])
    return tuple(r.results[0][name] for _, name in outs)
```

```python
from contextlib import ExitStack

import numpy as np

import concourse.bass as bass
from concourse import mybir

F32 = mybir.dt.float32
F32R = mybir.dt.float32r
I32 = mybir.dt.int32
U32 = mybir.dt.uint32
ALU = mybir.AluOpType
ACT = mybir.ActivationFunctionType
AX = mybir.AxisListType
ds = bass.ds

P = 128
D = 1024
SEQS = (1024, 256)
T = sum(SEQS)
NT = T // P
KT = D // P
EPS = 1e-6
NEG = -1e30

HEAD = 64
N_HEADS = 8
N_KV = 2
GQ = N_HEADS // N_KV
BAND = 3 * P
N_BUCKETS = 32
QB = SEQS[0] // P

N_SSD = 16
SSD_HEAD = 64
N_STATE = 64
HPG = 8
XBC = D + 2 * 128
CONV = 5
PADDED = T + 8
CONV_LEN = T + 4
SEQ2_AT = SEQS[0] + 4

N_GROUPS = 4
PER_GROUP = 4
N_EXP = 16
F = 256
NB = (2 * T - N_EXP) // P + N_EXP
NBLK = NB + 1 - NB % 2
PLE = 256

U_XBC = 0
U_REST = U_XBC + 10
U_Z = U_REST + 22
U_AO = U_Z + 8
U_SO = U_AO + 4
U_OUT = U_SO + 8
U_PG = U_OUT + 8
U_PP = U_PG + 8
N_UNITS = U_PP + 2

C_ID, C_REV, C_INCU, C_INCL, C_GT, C_LT, C_ONE = (P * n for n in range(7))
C_TH = 7 * P
C_IOTA = C_TH + NT
C_E16 = C_IOTA + NBLK
C_RANK = C_E16 + N_EXP
N_CONST = C_RANK + 4


def host_constants():
    c = np.zeros((P, N_CONST), np.float32)
    r = np.arange(P)
    c[:, C_ID:C_ID + P] = np.eye(P)
    c[:, C_REV:C_REV + P] = np.eye(P)[::-1]
    c[:, C_INCU:C_INCU + P] = r[:, None] <= r[None]
    c[:, C_INCL:C_INCL + P] = r[:, None] >= r[None]
    c[:, C_GT:C_GT + P] = r[:, None] > r[None]
    c[:, C_LT:C_LT + P] = r[:, None] < r[None]
    c[:, C_ONE:C_ONE + P] = 1.0
    c[:, C_TH:C_TH + NT] = P * np.arange(NT)
    c[:, C_IOTA:C_IOTA + NBLK] = np.arange(NBLK)
    c[:, C_E16:C_E16 + N_EXP] = np.arange(N_EXP)
    c[:, C_RANK:C_RANK + 4] = 4 - np.arange(4)
    ids = (np.arange(NT)[None] * P + r[:, None]).astype(np.int32)
    rel = np.arange(512) - 255
    half, exact = N_BUCKETS // 2, N_BUCKETS // 4
    n = np.abs(rel)
    large = exact + (np.log(np.maximum(n, 1) / exact) / np.log(128 / exact) * (half - exact)).astype(np.int32)
    bucket = (rel > 0) * half + np.where(n < exact, n, np.minimum(large, half - 1))
    hot = np.zeros((N_BUCKETS + 1, 512), np.float32)
    hot[bucket, np.arange(512)] = n <= 128
    hot[N_BUCKETS] = np.where(n <= 128, 0.0, NEG)
    return c, ids, hot


class Core:

    def __init__(self, nc, dram):
        self.nc = nc
        self.d = dram
        self.used = []
        self.const = self.at("const", [P, N_CONST], F32, O_CONST)

    def at(self, name, shape, dtype, offset):
        return self.nc.alloc_sbuf_tensor_at(name, shape, dtype, offset=offset)

    def sems(self, ctx, *names):
        made = [self.nc.alloc_semaphore(n) for n in names]
        self.used.extend(made)
        return made

    def clear_semaphores(self):
        self.nc.all_engine_barrier()
        self.nc.clear_and_free_semaphores(self.used)
        self.nc.all_engine_barrier()
        self.used = []


O_CONST = 16512
O_KEEP = O_CONST + 3872
O_W = O_KEEP + 4256
O_R1 = O_W + 12 * 4096
O_R2 = O_R1 + 20 * 4096
O_ST = O_R2 + 11 * 4096


def weight_ring(k, tag, slots=4):
    raw = k.at(f"wraw_{tag}", [P, slots, 1024], F32, O_W)
    hi = k.at(f"whi_{tag}", [P, slots, 1024], F32R, O_W + 4 * 4096)
    lo = k.at(f"wlo_{tag}", [P, slots, 1024], F32R, O_W + 8 * 4096)
    return raw, hi, lo


def split_pair(k, tag, ktiles=KT, offset=O_R1):
    hi = k.at(f"hi_{tag}", [P, ktiles, T], F32R, offset)
    lo = k.at(f"lo_{tag}", [P, ktiles, T], F32R, offset + ktiles * T * 4)
    return hi, lo


class ResidentUnits:

    def __init__(self, k, tag, base, more, n_units=8):
        self.k, self.base, self.n = k, base, n_units
        at = [O_W + 4096 * j for j in range(12)] + list(more)
        self.raw = [k.at(f"{tag}_raw{n}", [P, 1024], F32, at[2 * n]) for n in range(n_units)]
        self.lo = [k.at(f"{tag}_lo{n}", [P, 1024], F32R, at[2 * n]) for n in range(n_units)]
        self.hi = [k.at(f"{tag}_hi{n}", [P, 1024], F32R, at[2 * n + 1]) for n in range(n_units)]
        self.w_in = k.sems(None, *(f"{tag}_w_in{n}" for n in range(n_units)))
        self.w_hi, self.w_lo_even, self.w_lo_odd = k.sems(None, f"{tag}_w_hi", f"{tag}_w_lo_even", f"{tag}_w_lo_odd")

    def load(self, sp):
        for n in range(self.n):
            sp.dma_start(self.raw[n][:, :], self.k.d["units"][self.base + n]).then_inc(self.w_in[n], 16)

    def split_hi(self, act, n):
        act.wait_ge(self.w_in[n], 16)
        act.activation(self.hi[n][:, :], self.raw[n][:, :], ACT.Copy).then_inc(self.w_hi, 1)

    def split_lo(self, eng, n):
        eng.wait_ge(self.w_hi, n + 1)
        eng.tensor_tensor(self.lo[n][:, :], self.raw[n][:, :], self.hi[n][:, :].bitcast(F32), ALU.subtract
                          ).then_inc(self.w_lo_odd if n % 2 else self.w_lo_even, 1)

    def wait_unit(self, pe, n):
        pe.wait_ge(self.w_lo_odd if n % 2 else self.w_lo_even, n // 2 + 1)



def stage_load_constants(k):
    nc, d = k.nc, k.d
    with ExitStack() as ctx:
        (loaded,) = k.sems(ctx, "const_loaded")
        block = ctx.enter_context(nc.Block())

        @block.sync
        def _(sp):
            sp.dma_start(k.const[:, :], d["consts"]).then_inc(loaded, 16)
            sp.wait_ge(loaded, 16)



def stage_norm_transpose(k, tag, gain, hi, lo, x_dram=None, x_sbuf=None):
    nc, d = k.nc, k.d
    with ExitStack() as ctx:
        o = O_ST
        gb = k.at(f"{tag}_g", [P, D], F32, O_W)
        neg_half = k.at(f"{tag}_nh", [P, 1], F32, O_KEEP + 3008)
        eps = k.at(f"{tag}_st", [P, 2, 4], F32, O_KEEP + 3072)
        xin = k.at(f"{tag}_x", [P, 2, D], F32, O_W + 4096)
        xn = k.at(f"{tag}_xn", [P, 2, D], F32, O_W + 3 * 4096)
        junk = k.at(f"{tag}_j", [P, 2, D], F32, O_W + 5 * 4096)
        tp = [ctx.enter_context(nc.psum_tensor(f"{tag}_tp{s}", [P, KT, P], F32)) for s in range(2)]
        g_in, half_set, squared, scaled, rstd_ready, normed, turned, hi_ready, lo_ready, x_used = k.sems(
            ctx, *(f"{tag}_{n}" for n in ("g_in", "half_set", "squared", "scaled", "rstd_ready", "normed", "turned",
                                          "hi_ready", "lo_ready", "x_used")))
        x_in = k.sems(ctx, f"{tag}_x_in0", f"{tag}_x_in1")
        ident = k.const[:, C_ID:C_ID + P]

        def x_of(s, t):
            return xin[:, s, :] if x_dram is not None else x_sbuf[:, t, :]

        block = ctx.enter_context(nc.Block())

        @block.sync
        def _(sp):
            sp.dma_start(gb[:, :], gain.partition_broadcast(P)).then_inc(g_in, 16)
            if x_dram is not None:
                with sp.Fori(0, NT // 2) as i:
                    for s in range(2):
                        sp.wait_ge(x_used, 2 * i + s + 1)
                        sp.dma_start(xin[:, s, :], x_dram[ds((2 * i + s) * P, P), :]).then_inc(x_in[s], 16)

        @block.gpsimd
        def _(pool):
            pool.memset(neg_half[:, :], -0.5).then_inc(half_set, 1)
            pool.wait_ge(half_set, 1)
            with pool.Fori(0, NT // 2) as i:
                for s in range(2):
                    pool.wait_ge(scaled, 2 * i + s + 1)
                    pool.tensor_tensor(eps[:, s, 2:3], eps[:, s, 1:2], neg_half[:, :], ALU.pow).then_inc(rstd_ready, 1)

        @block.scalar
        def _(act):
            act.preload_act_table(ACT.Square)

            def square(t, s, n):
                if x_dram is not None:
                    act.wait_ge(x_in[s], 16 * n)
                act.wait_ge(x_used, t + 1)
                act.activation(junk[:, s, :], x_of(s, t), ACT.Square, accum_out=eps[:, s, 0:1]).then_inc(squared, 1)

            def split(t, s):
                act.wait_ge(turned, t + 1)
                act.activation(hi[:, :, ds(t * P, P)], tp[s][:, :, :], ACT.Copy).then_inc(hi_ready, 1)

            square(0, 0, 1)
            with act.Fori(0, NT // 2 - 1) as i:
                square(2 * i + 1, 1, i + 1)
                split(2 * i, 0)
                square(2 * i + 2, 0, i + 2)
                split(2 * i + 1, 1)
            square(NT - 1, 1, NT // 2)
            split(NT - 2, 0)
            split(NT - 1, 1)

        @block.vector
        def _(dve):
            dve.sem_inc(x_used, 2)
            dve.sem_inc(lo_ready, 2)
            dve.wait_ge(g_in, 16)

            def norm(t, s):
                dve.wait_ge(squared, t + 1)
                dve.tensor_scalar(eps[:, s, 1:2], eps[:, s, 0:1], 1.0 / D, EPS, ALU.mult, ALU.add).then_inc(scaled, 1)
                dve.wait_ge(rstd_ready, t + 1)
                dve.scalar_tensor_tensor(out=xn[:, s, :], in0=x_of(s, t), scalar=eps[:, s, 2:3],
                                         in1=gb[:, :], op0=ALU.mult, op1=ALU.mult).then_inc(normed, 1)
                dve.wait_ge(normed, t + 1)
                dve.sem_inc(x_used, 1)

            def rest(t, s):
                dve.wait_ge(hi_ready, t + 1)
                dve.tensor_tensor(lo[:, :, ds(t * P, P)], tp[s][:, :, :],
                                  hi[:, :, ds(t * P, P)].bitcast(F32), ALU.subtract).then_inc(lo_ready, 1)

            norm(0, 0)
            with dve.Fori(0, NT // 2 - 1) as i:
                norm(2 * i + 1, 1)
                rest(2 * i, 0)
                norm(2 * i + 2, 0)
                rest(2 * i + 1, 1)
            norm(NT - 1, 1)
            rest(NT - 2, 0)
            rest(NT - 1, 1)

        @block.tensor
        def _(pe):
            with pe.Fori(0, NT // 2) as i:
                for s in range(2):
                    pe.wait_ge(normed, 2 * i + s + 1)
                    pe.wait_ge(lo_ready, 2 * i + s + 1)
                    for c in range(KT):
                        mm = pe.transpose(tp[s][:, c, :], xn[:, s, c * P:(c + 1) * P], ident)
                    mm.then_inc(turned, 1)



def pe_channel_tile(pe, out, whi, wlo, hi, lo, ktiles):
    cols = [(0, 512), (512, 512), (1024, 256)]
    for kk in range(ktiles):
        for w, h in ((whi, hi), (whi, lo), (wlo, hi)):
            for n, (c, size) in enumerate(cols):
                mm = pe.matmul(out[:, n, 0:size], w[:, kk, :], h[:, kk, c:c + size],
                               start=(kk == 0 and w is whi and h is hi), stop=(kk == ktiles - 1 and w is wlo))
    return mm


def stage_project_conv(k, hi, lo):
    nc, d = k.nc, k.d
    with ExitStack() as ctx:
        raw, whi, wlo = weight_ring(k, "xbc")
        xpad = k.at("xpad", [P, 2, PADDED], F32, O_R2)
        cv = k.at("conv_acc", [P, 2, CONV_LEN], F32, O_R2 + 2 * PADDED * 4)
        xc = k.at("conv_out", [P, 2, T], F32, O_R2 + 4 * PADDED * 4)
        xt = k.at("conv_tok", [P, 2, NT, P], F32, O_R2 + 6 * PADDED * 4)
        cw = k.at("conv_w", [P, 10, CONV + 1], F32, O_KEEP)
        gp = [ctx.enter_context(nc.psum_tensor(f"xbc_p{s}", [P, 3, 512], F32)) for s in range(2)]
        tb = [ctx.enter_context(nc.psum_tensor(f"xbc_t{s}", [P, 4, P], F32)) for s in range(2)]
        w_in = k.sems(ctx, "xbc_w_in0", "xbc_w_in1")
        w_hi, w_lo, mm_done, padded, conv_step, conv_read, silu_done, turned, tok_copied = k.sems(
            ctx, "xbc_w_hi", "xbc_w_lo", "xbc_mm", "xbc_padded", "xbc_conv_step", "xbc_conv_read", "xbc_silu",
            "xbc_turned", "xbc_tok")
        cw_in, pads = k.sems(ctx, "cw_in", "xbc_pads")
        stored = k.sems(ctx, "xbc_stored0", "xbc_stored1")
        ch_stored, = k.sems(ctx, "xbc_ch_stored")
        ident = k.const[:, C_ID:C_ID + P]
        GROUPS = [(0, 4), (4, 4), (8, 2)]
        block = ctx.enter_context(nc.Block())

        @block.sync
        def _(sp):
            sp.dma_start(cw[:, :, :], d["conv"]).then_inc(cw_in, 16)
            sp.sem_inc(stored[0], 16)
            sp.sem_inc(stored[1], 16)
            xtok = d["xtok"].rearrange("(t p) c -> p t c", p=P)

            def load(c, s):
                sp.wait_ge(w_lo, c + 1)
                sp.dma_start(raw[:, s, :], d["units"][ds(U_XBC + c, 1), :, :].rearrange("u p n -> (u p) n")
                             ).then_inc(w_in[s], 16)

            def store(c, s):
                sp.wait_ge(tok_copied, 3 * c + 5)
                sp.dma_start(xtok[:, :, ds(c * P, P)], xt[:, s, :, :]).then_inc(stored[s], 16)

            for c in range(4):
                load(c, c % 2)
            with sp.Fori(0, 3) as i:
                for s in range(2):
                    load(2 * i + s + 4, s)
                    store(2 * i + s, s)
            for c in range(6, 10):
                store(c, c % 2)
            sp.wait_ge(stored[0], 96)
            sp.wait_ge(stored[1], 96)

        @block.scalar
        def _(act):
            act.preload_act_table(ACT.Silu)

            def split(c, s, n):
                act.wait_ge(w_in[s], 16 * n)
                act.wait_ge(mm_done, c + 1)
                act.activation(whi[:, s, :], raw[:, s, :], ACT.Copy).then_inc(w_hi, 1)

            def pad(c, s):
                act.wait_ge(mm_done, c + 3)
                act.wait_ge(conv_read, c + 1)
                act.activation(xpad[:, s, 2:2 + SEQS[0]].rearrange("p (a n) -> p a n", a=2), gp[s][:, 0:2, :], ACT.Copy)
                act.activation(xpad[:, s, SEQ2_AT + 2:SEQ2_AT + 2 + SEQS[1]], gp[s][:, 2, 0:SEQS[1]],
                               ACT.Copy).then_inc(padded, 1)

            def silu(c, s):
                act.wait_ge(conv_read, c + 3)
                act.wait_ge(turned, 3 * c + 1)
                act.activation(xc[:, s, 0:SEQS[0]], cv[:, s, 0:SEQS[0]], ACT.Silu)
                act.activation(xc[:, s, SEQS[0]:T], cv[:, s, SEQ2_AT:SEQ2_AT + SEQS[1]], ACT.Silu).then_inc(silu_done, 1)

            split(0, 0, 1)
            split(1, 1, 1)
            act.wait_ge(pads, 1)
            with act.Fori(0, 4) as i:
                for s in range(2):
                    pad(2 * i + s, s)
                    split(2 * i + s + 2, s, i + 2)
                    silu(2 * i + s, s)
            for s in range(2):
                pad(8 + s, s)
                silu(8 + s, s)
            act.wait_ge(silu_done, 12)
            act.dma_start(d["bc"].rearrange("(s p) t -> p s t", p=P), xc[:, :, :]).then_inc(ch_stored, 16)
            act.wait_ge(ch_stored, 16)

        @block.gpsimd
        def _(pool):
            pool.memset(xpad[:, :, :], 0.0).then_inc(pads, 1)
            pool.sem_inc(w_lo, 2)
            with pool.Fori(0, 5) as i:
                for s in range(2):
                    pool.wait_ge(w_hi, 2 * i + s + 1)
                    pool.tensor_tensor(wlo[:, s, :], raw[:, s, :], whi[:, s, :].bitcast(F32), ALU.subtract).then_inc(w_lo, 1)

        @block.tensor
        def _(pe):
            def product(c, s):
                pe.wait_ge(w_lo, c + 3)
                pe.wait_ge(padded, c + 1)
                w = whi[:, s, :].rearrange("p (k c) -> p k c", k=KT)
                wl = wlo[:, s, :].rearrange("p (k c) -> p k c", k=KT)
                pe_channel_tile(pe, gp[s], w, wl, hi, lo, KT).then_inc(mm_done, 1)

            def turn(c, s):
                pe.wait_ge(silu_done, c + 3)
                for n, (a, m) in enumerate(GROUPS):
                    pe.wait_ge(tok_copied, 3 * c + n + 1)
                    for j in range(m):
                        mm = pe.transpose(tb[(s + n) % 2][:, j, :], xc[:, s, (a + j) * P:(a + j + 1) * P], ident)
                    mm.then_inc(turned, 1)

            pe.sem_inc(mm_done, 2)
            pe.sem_inc(turned, 6)
            product(0, 0)
            with pe.Fori(0, 4) as i:
                product(2 * i + 1, 1)
                turn(2 * i, 0)
                product(2 * i + 2, 0)
                turn(2 * i + 1, 1)
            product(9, 1)
            turn(8, 0)
            turn(9, 1)

        @block.vector
        def _(dve):
            dve.sem_inc(padded, 2)
            dve.sem_inc(conv_read, 2)
            dve.sem_inc(silu_done, 2)
            dve.sem_inc(tok_copied, 2)
            dve.wait_ge(cw_in, 16)

            def conv(c, s):
                dve.wait_ge(padded, c + 3)
                dve.wait_ge(silu_done, c + 1)
                dve.tensor_scalar(cv[:, s, :], xpad[:, s, 0:CONV_LEN], cw[:, ds(c, 1), 0:1], cw[:, ds(c, 1), CONV:CONV + 1],
                                  ALU.mult, ALU.add).then_inc(conv_step, 1)
                for w in range(1, CONV):
                    dve.wait_ge(conv_step, 4 * c + w)
                    mm = dve.scalar_tensor_tensor(out=cv[:, s, :], in0=xpad[:, s, w:w + CONV_LEN],
                                                  scalar=cw[:, ds(c, 1), w:w + 1], in1=cv[:, s, :], op0=ALU.mult, op1=ALU.add)
                    mm.then_inc(conv_step if w < CONV - 1 else conv_read, 1)

            def tokens(c, s, i):
                dve.wait_ge(stored[s], 16 * (i + 1))
                for n, (a, m) in enumerate(GROUPS):
                    dve.wait_ge(turned, 3 * c + n + 7)
                    dve.tensor_copy(xt[:, s, a:a + m, :], tb[(s + n) % 2][:, 0:m, :]).then_inc(tok_copied, 1)

            conv(0, 0)
            with dve.Fori(0, 4) as i:
                tokens(2 * i, 0, i)
                conv(2 * i + 1, 1)
                tokens(2 * i + 1, 1, i)
                conv(2 * i + 2, 0)
            tokens(8, 0, 4)
            conv(9, 1)
            tokens(9, 1, 4)


def stage_project_rest(k, hi, lo):
    nc, d = k.nc, k.d
    n_tiles = 22
    with ExitStack() as ctx:
        raw, whi, wlo = weight_ring(k, "rest")
        got = k.at("rest_out", [P, 2, T], F32, O_R2)
        gp = [ctx.enter_context(nc.psum_tensor(f"rest_p{s}", [P, 3, 512], F32)) for s in range(2)]
        w_in = k.sems(ctx, "rest_w_in0", "rest_w_in1")
        stored = k.sems(ctx, "rest_stored0", "rest_stored1")
        w_hi, w_lo, mm_done, copied = k.sems(ctx, "rest_w_hi", "rest_w_lo", "rest_mm", "rest_copied")
        block = ctx.enter_context(nc.Block())

        @block.sync
        def _(sp):
            sp.sem_inc(stored[0], 16)
            sp.sem_inc(stored[1], 16)

            def load(c, s):
                sp.wait_ge(w_lo, c + 1)
                sp.dma_start(raw[:, s, :], d["units"][ds(U_REST + c, 1), :, :].rearrange("u p n -> (u p) n")
                             ).then_inc(w_in[s], 16)

            def store(c, s):
                sp.wait_ge(copied, c + 3)
                sp.dma_start(d["rest"][ds(c * P, P), :], got[:, s, :]).then_inc(stored[s], 16)

            for c in range(4):
                load(c, c % 2)
            with sp.Fori(0, (n_tiles - 4) // 2) as i:
                for s in range(2):
                    load(2 * i + s + 4, s)
                    store(2 * i + s, s)
            for c in range(n_tiles - 4, n_tiles):
                store(c, c % 2)
            for s in range(2):
                sp.wait_ge(stored[s], 16 * (n_tiles // 2 + 1))

        @block.scalar
        def _(act):
            act.sem_inc(copied, 2)

            def split(c, s, n):
                act.wait_ge(w_in[s], 16 * n)
                act.wait_ge(mm_done, c + 1)
                act.activation(whi[:, s, :], raw[:, s, :], ACT.Copy).then_inc(w_hi, 1)

            def copy(c, s, n):
                act.wait_ge(mm_done, c + 3)
                act.wait_ge(stored[s], 16 * n)
                act.activation(got[:, s, 0:1024].rearrange("p (a n) -> p a n", a=2), gp[s][:, 0:2, :], ACT.Copy)
                act.activation(got[:, s, 1024:T], gp[s][:, 2, 0:256], ACT.Copy).then_inc(copied, 1)

            split(0, 0, 1)
            split(1, 1, 1)
            with act.Fori(0, n_tiles // 2 - 1) as i:
                for s in range(2):
                    copy(2 * i + s, s, i + 1)
                    split(2 * i + s + 2, s, i + 2)
            for s in range(2):
                copy(n_tiles - 2 + s, s, n_tiles // 2)

        @block.gpsimd
        def _(pool):
            pool.sem_inc(w_lo, 2)
            with pool.Fori(0, n_tiles // 2) as i:
                for s in range(2):
                    pool.wait_ge(w_hi, 2 * i + s + 1)
                    pool.tensor_tensor(wlo[:, s, :], raw[:, s, :], whi[:, s, :].bitcast(F32), ALU.subtract).then_inc(w_lo, 1)

        @block.tensor
        def _(pe):
            pe.sem_inc(mm_done, 2)
            with pe.Fori(0, n_tiles // 2) as i:
                for s in range(2):
                    pe.wait_ge(w_lo, 2 * i + s + 3)
                    pe.wait_ge(copied, 2 * i + s + 1)
                    pe_channel_tile(pe, gp[s], whi[:, s, :].rearrange("p (k c) -> p k c", k=KT),
                                    wlo[:, s, :].rearrange("p (k c) -> p k c", k=KT), hi, lo, KT).then_inc(mm_done, 1)



def pe_token_tile(pe, out, hi, lo, t, w, c, ktiles=KT):
    tok = slice(t * P, (t + 1) * P)
    for kk in range(ktiles):
        n, half = c * (ktiles // 2) + kk // 2, slice((kk % 2) * 512, (kk % 2) * 512 + 512)
        if t == 0 and kk % 2 == 0:
            w.wait_unit(pe, n)
        pe.matmul(out, hi[:, kk, tok], w.hi[n][:, half], start=(kk == 0), stop=False)
        pe.matmul(out, hi[:, kk, tok], w.lo[n][:, half], start=False, stop=False)
        mm = pe.matmul(out, lo[:, kk, tok], w.hi[n][:, half], start=False, stop=(kk == ktiles - 1))
    return mm


def stage_project_z(k, hi, lo):
    nc, d = k.nc, k.d
    with ExitStack() as ctx:
        w = ResidentUnits(k, "z", U_Z, [O_R2 + 4096 * j for j in range(4)])
        zt = k.at("z_out", [P, 2, D], F32, O_R2 + 4 * 4096)
        wd_raw = k.at("wd_raw", [P, KT, 32], F32, O_R2 + 6 * 4096)
        wd_hi = k.at("wd_hi", [P, KT, 32], F32R, O_R2 + 6 * 4096 + 1024)
        wd_lo = k.at("wd_lo", [P, KT, 32], F32R, O_R2 + 6 * 4096 + 2048)
        dt_ch = k.at("dt_ch", [32, T], F32, O_R2 + 7 * 4096)
        dc = ctx.enter_context(nc.psum_tensor("dt_c", [32, 3, 512], F32))
        dp = ctx.enter_context(nc.psum_tensor("dt_p", [P, NT, 32], F32))
        zp = [ctx.enter_context(nc.psum_tensor(f"z_p{b}", [P, D], F32)) for b in range(2)]
        stored = k.sems(ctx, "z_stored0", "z_stored1")
        tile_done, silued, wd_in, wd_h, wd_l, dt_done, dt_copied, dt_turned = k.sems(
            ctx, "z_tile", "z_silu", "wd_in", "wd_h", "wd_l", "dt_done", "dt_copied", "dt_turned")
        ident = k.const[0:32, C_ID:C_ID + 32]
        block = ctx.enter_context(nc.Block())

        @block.sync
        def _(sp):
            sp.dma_start(wd_raw[:, :, :], d["w_dt"]).then_inc(wd_in, 16)
            w.load(sp)
            for t in range(NT):
                sp.wait_ge(silued, t + 1)
                sp.dma_start(d["ztok"][t * P:(t + 1) * P, :], zt[:, t % 2, :]).then_inc(stored[t % 2], 16)
            sp.wait_ge(stored[0], 16 * (NT // 2))
            sp.wait_ge(stored[1], 16 * (NT // 2))

        @block.scalar
        def _(act):
            act.preload_act_table(ACT.Silu)
            act.wait_ge(wd_in, 16)
            act.activation(wd_hi[:, :, :], wd_raw[:, :, :], ACT.Copy).then_inc(wd_h, 1)
            for n in range(8):
                w.split_hi(act, n)
            act.wait_ge(dt_done, 1)
            act.activation(dt_ch[:, 0:SEQS[0]].rearrange("p (a n) -> p a n", a=2), dc[:, 0:2, :], ACT.Copy)
            act.activation(dt_ch[:, SEQS[0]:T], dc[:, 2, 0:SEQS[1]], ACT.Copy).then_inc(dt_copied, 1)
            for t in range(NT):
                act.wait_ge(tile_done, t + 1)
                if t >= 2:
                    act.wait_ge(stored[t % 2], 16 * (t // 2))
                act.activation(zt[:, t % 2, :], zp[t % 2][:, :], ACT.Silu).then_inc(silued, 1)

        @block.gpsimd
        def _(pool):
            for n in range(1, 8, 2):
                w.split_lo(pool, n)

        @block.tensor
        def _(pe):
            pe.wait_ge(wd_l, 1)
            pe_channel_tile(pe, dc, wd_hi, wd_lo, hi, lo, KT).then_inc(dt_done, 1)
            for t in range(NT):
                if t >= 2:
                    pe.wait_ge(silued, t - 1)
                for c in range(2):
                    mm = pe_token_tile(pe, zp[t % 2][:, c * 512:(c + 1) * 512], hi, lo, t, w, c)
                mm.then_inc(tile_done, 1)
                if t == 0:
                    pe.wait_ge(dt_copied, 1)
                    for n in range(NT):
                        mm = pe.transpose(dp[:, n, :], dt_ch[:, n * P:(n + 1) * P], ident)
                    mm.then_inc(dt_turned, 1)

        @block.vector
        def _(dve):
            dve.wait_ge(wd_h, 1)
            dve.tensor_tensor(wd_lo[:, :, :], wd_raw[:, :, :], wd_hi[:, :, :].bitcast(F32), ALU.subtract).then_inc(wd_l, 1)
            for n in range(0, 8, 2):
                w.split_lo(dve, n)
            dve.wait_ge(dt_turned, 1)
            dve.tensor_copy(k.dt_raw[:, :, :], dp[:, :, :])



O_BIAS = O_W


def stage_bias_tables(k):
    nc, d = k.nc, k.d
    with ExitStack() as ctx:
        hot = k.at("hot", [N_BUCKETS + 1, 512], F32, O_R2)
        rel = k.at("rel", [N_BUCKETS + 1, N_HEADS], F32, O_R2 + 2048)
        line = k.at("line", [N_HEADS, 512], F32, O_R2 + 4096)
        slid = k.at("slid", [P, N_HEADS, BAND], F32, O_R2 + 8192)
        lp = ctx.enter_context(nc.psum_tensor("line_p", [P, 512], F32))
        bp = [ctx.enter_context(nc.psum_tensor(f"bias_p{s}", [P, 512], F32)) for s in range(2)]
        ones_set, tab_in, line_done, line_copied, line_stored, slid_in, flipped, copied, firsts = k.sems(
            ctx, "ones_set", "tab_in", "line_done", "line_copied", "line_stored", "slid_in", "flipped", "bias_copied",
            "bias_first")
        block = ctx.enter_context(nc.Block())

        @block.sync
        def _(sp):
            sp.dma_start(hot[:, :], d["hot"]).then_inc(tab_in, 16)
            sp.wait_ge(ones_set, 1)
            sp.dma_start(rel[0:N_BUCKETS, :], d["rel_bias"]).then_inc(tab_in, 16)
            sp.wait_ge(line_copied, 1)
            sp.dma_start(d["bias_line"], line[:, :]).then_inc(line_stored, 16)
            sp.wait_ge(line_stored, 16)
            src = bass.AP(tensor=d["bias_line"].tensor, offset=0, ap=[[1, P], [512, N_HEADS], [1, BAND]])
            sp.dma_start(slid[:, :, :], src).then_inc(slid_in, 16)

        @block.tensor
        def _(pe):
            pe.wait_ge(tab_in, 32)
            pe.matmul(lp[0:N_HEADS, :], rel[:, :], hot[:, :], start=True, stop=True).then_inc(line_done, 1)
            pe.wait_ge(slid_in, 16)
            for h in range(N_HEADS):
                if h >= 2:
                    pe.wait_ge(copied, h - 1)
                pe.matmul(bp[h % 2][:, 0:BAND], k.const[:, C_REV:C_REV + P], slid[:, h, :], start=True,
                          stop=True).then_inc(flipped, 1)

        @block.vector
        def _(dve):
            dve.memset(rel[:, :], 1.0).then_inc(ones_set, 1)
            dve.wait_ge(line_done, 1)
            dve.tensor_copy(line[:, :], lp[0:N_HEADS, :]).then_inc(line_copied, 1)
            for h in range(N_HEADS):
                dve.wait_ge(flipped, h + 1)
                dve.tensor_copy(k.bias[:, 0, h, :], bp[h % 2][:, 0:BAND]).then_inc(copied, 1)
            dve.wait_ge(copied, N_HEADS)
            for v in (1, 2):
                dve.tensor_copy(k.bias[:, v, :, :], k.bias[:, 0, :, :]).then_inc(firsts, 1)
            dve.wait_ge(firsts, 2)
            dve.memset(k.bias[:, 1, :, 0:P], NEG)
            dve.memset(k.bias[:, 2, :, 2 * P:], NEG)


def stage_attention(k, att_hi, att_lo):
    nc, d = k.nc, k.d
    with ExitStack() as ctx:
        o = O_R2
        qs = k.at("q_blk", [P, 2, 4, P], F32, o)
        ks = k.at("k_win", [P, 2, BAND], F32, o + 4096)
        vt = k.at("v_ch", [P, T], F32, o + 7168)
        vn = k.at("v_tok", [P, NT + 4, P], F32, o + 12288)
        sc = k.at("scores", [P, 2, GQ, BAND], F32, o + 19456)
        pt = k.at("probs_t", [P, 2, BAND], F32, o + 31744)
        att = k.at("att_tok", [P, 2, N_HEADS * HEAD], F32, o + 34816)
        sink = k.at("sink", [P, N_HEADS], F32, o + 38912)
        nsink = k.at("nsink", [P, N_HEADS], F32, o + 38944)
        st = k.at("att_stat", [P, 2, 6, GQ], F32, o + 38976)
        rden = k.at("att_rden", [P, 2, N_HEADS], F32, o + 39168)
        sp_ = ctx.enter_context(nc.psum_tensor("score_p", [P, GQ, 512], F32))
        tp = [ctx.enter_context(nc.psum_tensor(f"att_tp{s}", [P, 512], F32)) for s in range(2)]
        pv = ctx.enter_context(nc.psum_tensor("pv_p", [P, N_HEADS * HEAD], F32))
        ap_ = ctx.enter_context(nc.psum_tensor("att_t", [P, 4, P], F32))
        qk_in = k.sems(ctx, "qk_in0", "qk_in1")
        names = ("v_in", "v_zero", "v_turned", "v_copied", "sink_in", "sink_neg", "score_done", "scored", "step",
                 "probs", "turned", "pt_ready", "pv_done", "att_done", "att_turned", "att_hi_s",
                 "att_lo_s", "ready", "pv_step")
        (v_in, v_zero, v_turned, v_copied, sink_in, sink_neg, score_done, scored, step, probs,
         turned, pt_ready, pv_done, att_done, att_turned, att_hi_s, att_lo_s, ready, pv_step) = k.sems(
             ctx, *(f"att_{n}" for n in names))
        ident = k.const[:, C_ID:C_ID + P]
        MID = (0, 0)
        block = ctx.enter_context(nc.Block())

        def pairs(eng, body):
            body(0, (1, 0), 0, 0)
            with eng.Fori(1, QB // 2 - 1) as i:
                body(2 * i, MID, 0, 0)
            body(QB - 2, (0, 2), 0, 1)
            body(QB, (1, 2), 1, None)

        def first(n):
            return isinstance(n, int) and n == 0

        @block.sync
        def _(sp):
            sp.dma_start(vt[:, :], d["rest"][5 * P:6 * P, :]).then_inc(v_in, 16)
            sp.dma_start(sink[:, :], d["sink"].partition_broadcast(P)).then_inc(sink_in, 16)
            sp.wait_ge(v_zero, 2)

            def body(n0, tables, seq, after):
                for s in range(2):
                    n = n0 + s
                    sp.wait_ge(score_done, 2 * n + 2)
                    sp.dma_start(qs[:, s, :, :], d["rest"][0:4 * P, ds(n * P, P)].rearrange("(m p) t -> p m t", p=P)
                                 ).then_inc(qk_in[s], 16)
                    a = 1 if tables[s] == 1 else 0
                    b = 2 if tables[s] == 2 else 3
                    sp.dma_start(ks[:, s, a * P:b * P], d["rest"][4 * P:5 * P, ds((n - 1 + a) * P, (b - a) * P)]
                                 ).then_inc(qk_in[s], 16)

            pairs(sp, body)

        @block.gpsimd
        def _(pool):
            pool.memset(vn[:, :, :], 0.0).then_inc(v_zero, 1)
            pool.memset(ks[:, :, :], 0.0).then_inc(v_zero, 1)

        @block.tensor
        def _(pe):
            pe.sem_inc(score_done, 4)
            pe.sem_inc(turned, 8)
            pe.sem_inc(pv_done, 2)
            pe.wait_ge(v_in, 16)
            for t in range(NT):
                if t >= 2:
                    pe.wait_ge(v_copied, t - 1)
                pe.transpose(tp[t % 2][:, 0:P], vt[:, t * P:(t + 1) * P], ident).then_inc(v_turned, 1)
            pe.wait_ge(v_copied, NT)

            def score(n, s, g):
                u = 2 * n + g
                if g == 0:
                    pe.wait_ge(qk_in[s], 16 * (n - s) + 32)
                pe.wait_ge(scored, u + 1)
                for m in range(GQ):
                    mm = pe.matmul(sp_[:, m, 0:BAND], qs[g * HEAD:(g + 1) * HEAD, s, m, :],
                                   ks[g * HEAD:(g + 1) * HEAD, s, :], start=True, stop=True)
                mm.then_inc(score_done, 1)

            def turn(n, s, g, m):
                if m == 0:
                    pe.wait_ge(probs, 2 * n + g + 1)
                pe.wait_ge(pt_ready, 4 * (2 * n + g) + m + 1)
                for b in range(3):
                    mm = pe.transpose(tp[m % 2][:, b * P:(b + 1) * P], sc[:, g, m, b * P:(b + 1) * P], ident)
                mm.then_inc(turned, 1)

            def weigh(n, s, g, m, seq):
                pe.wait_ge(pt_ready, 4 * (2 * n + g) + m + 3)
                if g == 0 and m == 0:
                    pe.wait_ge(att_done, n + 1)
                hd = (4 * g + m) * HEAD
                for b in range(3):
                    mm = pe.matmul(pv[:, hd:hd + HEAD], pt[:, m % 2, b * P:(b + 1) * P],
                                   vn[:, ds(n + seq + b, 1), g * HEAD:(g + 1) * HEAD].rearrange("p a n -> p (a n)"),
                                   start=(b == 0), stop=(b == 2))
                mm.then_inc(pv_done, 1)

            def values(n, s, g, seq):
                turn(n, s, g, 0)
                for m in range(1, GQ):
                    turn(n, s, g, m)
                    weigh(n, s, g, m - 1, seq)
                weigh(n, s, g, GQ - 1, seq)

            def out(n, s):
                pe.wait_ge(att_done, n + 2)
                pe.wait_ge(att_lo_s, n + 1)
                for m in range(4):
                    mm = pe.transpose(ap_[:, m, :], att[:, s, m * P:(m + 1) * P], ident)
                mm.then_inc(att_turned, 1)

            def body(n, tables, seq, after):
                score(n, 0, 1)
                values(n, 0, 0, seq)
                if not first(n):
                    out(n - 1, 1)
                score(n + 1, 1, 0)
                values(n, 0, 1, seq)
                score(n + 1, 1, 1)
                values(n + 1, 1, 0, seq)
                out(n, 0)
                if after is not None:
                    score(n + 2, 0, 0)
                values(n + 1, 1, 1, seq)

            score(0, 0, 0)
            pairs(pe, body)
            out(NT - 1, 1)

        @block.scalar
        def _(act):
            act.preload_act_table(ACT.Exp)
            act.sem_inc(pt_ready, 2)

            def exps(n, g):
                u = 2 * n + g
                act.wait_ge(ready, u + 1)
                for m in range(GQ):
                    act.activation(sc[:, g, m, :], sc[:, g, m, :], ACT.Exp, bias=st[:, g, 1, m:m + 1],
                                   accum_out=st[:, g, 4, m:m + 1])
                act.activation(st[:, g, 3, :], st[:, g, 2, :], ACT.Exp).then_inc(probs, 1)

            def copies(n, g):
                for m in range(GQ):
                    act.wait_ge(turned, 4 * (2 * n + g) + m + 9)
                    act.wait_ge(pv_done, 4 * (2 * n + g) + m + 1)
                    act.activation(pt[:, m % 2, :], tp[m % 2][:, 0:BAND], ACT.Copy).then_inc(pt_ready, 1)

            def split(n):
                act.wait_ge(att_turned, n + 1)
                act.activation(att_hi[:, :, ds(n * P, P)], ap_[:, :, :], ACT.Copy).then_inc(att_hi_s, 1)

            def body(n, tables, seq, after):
                copies(n, 0)
                exps(n, 1)
                if not first(n):
                    split(n - 1)
                copies(n, 1)
                exps(n + 1, 0)
                copies(n + 1, 0)
                exps(n + 1, 1)
                split(n)
                copies(n + 1, 1)
                if after is not None:
                    exps(n + 2, 0)

            exps(0, 0)
            pairs(act, body)
            split(NT - 1)

        @block.vector
        def _(dve):
            dve.sem_inc(scored, 1)
            dve.sem_inc(att_done, 1)
            dve.sem_inc(att_lo_s, 1)
            dve.wait_ge(sink_in, 16)
            dve.tensor_scalar(nsink[:, :], sink[:, :], -1.0, None, ALU.mult).then_inc(sink_neg, 1)
            dve.wait_ge(v_zero, 2)
            for t in range(NT):
                dve.wait_ge(v_turned, t + 1)
                at = t + 1 if t < QB else t + 2
                dve.tensor_copy(vn[:, at, :], tp[t % 2][:, 0:P]).then_inc(v_copied, 1)
            dve.wait_ge(sink_neg, 1)

            def stats(n, g, table):
                u = 2 * n + g
                dve.wait_ge(score_done, u + 5)
                dve.wait_ge(turned, 4 * u + 4)
                dve.scalar_tensor_tensor(out=sc[:, g, :, :], in0=sp_[:, :, 0:BAND], scalar=HEAD ** -0.5,
                                         in1=k.bias[:, table, g * GQ:(g + 1) * GQ, :], op0=ALU.mult,
                                         op1=ALU.add).then_inc(scored, 1)
                dve.wait_ge(scored, u + 2)
                dve.tensor_reduce(st[:, g, 0, :], sc[:, g, :, :], AX.X, ALU.max).then_inc(step, 1)
                dve.wait_ge(step, 2 * u + 1)
                dve.scalar_tensor_tensor(out=st[:, g, 1, :], in0=st[:, g, 0, :], scalar=-1.0,
                                         in1=nsink[:, g * GQ:(g + 1) * GQ], op0=ALU.mult, op1=ALU.min).then_inc(step, 1)
                dve.wait_ge(step, 2 * u + 2)
                dve.tensor_tensor(st[:, g, 2, :], st[:, g, 1, :], sink[:, g * GQ:(g + 1) * GQ], ALU.add).then_inc(ready, 1)

            def sums(n, s, g):
                u = 2 * n + g
                dve.wait_ge(probs, u + 1)
                dve.tensor_tensor(st[:, g, 5, :], st[:, g, 4, :], st[:, g, 3, :], ALU.add).then_inc(pv_step, 1)
                dve.wait_ge(pv_step, 2 * u + 1)
                dve.reciprocal(rden[:, s, g * GQ:(g + 1) * GQ], st[:, g, 5, :]).then_inc(pv_step, 1)

            def scale(n, s):
                dve.wait_ge(pv_done, 8 * n + 10)
                dve.wait_ge(pv_step, 4 * n + 4)
                dve.tensor_tensor(att[:, s, :].rearrange("p (h e) -> p h e", e=HEAD),
                                  pv[:, :].rearrange("p (h e) -> p h e", e=HEAD),
                                  rden[:, s, :].unsqueeze(2).to_broadcast([P, N_HEADS, HEAD]), ALU.mult).then_inc(att_done, 1)

            def rest(n):
                dve.wait_ge(att_hi_s, n + 1)
                dve.tensor_tensor(att_lo[:, :, ds(n * P, P)], ap_[:, :, :], att_hi[:, :, ds(n * P, P)].bitcast(F32),
                                  ALU.subtract).then_inc(att_lo_s, 1)

            def body(n, tables, seq, after):
                stats(n, 1, tables[0])
                sums(n, 0, 0)
                if not first(n):
                    rest(n - 1)
                stats(n + 1, 0, tables[1])
                sums(n, 0, 1)
                scale(n, 0)
                stats(n + 1, 1, tables[1])
                sums(n + 1, 1, 0)
                rest(n)
                if after is not None:
                    stats(n + 2, 0, after)
                sums(n + 1, 1, 1)
                scale(n + 1, 1)

            stats(0, 0, 1)
            pairs(dve, body)
            rest(NT - 1)



def stage_gated(k, tag, hi, lo, ktiles, unit0, gate0, add, out_sbuf=None):
    nc, d = k.nc, k.d
    per_unit = KT // ktiles
    n_units = KT // per_unit
    with ExitStack() as ctx:
        raw, whi, wlo = weight_ring(k, tag)
        gate = [k.at(f"{tag}_gate{s}", [P, T], F32, O_ST + s * 5120) for s in range(2)]
        other = [k.at(f"{tag}_other{s}", [P, T], F32, O_ST + 2 * 5120 + s * 5120) for s in range(2)] if add else None
        prod = [k.at(f"{tag}_prod{s}", [P, T], F32, O_W + 2 * 4096 + s * 16384) for s in range(2)]
        gp = [ctx.enter_context(nc.psum_tensor(f"{tag}_p{s}", [P, 3, 512], F32)) for s in range(2)]
        w_in = k.sems(ctx, f"{tag}_w_in0", f"{tag}_w_in1")
        g_in = k.sems(ctx, f"{tag}_g_in0", f"{tag}_g_in1")
        stored = k.sems(ctx, f"{tag}_stored0", f"{tag}_stored1")
        w_hi, w_lo, mm_done, sig, used, prod_done = k.sems(
            ctx, *(f"{tag}_{n}" for n in ("w_hi", "w_lo", "mm", "sig", "used", "prod")))
        loads = 2 if add else 1
        block = ctx.enter_context(nc.Block())

        @block.sync
        def _(sp):
            if not add:
                sp.sem_inc(stored[0], 16)
                sp.sem_inc(stored[1], 16)

            def load_unit(u, s):
                sp.wait_ge(w_lo, u + 1)
                sp.dma_start(raw[:, s, :], d["units"][ds(unit0 + u, 1), :, :].rearrange("u p n -> (u p) n")
                             ).then_inc(w_in[s], 16)

            def load_gate(c, s):
                sp.wait_ge(used, c + 1)
                sp.dma_start(gate[s][:, :], d["rest"][ds((gate0 + c) * P, P), :]).then_inc(g_in[s], 16)
                if add:
                    sp.dma_start(other[s][:, :], d["mix_a"][ds(c * P, P), :]).then_inc(g_in[s], 16)

            def store(c, s):
                sp.wait_ge(used, c + 3)
                sp.dma_start(d["mix_a"][ds(c * P, P), :], prod[s][:, :]).then_inc(stored[s], 16)

            load_unit(0, 0)
            load_unit(1, 1)
            load_gate(0, 0)
            load_gate(1, 1)
            with sp.Fori(0, n_units // 2 - 1) as i:
                for s in range(2):
                    load_unit(2 * i + s + 2, s)
                    for c in range(per_unit):
                        if not add:
                            store((2 * i + s) * per_unit + c, (s * per_unit + c) % 2)
                        load_gate((2 * i + s) * per_unit + c + 2, (s * per_unit + c) % 2)
            for c in range(KT - 2 * per_unit, KT):
                if not add:
                    store(c, c % 2)
                if c < KT - 2:
                    load_gate(c + 2, c % 2)
            if not add:
                sp.wait_ge(stored[0], 16 * (KT // 2 + 1))
                sp.wait_ge(stored[1], 16 * (KT // 2 + 1))

        @block.scalar
        def _(act):
            act.preload_act_table(ACT.Sigmoid)

            def split(u, s, n):
                act.wait_ge(w_in[s], 16 * n)
                act.wait_ge(mm_done, per_unit * (u + 1))
                act.activation(whi[:, s, :], raw[:, s, :], ACT.Copy).then_inc(w_hi, 1)

            def gates(c, s, n):
                act.wait_ge(g_in[s], 16 * loads * n)
                act.activation(gate[s][:, :], gate[s][:, :], ACT.Sigmoid).then_inc(sig, 1)

            split(0, 0, 1)
            split(1, 1, 1)
            with act.Fori(0, n_units // 2 - 1) as i:
                for s in range(2):
                    for c in range(per_unit):
                        gates((2 * i + s) * per_unit + c, (s * per_unit + c) % 2, i * per_unit + (s * per_unit + c) // 2 + 1)
                    split(2 * i + s + 2, s, i + 2)
            for c in range(KT - 2 * per_unit, KT):
                gates(c, c % 2, c // 2 + 1)

        @block.gpsimd
        def _(pool):
            pool.sem_inc(w_lo, 2)
            with pool.Fori(0, n_units // 2) as i:
                for s in range(2):
                    pool.wait_ge(w_hi, 2 * i + s + 1)
                    pool.tensor_tensor(wlo[:, s, :], raw[:, s, :], whi[:, s, :].bitcast(F32), ALU.subtract).then_inc(w_lo, 1)

        @block.tensor
        def _(pe):
            pe.sem_inc(mm_done, 2 * per_unit)
            with pe.Fori(0, n_units // 2) as i:
                for s in range(2):
                    pe.wait_ge(w_lo, 2 * i + s + 3)
                    for c in range(per_unit):
                        pe.wait_ge(used, (2 * i + s) * per_unit + c + 1)
                        w = (x[:, s, c * ktiles * P:(c + 1) * ktiles * P].rearrange("p (k c) -> p k c", k=ktiles)
                             for x in (whi, wlo))
                        pe_channel_tile(pe, gp[(s * per_unit + c) % 2], *w, hi, lo, ktiles).then_inc(mm_done, 1)

        @block.vector
        def _(dve):
            dve.sem_inc(used, 2)
            with dve.Fori(0, KT // 2) as i:
                for s in range(2):
                    c = 2 * i + s
                    dve.wait_ge(sig, c + 1)
                    dve.wait_ge(mm_done, c + 2 * per_unit + 1)
                    if not add:
                        dve.wait_ge(stored[s], 16 * (i + 1))
                    dve.tensor_tensor(prod[s][:, 0:1024].rearrange("p (a n) -> p a n", a=2), gp[s][:, 0:2, :],
                                      gate[s][:, 0:1024].rearrange("p (a n) -> p a n", a=2), ALU.mult).then_inc(prod_done, 1)
                    mm = dve.tensor_tensor(prod[s][:, 1024:T], gp[s][:, 2, 0:256], gate[s][:, 1024:T], ALU.mult)
                    if not add:
                        mm.then_inc(used, 1)
                    else:
                        mm.then_inc(prod_done, 1)
                        dve.wait_ge(prod_done, 2 * c + 2)
                        dve.tensor_tensor(out_sbuf[:, ds(c, 1), :].rearrange("p a t -> p (a t)"), prod[s][:, :],
                                          other[s][:, :], ALU.add).then_inc(used, 1)



class SsdTiles:

    def __init__(self, k):
        o = O_W
        self.dt = k.at("ssd_dt", [P, NT, 32], F32, o)
        self.dta = k.at("ssd_dta", [P, NT, 32], F32, o + 1280)
        self.e0 = k.at("ssd_e0", [P, 3, NT, N_SSD], F32, o + 2560)
        self.e1 = k.at("ssd_e1", [P, NT * 16 * 3], F32, o + 2560 + 1920)
        self.inc_f = self.e0[:, 2, :, :]
        self.inc_b = self.e1[:, 0:160].rearrange("p (t h) -> p t h", t=NT)
        self.tot = self.e1[:, 160:480].rearrange("p (t h) -> p t h", t=NT)
        self.cf = k.at("ssd_cf", [P, 2, NT, N_SSD], F32, o + 6400)
        self.et = k.at("ssd_et", [P, 2, NT, HPG], F32, o + 7680)
        self.st = [k.at(f"ssd_state{n}", [P, NT + 1, 512], F32, O_R2 + n * (NT + 1) * 2048) for n in range(2)]


def of_chunk(x, t):
    return x[:, ds(t, 1), :].rearrange("p a h -> p (a h)")


def per_head(x, width=SSD_HEAD):
    return x.unsqueeze(2).to_broadcast([P, x.shape[1], width])


def stage_ssd_decays(k, q):
    nc, d = k.nc, k.d
    with ExitStack() as ctx:
        w = k.at("dec_w", [P, 8, NT, 32], F32, O_R2)
        bias = k.at("dec_bias", [P, 32], F32, O_ST)
        alog = k.at("dec_alog", [P, 32], F32, O_ST + 128)
        sums = [ctx.enter_context(nc.psum_tensor(f"dec_p{n}", [P, 512], F32)) for n in range(2)]
        par_in, chain, exp_a, exp_v, ln_u, dta_ready, summed, exped = k.sems(
            ctx, *(f"dec_{n}" for n in ("par_in", "chain", "exp_a", "exp_v", "ln_u", "dta", "summed", "exped")))
        v, neg, mag, e, u, lnu, d0, z = (w[:, n, :, :] for n in range(8))
        block = ctx.enter_context(nc.Block())

        @block.sync
        def _(sp):
            sp.dma_start(bias[:, :], d["dt_bias"].partition_broadcast(P)).then_inc(par_in, 16)
            sp.dma_start(alog[:, :], d["a_log"].partition_broadcast(P)).then_inc(par_in, 16)

        @block.vector
        def _(dve):
            steps = [0]

            def step(ins):
                steps[0] += 1
                ins.then_inc(chain, 1)
                dve.wait_ge(chain, steps[0])

            dve.wait_ge(par_in, 32)
            step(dve.tensor_tensor(v, k.dt_raw[:, :, :], bias[:, :].unsqueeze(1).to_broadcast([P, NT, 32]), ALU.add))
            step(dve.tensor_scalar(neg, v, -1.0, None, ALU.mult))
            step(dve.tensor_tensor(mag, v, neg, ALU.max))
            dve.wait_ge(exp_v, 1)
            step(dve.tensor_scalar(u, e, 1.0, None, ALU.add))
            step(dve.tensor_scalar(d0, u, -1.0, None, ALU.add))
            step(dve.tensor_scalar(z, d0, 0.0, None, ALU.is_equal))
            step(dve.tensor_tensor(d0, d0, z, ALU.add))
            step(dve.reciprocal(mag, d0))
            step(dve.tensor_tensor(mag, mag, e, ALU.mult))
            step(dve.tensor_tensor(z, z, e, ALU.mult))
            dve.wait_ge(ln_u, 1)
            step(dve.tensor_tensor(mag, mag, lnu, ALU.mult))
            step(dve.tensor_tensor(mag, mag, z, ALU.add))
            step(dve.scalar_tensor_tensor(out=q.dt[:, :, :], in0=v, scalar=0.0, in1=mag, op0=ALU.max, op1=ALU.add))
            dve.wait_ge(exp_a, 1)
            dve.scalar_tensor_tensor(out=q.dta[:, :, :], in0=q.dt[:, :, :], scalar=-1.0,
                                     in1=alog[:, :].unsqueeze(1).to_broadcast([P, NT, 32]), op0=ALU.mult,
                                     op1=ALU.mult).then_inc(dta_ready, 1)
            dve.wait_ge(exped, 2)
            for n in range(2):
                dve.tensor_tensor(q.cf[:, n, :, :], q.dt[:, :, n * 16:(n + 1) * 16], q.e0[:, n, :, :], ALU.mult)
                for g in range(2):
                    rows = slice(g * 64, (g + 1) * 64)
                    dve.tensor_copy(q.et[rows, n, :, :], q.tot[rows, :, n * 16 + g * HPG:n * 16 + (g + 1) * HPG])

        @block.scalar
        def _(act):
            act.preload_act_table_set("natural_log_exp_and_others")
            act.wait_ge(par_in, 32)
            act.activation(alog[:, :], alog[:, :], ACT.Exp).then_inc(exp_a, 1)
            act.wait_ge(chain, 3)
            act.activation(e, mag, ACT.Exp, scale=-1.0).then_inc(exp_v, 1)
            act.wait_ge(chain, 4)
            act.activation(lnu, u, ACT.Ln).then_inc(ln_u, 1)
            act.wait_ge(summed, 1)
            act.activation(q.e0[:, :, :, :].rearrange("p a t h -> p (a t h)"), sums[0][:, 0:480], ACT.Exp).then_inc(exped, 1)
            act.activation(q.e1[:, :], sums[1][:, 0:480], ACT.Exp).then_inc(exped, 1)

        @block.tensor
        def _(pe):
            pe.wait_ge(dta_ready, 1)
            f, b = q.dta[:, :, 0:16], q.dta[:, :, 16:32]
            for bank, at, mask, rhs in ((0, 0, C_GT, f), (0, 160, C_LT, b), (0, 320, C_INCU, f), (1, 0, C_INCL, b),
                                        (1, 160, C_ONE, q.dta[:, :, :])):
                n = NT * rhs.shape[2]
                mm = pe.matmul(sums[bank][:, at:at + n].rearrange("p (t h) -> p t h", t=NT), k.const[:, mask:mask + P], rhs,
                               start=True, stop=True)
            mm.then_inc(summed, 1)


def stage_ssd_states(k, q):
    nc, d = k.nc, k.d
    sf, sb = q.st
    with ExitStack() as ctx:
        o = O_W + 9 * 1024
        xb = [k.at(f"sst_x{s}", [P, D + P], F32, o + s * 4608) for s in range(2)]
        xd = [[k.at(f"sst_xd{n}{s}", [P, D], F32, o + 9216 + (2 * n + s) * 4096) for s in range(2)] for n in range(2)]
        tmp = [k.at(f"sst_tmp{n}", [P, 512], F32, O_ST + 2048 * n) for n in range(2)]
        pp = [[ctx.enter_context(nc.psum_tensor(f"sst_p{n}{s}", [P, 512], F32)) for s in range(2)] for n in range(2)]
        x_in = k.sems(ctx, "sst_x_in0", "sst_x_in1")
        scaled_f, scaled_b, state_mm, saved, zeroed, chain_f, chain_b = k.sems(
            ctx, *(f"sst_{n}" for n in ("scaled_f", "scaled_b", "mm", "saved", "zeroed", "chain_f", "chain_b")))
        block = ctx.enter_context(nc.Block())

        @block.sync
        def _(sp):
            with sp.Fori(0, NT // 2) as i:
                for s in range(2):
                    sp.wait_ge(state_mm, 2 * i + s + 1)
                    sp.dma_start(xb[s][:, :], d["xtok"][ds((2 * i + s) * P, P), 0:D + P]).then_inc(x_in[s], 16)

        def scale(eng, n, i, s, done):
            t = 2 * i + s
            eng.wait_ge(x_in[s], 16 * (i + 1))
            eng.wait_ge(state_mm, t + 1)
            eng.tensor_tensor(xd[n][s][:, :].rearrange("p (h e) -> p h e", e=SSD_HEAD),
                              xb[s][:, 0:D].rearrange("p (h e) -> p h e", e=SSD_HEAD),
                              per_head(of_chunk(q.cf[:, n, :, :], t)), ALU.mult).then_inc(done, 1)

        @block.tensor
        def _(pe):
            pe.sem_inc(state_mm, 2)
            with pe.Fori(0, NT // 2) as i:
                for s in range(2):
                    t = 2 * i + s
                    pe.wait_ge(scaled_f, t + 1)
                    pe.wait_ge(scaled_b, t + 1)
                    pe.wait_ge(saved, t + 1)
                    for n in range(2):
                        for g in range(2):
                            mm = pe.matmul(pp[n][s][g * 64:(g + 1) * 64, :], xb[s][:, D + g * 64:D + (g + 1) * 64],
                                           xd[n][s][:, g * 512:(g + 1) * 512], start=True, stop=True)
                    mm.then_inc(state_mm, 1)

        @block.scalar
        def _(act):
            act.sem_inc(saved, 2)
            with act.Fori(0, NT // 2) as i:
                for s in range(2):
                    t = 2 * i + s
                    act.wait_ge(state_mm, t + 3)
                    act.activation(of_chunk(sf, t + 1), pp[0][s][:, :], ACT.Copy)
                    act.activation(of_chunk(sb, t), pp[1][s][:, :], ACT.Copy).then_inc(saved, 1)

        def carry(eng, n, to, frm, at, done, m):
            st = q.st[n]
            eng.tensor_tensor(tmp[n][:, :].rearrange("p (h e) -> p h e", e=SSD_HEAD),
                              st[:, frm, :].rearrange("p (h e) -> p h e", e=SSD_HEAD),
                              per_head(q.et[:, n, at, :]), ALU.mult).then_inc(done, 1)
            eng.wait_ge(done, 2 * m + 1)
            eng.tensor_tensor(st[:, to, :], st[:, to, :], tmp[n][:, :], ALU.add).then_inc(done, 1)
            eng.wait_ge(done, 2 * m + 2)

        @block.vector
        def _(dve):
            with dve.Fori(0, NT // 2) as i:
                for s in range(2):
                    scale(dve, 0, i, s, scaled_f)
            dve.wait_ge(saved, NT + 2)
            for x, slot in ((sf, 0), (sf, QB), (sb, QB), (sb, NT)):
                dve.memset(x[:, slot, :], 0.0).then_inc(zeroed, 1)
            for m, t in enumerate(range(1, QB - 1)):
                carry(dve, 0, t + 1, t, t, chain_f, m)

        @block.gpsimd
        def _(pool):
            with pool.Fori(0, NT // 2) as i:
                for s in range(2):
                    scale(pool, 1, i, s, scaled_b)
            pool.wait_ge(saved, NT + 2)
            for m, p in enumerate(range(QB - 2, 0, -1)):
                carry(pool, 1, p, p + 1, p, chain_b, m)


def stage_ssd_scan(k, q, y_hi, y_lo):
    nc, d = k.nc, k.d
    sf, sb = q.st
    with ExitStack() as ctx:
        at = [O_W + 9 * 1024]

        def tile(name, shape, dtype=F32):
            size = 4 * int(np.prod(shape[1:]))
            if at[0] < O_R1 and at[0] + size > O_R1:
                at[0] = O_ST
            x = k.at("scan_" + name, shape, dtype, at[0])
            at[0] += -(-size // 32) * 32
            return x

        xs = tile("x", [P, D])
        zs = tile("z", [P, D])
        hs = [tile(f"h{s}", [P, 2, 512]) for s in range(2)]
        bc = [tile(f"bc{s}", [P, 2, P]) for s in range(2)]
        xw = [tile(f"xw{s}", [P, 2, D]) for s in range(2)]
        xd = tile("xd", [P, D])
        rf = [tile(f"rf{s}", [P, 4, P]) for s in range(2)]
        rb = [tile(f"rb{s}", [P, 4, P]) for s in range(2)]
        mu = [tile(f"mu{s}", [P, 4, P]) for s in range(2)]
        ml = [tile(f"ml{s}", [P, 4, P]) for s in range(2)]
        cbm = tile("cbm", [P, 2, 2, P])
        y = tile("y", [P, D])
        t2 = tile("t2", [P, D])
        gain = k.at("scan_gain", [P, D], F32, O_KEEP)
        dsk = tile("dsk", [P, N_SSD])
        stat = tile("stat", [P, 3, 2])
        nh = tile("nh", [P, 2])
        assert at[0] <= 229368, at[0]
        seg = [ctx.enter_context(nc.psum_tensor(f"scan_seg{s}", [P, 4, P], F32)) for s in range(2)]
        cbp = ctx.enter_context(nc.psum_tensor("scan_cb", [P, 2, P], F32))
        yp = ctx.enter_context(nc.psum_tensor("scan_y", [P, D], F32))
        yo = ctx.enter_context(nc.psum_tensor("scan_yo", [P, 2, 512], F32))
        tr = ctx.enter_context(nc.psum_tensor("scan_tr", [P, 4, P], F32))
        bh_in = k.sems(ctx, "scan_bh_in0", "scan_bh_in1")
        names = ("par_in", "nh_set", "x_in", "z_in", "x_dt", "x_skip", "x_read", "r_ready", "seg_done", "exped", "m_ready",
                 "m_used", "cb_done", "cb_masked", "yo_done", "yo_read", "skip_done", "y_read", "turned", "hi_done",
                 "lo_done", "y_step", "gated", "squared", "var", "rstd", "ydone", "cb_half")
        (par_in, nh_set, x_in, z_in, x_dt, x_skip, x_read, r_ready, seg_done, exped, m_ready, m_used, cb_done, cb_masked,
         yo_done, yo_read, skip_done, y_read, turned, hi_done, lo_done, y_step, gated, squared, var, rstd, ydone,
         cb_half) = k.sems(ctx, *(f"scan_{n}" for n in names))
        ident = k.const[:, C_ID:C_ID + P]

        def heads(x, width=SSD_HEAD):
            return x.rearrange("p (h e) -> p h e", e=width)

        def chunks(eng, body):
            body(0, 0, True, False)
            with eng.Fori(0, NT // 2 - 1) as i:
                body(2 * i + 1, 1, False, False)
                body(2 * i + 2, 0, False, False)
            body(NT - 1, 1, False, True)

        def wait_past(eng, sem, count):
            if not (isinstance(count, int) and count < 1):
                eng.wait_ge(sem, count)

        block = ctx.enter_context(nc.Block())

        @block.sync
        def _(sp):
            sp.dma_start(gain[:, :], d["norm_g"].partition_broadcast(P)).then_inc(par_in, 16)
            sp.dma_start(dsk[:, :], d["d_skip"].partition_broadcast(P)).then_inc(par_in, 16)

            def load(t, s):
                wait_past(sp, yo_done, 2 * t - 2)
                wait_past(sp, x_read, 2 * t)
                sp.dma_start(xs[:, :], d["xtok"][ds(t * P, P), 0:D]).then_inc(x_in, 16)
                sp.dma_start(bc[s][:, :, :], d["bc"][:, ds(t * P, P)].rearrange("(m p) t -> p m t", p=P)).then_inc(bh_in[s], 16)
                sp.dma_start(hs[s][:, 0, :], of_chunk(sf, t)).then_inc(bh_in[s], 16)
                sp.dma_start(hs[s][:, 1, :], of_chunk(sb, t + 1)).then_inc(bh_in[s], 16)

            def body(t, s, first, last):
                if not last:
                    load(t + 1, 1 - s)
                wait_past(sp, gated, t)
                sp.dma_start(zs[:, :], d["ztok"][ds(t * P, P), :]).then_inc(z_in, 16)

            load(0, 0)
            chunks(sp, body)

        @block.gpsimd
        def _(pool):
            pool.memset(nh[:, :], -0.5).then_inc(nh_set, 1)

            def spans(t, quad):
                wait_past(pool, seg_done, 4 * t + quad - 1)
                for r, mask, first in ((rf, C_INCU, 0), (rb, C_INCL, 16)):
                    m = k.const[:, mask:mask + P].unsqueeze(1).to_broadcast([P, 4, P])
                    h = of_chunk(q.dta[:, :, first + 4 * quad:first + 4 * quad + 4], t)
                    ins = pool.tensor_tensor(r[quad % 2][:, :, :], m, per_head(h, P), ALU.mult)
                ins.then_inc(r_ready, 1)

            def skip(t):
                pool.wait_ge(x_in, 16 * (t + 1))
                wait_past(pool, skip_done, t)
                pool.tensor_tensor(heads(xd[:, :]), heads(xs[:, :]), per_head(dsk[:, :]), ALU.mult).then_inc(x_skip, 1)
                pool.wait_ge(x_skip, t + 1)
                pool.sem_inc(x_read, 1)

            def root(t):
                pool.wait_ge(var, t + 1)
                pool.tensor_tensor(stat[:, 2, :], stat[:, 1, :], nh[:, :], ALU.pow).then_inc(rstd, 1)

            def body(t, s, first, last):
                spans(t, 3)
                if not last:
                    spans(t + 1, 0)
                if not first:
                    root(t - 1)
                if not last:
                    spans(t + 1, 1)
                    spans(t + 1, 2)
                    skip(t + 1)

            pool.wait_ge(par_in, 32)
            pool.wait_ge(nh_set, 1)
            spans(0, 0)
            spans(0, 1)
            spans(0, 2)
            skip(0)
            chunks(pool, body)
            root(NT - 1)

        @block.tensor
        def _(pe):
            def sums(t, quad):
                n = 4 * t + quad
                pe.wait_ge(r_ready, n + 1)
                wait_past(pe, exped, n - 1)
                out = seg[quad % 2][:, :, :]
                pe.matmul(out, k.const[:, C_GT:C_GT + P], rf[quad % 2][:, :, :], start=True, stop=False)
                pe.matmul(out, k.const[:, C_LT:C_LT + P], rb[quad % 2][:, :, :], start=False, stop=True).then_inc(seg_done, 1)

            def cb(t, s):
                pe.wait_ge(bh_in[s], 24 * (t - s) + 48)
                wait_past(pe, cb_masked, t)
                for g in range(2):
                    mm = pe.matmul(cbp[:, g, :], bc[s][g * 64:(g + 1) * 64, 0, :], bc[s][g * 64:(g + 1) * 64, 1, :],
                                   start=True, stop=True)
                    if g == 0:
                        mm.then_inc(cb_half, 1)
                        pe.wait_ge(cb_half, t + 1)
                mm.then_inc(cb_done, 1)

            def apply(t, s, quad):
                if quad == 0:
                    pe.wait_ge(x_dt, t + 1)
                pe.wait_ge(m_ready, 4 * t + quad + 1)
                for m in range(4):
                    c = slice((4 * quad + m) * SSD_HEAD, (4 * quad + m + 1) * SSD_HEAD)
                    pe.matmul(yp[:, c], mu[quad % 2][:, m, :], xw[s][:, 0, c], start=False, stop=False)
                    mm = pe.matmul(yp[:, c], ml[quad % 2][:, m, :], xw[s][:, 1, c], start=False,
                                   stop=(m == 3 and quad % 2 == 1))
                mm.then_inc(m_used, 1)

            def skip(t):
                pe.wait_ge(x_skip, t + 1)
                wait_past(pe, y_read, t)
                for g in range(2):
                    c = slice(g * 512, (g + 1) * 512)
                    mm = pe.matmul(yp[:, c], ident, xd[:, c], start=True, stop=False)
                mm.then_inc(skip_done, 1)

            def carried(t, s, n):
                wait_past(pe, yo_read, 2 * t + n)
                for g in range(2):
                    mm = pe.matmul(yo[:, g, :], bc[s][g * 64:(g + 1) * 64, 1, :], hs[s][g * 64:(g + 1) * 64, n, :],
                                   start=True, stop=True)
                mm.then_inc(yo_done, 1)

            def turn(t, r):
                pe.wait_ge(ydone, t + 1)
                wait_past(pe, lo_done, 2 * t + r)
                for m in range(4):
                    c = 4 * r + m
                    mm = pe.transpose(tr[:, m, :], y[:, c * P:(c + 1) * P], ident)
                mm.then_inc(turned, 1)

            def body(t, s, first, last):
                skip(t)
                apply(t, s, 0)
                sums(t, 2)
                apply(t, s, 1)
                sums(t, 3)
                if not last:
                    cb(t + 1, 1 - s)
                apply(t, s, 2)
                if not first:
                    turn(t - 1, 0)
                if not last:
                    sums(t + 1, 0)
                apply(t, s, 3)
                if not first:
                    turn(t - 1, 1)
                carried(t, s, 0)
                carried(t, s, 1)
                if not last:
                    sums(t + 1, 1)

            cb(0, 0)
            sums(0, 0)
            sums(0, 1)
            chunks(pe, body)
            turn(NT - 1, 0)
            turn(NT - 1, 1)

        @block.scalar
        def _(act):
            def exp(t, quad):
                n = 4 * t + quad
                act.wait_ge(seg_done, n + 1)
                wait_past(act, m_used, n - 1)
                act.activation(mu[quad % 2][:, :, :], seg[quad % 2][:, :, :], ACT.Exp).then_inc(exped, 1)

            def split(t, r):
                act.wait_ge(turned, 2 * t + r + 1)
                act.activation(y_hi[:, 4 * r:4 * r + 4, ds(t * P, P)], tr[:, :, :], ACT.Copy).then_inc(hi_done, 1)

            def squares(t):
                act.wait_ge(gated, t + 1)
                for g in range(2):
                    ins = act.activation(t2[:, g * 512:(g + 1) * 512], y[:, g * 512:(g + 1) * 512], ACT.Square,
                                         accum_out=stat[:, 0, g:g + 1])
                ins.then_inc(squared, 1)

            def body(t, s, first, last):
                exp(t, 1)
                exp(t, 2)
                if not first:
                    squares(t - 1)
                exp(t, 3)
                if not first:
                    split(t - 1, 0)
                if not last:
                    exp(t + 1, 0)
                if not first:
                    split(t - 1, 1)

            exp(0, 0)
            chunks(act, body)
            squares(NT - 1)
            split(NT - 1, 0)
            split(NT - 1, 1)

        @block.vector
        def _(dve):
            dve.wait_ge(par_in, 32)

            def weigh(t, quad):
                n = 4 * t + quad
                dve.wait_ge(exped, n + 1)
                wait_past(dve, m_used, n - 1)
                for out, half in ((ml, 1), (mu, 0)):
                    ins = dve.tensor_tensor(out[quad % 2][:, :, :], mu[quad % 2][:, :, :],
                                            cbm[:, half, quad // 2, :].unsqueeze(1).to_broadcast([P, 4, P]), ALU.mult)
                ins.then_inc(m_ready, 1)

            def rest(t, r):
                dve.wait_ge(hi_done, 2 * t + r + 1)
                dve.tensor_tensor(y_lo[:, 4 * r:4 * r + 4, ds(t * P, P)], tr[:, :, :],
                                  y_hi[:, 4 * r:4 * r + 4, ds(t * P, P)].bitcast(F32), ALU.subtract).then_inc(lo_done, 1)

            def weigh_x(t, s):
                dve.wait_ge(x_in, 16 * (t + 1))
                wait_past(dve, m_used, 4 * t - 4)
                for n in range(2):
                    ins = dve.tensor_tensor(heads(xw[s][:, n, :]), heads(xs[:, :]),
                                            per_head(of_chunk(q.dt[:, :, n * 16:(n + 1) * 16], t)), ALU.mult)
                ins.then_inc(x_dt, 1)
                dve.wait_ge(x_dt, t + 1)
                dve.sem_inc(x_read, 1)

            def mask_cb(t):
                dve.wait_ge(cb_done, t + 1)
                wait_past(dve, m_ready, 4 * t)
                for half, mask in ((0, C_INCU), (1, C_INCL)):
                    ins = dve.tensor_tensor(cbm[:, half, :, :], cbp[:, :, :],
                                            k.const[:, mask:mask + P].unsqueeze(1).to_broadcast([P, 2, P]), ALU.mult)
                ins.then_inc(cb_masked, 1)

            def forward(t):
                dve.wait_ge(yo_done, 2 * t + 1)
                wait_past(dve, turned, 2 * t)
                dve.tensor_tensor(heads(y[:, :]), yo[:, :, :].rearrange("p g (h e) -> p (g h) e", e=SSD_HEAD),
                                  per_head(of_chunk(q.inc_f, t)), ALU.mult).then_inc(yo_read, 1)

            def within(t):
                dve.wait_ge(m_used, 4 * t + 4)
                dve.wait_ge(yo_read, 2 * t + 1)
                dve.tensor_tensor(y[:, :], yp[:, :], y[:, :], ALU.add).then_inc(y_read, 1)

            def backward(t):
                dve.wait_ge(yo_done, 2 * t + 2)
                dve.tensor_tensor(heads(t2[:, :]), yo[:, :, :].rearrange("p g (h e) -> p (g h) e", e=SSD_HEAD),
                                  per_head(of_chunk(q.inc_b, t)), ALU.mult).then_inc(yo_read, 1)

            def gate(t):
                dve.wait_ge(yo_read, 2 * t + 2)
                dve.wait_ge(y_read, t + 1)
                dve.tensor_tensor(y[:, :], y[:, :], t2[:, :], ALU.add).then_inc(y_step, 1)
                dve.wait_ge(y_step, 2 * t + 1)
                dve.wait_ge(z_in, 16 * (t + 1))
                dve.tensor_tensor(y[:, :], y[:, :], zs[:, :], ALU.mult).then_inc(gated, 1)

            def norm(t):
                dve.wait_ge(squared, t + 1)
                dve.tensor_scalar(stat[:, 1, :], stat[:, 0, :], 1.0 / 512, EPS, ALU.mult, ALU.add).then_inc(var, 1)
                dve.wait_ge(rstd, t + 1)
                for g in range(2):
                    c = slice(g * 512, (g + 1) * 512)
                    dve.scalar_tensor_tensor(out=y[:, c], in0=y[:, c], scalar=stat[:, 2, g:g + 1], in1=gain[:, c],
                                             op0=ALU.mult, op1=ALU.mult).then_inc(ydone if g else y_step, 1)

            def body(t, s, first, last):
                if not first:
                    within(t - 1)
                    backward(t - 1)
                weigh(t, 1)
                if not first:
                    gate(t - 1)
                weigh(t, 2)
                if not first:
                    norm(t - 1)
                weigh(t, 3)
                if not last:
                    mask_cb(t + 1)
                    weigh_x(t + 1, 1 - s)
                if not first:
                    rest(t - 1, 0)
                if not last:
                    dve.wait_ge(cb_masked, t + 2)
                    weigh(t + 1, 0)
                if not first:
                    rest(t - 1, 1)
                forward(t)

            mask_cb(0)
            weigh_x(0, 0)
            dve.wait_ge(cb_masked, 1)
            weigh(0, 0)
            chunks(dve, body)
            within(NT - 1)
            backward(NT - 1)
            gate(NT - 1)
            norm(NT - 1)
            rest(NT - 1, 0)
            rest(NT - 1, 1)

class Routing:

    def __init__(self, k):
        o = O_KEEP
        self.logits = k.at("logits", [P, NT, 20], F32, o)
        self.weight = k.at("pair_weight", [P, 2, NT], F32, o + 800)
        self.slot = k.at("pair_slot", [P, 2, NT], I32, o + 896)
        self.expert = k.at("block_expert", [P, NBLK], I32, o + 992)
        self.ids = k.at("token_ids", [P, NT], I32, o + 1152)


class TileNorm:

    def __init__(self, k, tag, gain, o_gain, o_stats):
        self.gain = gain
        self.gb = k.at(f"{tag}_g", [P, D], F32, o_gain)
        self.st = k.at(f"{tag}_st", [P, NT, 4], F32, o_stats)
        self.nh = k.at(f"{tag}_nh", [P, 1], F32, o_stats + 160)
        self.g_in, self.half_set, self.squared, self.scaled, self.rstd, self.normed = k.sems(
            None, *(f"{tag}_{n}" for n in ("g_in", "half_set", "squared", "scaled", "rstd", "normed")))

    def load(self, sp):
        sp.dma_start(self.gb[:, :], self.gain.partition_broadcast(P)).then_inc(self.g_in, 16)

    def square(self, act, t, x, junk):
        act.activation(junk, x, ACT.Square, accum_out=self.st[:, t, 0:1]).then_inc(self.squared, 1)

    def root(self, pool):
        pool.memset(self.nh[:, :], -0.5).then_inc(self.half_set, 1)
        pool.wait_ge(self.half_set, 1)
        for t in range(NT):
            pool.wait_ge(self.scaled, t + 1)
            pool.tensor_tensor(self.st[:, t, 2:3], self.st[:, t, 1:2], self.nh[:, :], ALU.pow).then_inc(self.rstd, 1)

    def norm(self, dve, t, x, out):
        if t == 0:
            dve.wait_ge(self.g_in, 16)
        dve.wait_ge(self.squared, t + 1)
        dve.tensor_scalar(self.st[:, t, 1:2], self.st[:, t, 0:1], 1.0 / D, EPS, ALU.mult, ALU.add).then_inc(self.scaled, 1)
        dve.wait_ge(self.rstd, t + 1)
        dve.scalar_tensor_tensor(out=out, in0=x, scalar=self.st[:, t, 2:3], in1=self.gb[:, :], op0=ALU.mult,
                                 op1=ALU.mult).then_inc(self.normed, 1)


def tile_views(k, tag, offset):
    return [k.at(f"{tag}_hi_done", [P, KT, T], F32, offset), k.at(f"{tag}_lo_done", [P, KT, T], F32, offset + KT * T * 4)]


def of_tile(x, t):
    return x[:, :, t * P:(t + 1) * P]


def by_ktile(x):
    return x.rearrange("p (k n) -> p k n", k=KT)



def stage_out_route(k, mixed, hi, lo, x1, r):
    nc, d = k.nc, k.d
    with ExitStack() as ctx:
        w = ResidentUnits(k, "out", U_OUT, [O_ST + 4096 * j for j in range(4)])
        xin = [k.at(f"out_x{s}", [P, D], F32, O_ST + 4096 * (4 + s)) for s in range(2)]
        rw = k.at("nr_rw", [P, KT, 20], F32, O_ST + 6 * 4096)
        rb = k.at("nr_rb", [P, 20], F32, O_ST + 6 * 4096 + 640)
        norm = TileNorm(k, "nr", d["g_ffn"], O_R2 + 10 * 4096, O_ST + 6 * 4096 + 736)
        h2, turned_h2 = tile_views(k, "out", O_R1)
        zp = [ctx.enter_context(nc.psum_tensor(f"out_p{b}", [P, D], F32)) for b in range(2)]
        tp = ctx.enter_context(nc.psum_tensor("nr_tp", [P, KT, P], F32))
        lp = ctx.enter_context(nc.psum_tensor("nr_lg", [P, NT, 20], F32))
        x_in = k.sems(ctx, "out_x_in0", "out_x_in1")
        tile_done, added, m_hi, m_lo, par_in, stored, turned, copied, routed = k.sems(
            ctx, "out_tile", "out_added", "out_m_hi", "out_m_lo", "nr_par_in", "nr_stored", "nr_turned", "nr_copied",
            "nr_routed")
        ident = k.const[:, C_ID:C_ID + P]
        block = ctx.enter_context(nc.Block())

        @block.sync
        def _(sp):
            w.load(sp)
            norm.load(sp)
            sp.dma_start(rw[:, :, :], d["router"]).then_inc(par_in, 16)
            sp.dma_start(rb[:, :], d["router_b"].partition_broadcast(P)).then_inc(par_in, 16)
            sp.dma_start(r.ids[:, :], d["ids"]).then_inc(par_in, 16)
            for t in range(NT):
                if t >= 2:
                    sp.wait_ge(added, t - 1)
                sp.dma_start(xin[t % 2][:, :], d["x"][t * P:(t + 1) * P, :]).then_inc(x_in[t % 2], 16)
                if t >= 2:
                    sp.wait_ge(norm.normed, t - 1)
                    sp.dma_start(by_ktile(d["h2"][(t - 2) * P:(t - 1) * P, :]), of_tile(h2, t - 2)).then_inc(stored, 16)
            for t in (NT - 2, NT - 1):
                sp.wait_ge(norm.normed, t + 1)
                sp.dma_start(by_ktile(d["h2"][t * P:(t + 1) * P, :]), of_tile(h2, t)).then_inc(stored, 16)
            sp.wait_ge(stored, 16 * NT)

        @block.gpsimd
        def _(pool):
            for n in range(1, 8, 2):
                w.split_lo(pool, n)
            norm.root(pool)

        @block.scalar
        def _(act):
            for t in range(NT):
                act.activation(of_tile(hi, t), of_tile(mixed, t), ACT.Copy).then_inc(m_hi, 1)
                for n in range(2 * t, min(2 * t + 2, 8)):
                    w.split_hi(act, n)
            for t in range(NT + 1):
                if t < NT:
                    act.wait_ge(added, t + 1)
                    norm.square(act, t, by_ktile(x1[:, t, :]), of_tile(turned_h2, t))
                if t:
                    act.wait_ge(turned, t)
                    act.activation(of_tile(turned_h2, t - 1), tp[:, :, :], ACT.Copy).then_inc(copied, 1)

        @block.tensor
        def _(pe):
            def turn(t):
                pe.wait_ge(norm.normed, t + 1)
                if t:
                    pe.wait_ge(copied, t)
                for c in range(KT):
                    mm = pe.transpose(tp[:, c, :], h2[:, c, t * P:(t + 1) * P], ident)
                mm.then_inc(turned, 1)

            def logits(t):
                pe.wait_ge(copied, t + 1)
                for c in range(KT):
                    mm = pe.matmul(lp[:, t, :], turned_h2[:, c, t * P:(t + 1) * P], rw[:, c, :], start=(c == 0),
                                   stop=(c == KT - 1))
                mm.then_inc(routed, 1)

            for t in range(NT):
                pe.wait_ge(m_lo, t + 1)
                if t >= 2:
                    pe.wait_ge(added, t - 1)
                for c in range(2):
                    mm = pe_token_tile(pe, zp[t % 2][:, c * 512:(c + 1) * 512], hi, lo, t, w, c)
                mm.then_inc(tile_done, 1)
                if t == 1:
                    pe.wait_ge(par_in, 48)
                if t >= 2:
                    logits(t - 2)
                if t >= 1:
                    turn(t - 1)
            logits(NT - 2)
            turn(NT - 1)
            logits(NT - 1)

        @block.vector
        def _(dve):
            for t in range(NT):
                dve.wait_ge(m_hi, t + 1)
                dve.tensor_tensor(of_tile(lo, t), of_tile(mixed, t), of_tile(hi, t).bitcast(F32), ALU.subtract
                                  ).then_inc(m_lo, 1)
                if t < 4:
                    w.split_lo(dve, 2 * t)
            dve.wait_ge(m_lo, NT)
            for t in range(NT):
                dve.wait_ge(x_in[t % 2], 16 * (t // 2 + 1))
                dve.wait_ge(tile_done, t + 1)
                dve.tensor_tensor(x1[:, t, :], zp[t % 2][:, :], xin[t % 2][:, :], ALU.add).then_inc(added, 1)
                norm.norm(dve, t, by_ktile(x1[:, t, :]), of_tile(h2, t))
            dve.wait_ge(routed, NT)
            dve.wait_ge(par_in, 48)
            dve.tensor_tensor(r.logits[:, :, :], lp[:, :, :], rb[:, :].unsqueeze(1).to_broadcast([P, NT, 20]), ALU.add)


def stage_route(k, r):
    nc, d = k.nc, k.d
    with ExitStack() as ctx:
        at = [O_R1 + 11 * 4096]

        def tile(name, shape, dtype=F32):
            x = k.at("rt_" + name, shape, dtype, at[0])
            at[0] += -(-4 * int(np.prod(shape[1:])) // 32) * 32
            return x

        gmax, gsum, psel = (tile(n, [P, NT]) for n in ("gmax", "gsum", "psel"))
        gexp, geq, goh, sel, sel2, eeq, o1, o2 = (tile(n, [P, NT, 4]) for n in (
            "gexp", "geq", "goh", "sel", "sel2", "eeq", "o1", "o2"))
        m1, m2, e2, mr = (tile(n, [P, NT]) for n in ("m1", "m2", "e2", "mr"))
        wide = tile("wide", [P, NT, 4, 4])
        a1, a2, both, off, w16 = (tile(n, [P, NT, N_EXP]) for n in ("a1", "a2", "both", "off", "w16"))
        base = tile("base", [P, NT + 1, N_EXP])
        over = tile("over", [P, N_EXP, NT])
        nb, upto, first, ones = (tile(n, [P, N_EXP]) for n in ("nb", "upto", "first", "ones"))
        past = tile("past", [P, NBLK, N_EXP])
        bex = tile("bex", [P, NBLK])
        slot = tile("slot", [P, 2, NT])
        zero = tile("zero", [P, NBLK], I32)
        pp = [ctx.enter_context(nc.psum_tensor(f"rt_p{n}", [P, 512], F32)) for n in range(2)]
        chain, exps, counted, table_zero, slots_ready, zero_set = k.sems(
            ctx, "rt_chain", "rt_exps", "rt_counted", "rt_table_zero", "rt_slots", "rt_zero")
        scattered = k.sems(ctx, "rt_scattered0", "rt_scattered1")
        pair_done, exp_in = k.sems(ctx, "rt_pairs", "rt_exp_in")
        kt = PLE // P
        w = ResidentUnits(k, "pp", U_PP, [], 2)
        p_hi, p_lo = split_pair(k, "p", kt)
        pin = k.at("p_in", [P, NT, PLE], F32, O_R1 + 6 * 4096)
        out = [k.at(f"pp_out{s}", [P, D], F32, O_R1 + (9 + s) * 4096) for s in range(2)]
        tp = [ctx.enter_context(nc.psum_tensor(f"pp_tp{s}", [P, kt, P], F32)) for s in range(2)]
        zp = [ctx.enter_context(nc.psum_tensor(f"pp_p{s}", [P, D], F32)) for s in range(2)]
        pp_stored = k.sems(ctx, "pp_stored0", "pp_stored1")
        p_in, p_turned, hi_s, lo_s, pp_done, pp_copied = k.sems(
            ctx, *(f"pp_{n}" for n in ("p_in", "turned", "hi", "lo", "done", "copied")))
        ident = k.const[:, C_ID:C_ID + P]
        rank = k.const[:, C_RANK:C_RANK + 4].unsqueeze(1).to_broadcast([P, NT, 4])
        block = ctx.enter_context(nc.Block())

        @block.sync
        def _(sp):
            sp.dma_start(pin[:, :, :], d["p"].rearrange("(t p) c -> p t c", p=P)).then_inc(p_in, 16)
            w.load(sp)
            for t in range(NT):
                sp.wait_ge(pp_copied, t + 1)
                sp.dma_start(d["pp"][t * P:(t + 1) * P, :], out[t % 2][:, :]).then_inc(pp_stored[t % 2], 16)
            for s in range(2):
                sp.wait_ge(pp_stored[s], 16 * (NT // 2))

        @block.vector
        def _(dve):
            steps = [0]

            def step(ins):
                steps[0] += 1
                ins.then_inc(chain, 1)
                dve.wait_ge(chain, steps[0])

            def over4(x):
                return x.unsqueeze(2).to_broadcast([P, NT, 4])

            def first_max(x, top, hot):
                step(dve.tensor_reduce(top, x, AX.X, ALU.max))
                step(dve.tensor_tensor(hot, x, over4(top), ALU.is_equal))
                step(dve.tensor_tensor(hot, hot, rank, ALU.mult))
                step(dve.tensor_reduce(mr[:, :], hot, AX.X, ALU.max))
                step(dve.tensor_tensor(hot, hot, over4(mr[:, :]), ALU.is_equal))

            dve.memset(zero[:, :], 0).then_inc(zero_set, 1)
            dve.memset(base[:, 0, :], 0.0)
            dve.memset(ones[:, :], 1.0)
            lg, le = r.logits[:, :, 0:4], r.logits[:, :, 4:20].rearrange("p t (g e) -> p t g e", g=4)
            first_max(lg, gmax[:, :], goh[:, :, :])
            dve.tensor_tensor(gexp[:, :, :], lg, over4(gmax[:, :]), ALU.subtract).then_inc(exp_in, 1)
            step(dve.tensor_tensor(wide[:, :, :, :], le, goh[:, :, :].unsqueeze(3).to_broadcast([P, NT, 4, 4]), ALU.mult))
            step(dve.tensor_reduce(sel[:, :, :], wide[:, :, :, :].rearrange("p t g e -> p t e g"), AX.X, ALU.add))
            first_max(sel[:, :, :], m1[:, :], o1[:, :, :])
            step(dve.scalar_tensor_tensor(out=sel2[:, :, :], in0=o1[:, :, :], scalar=NEG, in1=sel[:, :, :], op0=ALU.mult,
                                          op1=ALU.add))
            first_max(sel2[:, :, :], m2[:, :], o2[:, :, :])
            dve.tensor_tensor(e2[:, :], m2[:, :], m1[:, :], ALU.subtract).then_inc(exp_in, 1)
            for a, o in ((a1, o1), (a2, o2)):
                step(dve.tensor_tensor(a[:, :, :].rearrange("p t (g e) -> p t g e", g=4),
                                       goh[:, :, :].unsqueeze(3).to_broadcast([P, NT, 4, 4]),
                                       o[:, :, :].unsqueeze(2).to_broadcast([P, NT, 4, 4]), ALU.mult))
            dve.tensor_tensor(both[:, :, :], a1[:, :, :], a2[:, :, :], ALU.add).then_inc(pair_done, 1)
            dve.wait_ge(exps, 1)
            step(dve.tensor_reduce(gsum[:, :], gexp[:, :, :], AX.X, ALU.add))
            step(dve.reciprocal(psel[:, :], gsum[:, :]))
            dve.wait_ge(exps, 2)
            step(dve.tensor_scalar(m1[:, :], e2[:, :], 1.0, None, ALU.add))
            step(dve.reciprocal(m2[:, :], m1[:, :]))
            step(dve.tensor_tensor(r.weight[:, 0, :], m2[:, :], psel[:, :], ALU.mult))
            step(dve.tensor_tensor(r.weight[:, 1, :], e2[:, :], r.weight[:, 0, :], ALU.mult))
            dve.wait_ge(counted, 1)
            tot = pp[1][:, 0:160].rearrange("p (t e) -> p t e", t=NT)
            for t in range(NT):
                step(dve.tensor_tensor(base[:, t + 1, :], tot[:, t, :], base[:, t, :], ALU.add))
            step(dve.tensor_tensor(over[:, :, :], base[:, NT, :].unsqueeze(2).to_broadcast([P, N_EXP, NT]),
                                   k.const[:, C_TH:C_TH + NT].unsqueeze(1).to_broadcast([P, N_EXP, NT]), ALU.is_gt))
            step(dve.tensor_reduce(nb[:, :], over[:, :, :], AX.X, ALU.add))
            step(dve.tensor_tensor_scan(upto[:, :], ones[:, :], nb[:, :], 0.0, ALU.mult, ALU.add))
            step(dve.tensor_tensor(first[:, :], upto[:, :], nb[:, :], ALU.subtract))
            step(dve.tensor_tensor(off[:, :, :], pp[0][:, 0:160].rearrange("p (t e) -> p t e", t=NT), base[:, 0:NT, :], ALU.add))
            step(dve.scalar_tensor_tensor(out=off[:, :, :], in0=first[:, :].unsqueeze(1).to_broadcast([P, NT, N_EXP]),
                                          scalar=float(P), in1=off[:, :, :], op0=ALU.mult, op1=ALU.add))
            for n, a in enumerate((a1, a2)):
                step(dve.tensor_tensor(w16[:, :, :], a[:, :, :], off[:, :, :], ALU.mult))
                step(dve.tensor_reduce(slot[:, n, :], w16[:, :, :], AX.X, ALU.add))
            dve.tensor_copy(r.slot[:, :, :], slot[:, :, :]).then_inc(slots_ready, 1)
            step(dve.tensor_tensor(past[:, :, :], upto[:, :].unsqueeze(1).to_broadcast([P, NBLK, N_EXP]),
                                   k.const[:, C_IOTA:C_IOTA + NBLK].unsqueeze(2).to_broadcast([P, NBLK, N_EXP]), ALU.is_le))
            step(dve.tensor_reduce(bex[:, :], past[:, :, :], AX.X, ALU.add))
            dve.tensor_scalar(r.expert[:, :], bex[:, :], float(N_EXP - 1), None, ALU.min)
            for n in range(2):
                w.split_lo(dve, n)
            for t in range(NT):
                dve.wait_ge(hi_s, t + 1)
                dve.tensor_tensor(of_tile(p_lo, t), tp[t % 2][:, :, :], of_tile(p_hi, t).bitcast(F32), ALU.subtract
                                  ).then_inc(lo_s, 1)

        @block.scalar
        def _(act):
            act.preload_act_table(ACT.Exp)
            act.wait_ge(exp_in, 1)
            act.activation(gexp[:, :, :], gexp[:, :, :], ACT.Exp).then_inc(exps, 1)
            act.wait_ge(exp_in, 2)
            act.activation(e2[:, :], e2[:, :], ACT.Exp).then_inc(exps, 1)
            for n in range(2):
                w.split_hi(act, n)
            for t in range(NT + 1):
                if t < NT:
                    act.wait_ge(p_turned, t + 1)
                    act.activation(of_tile(p_hi, t), tp[t % 2][:, :, :], ACT.Copy).then_inc(hi_s, 1)
                if t:
                    act.wait_ge(pp_done, t)
                    if t >= 3:
                        act.wait_ge(pp_stored[(t - 1) % 2], 16 * ((t - 1) // 2))
                    act.activation(out[(t - 1) % 2][:, :], zp[(t - 1) % 2][:, :], ACT.Copy).then_inc(pp_copied, 1)

        @block.tensor
        def _(pe):
            pe.wait_ge(pair_done, 1)
            rhs = both[:, :, :]
            for n, mask in ((0, C_LT), (1, C_ONE)):
                mm = pe.matmul(pp[n][:, 0:160].rearrange("p (t e) -> p t e", t=NT), k.const[:, mask:mask + P], rhs,
                               start=True, stop=True)
            mm.then_inc(counted, 1)

            def turn(t):
                if t >= 2:
                    pe.wait_ge(lo_s, t - 1)
                for c in range(kt):
                    mm = pe.transpose(tp[t % 2][:, c, :], pin[:, t, c * P:(c + 1) * P], ident)
                mm.then_inc(p_turned, 1)

            pe.wait_ge(p_in, 16)
            turn(0)
            for t in range(NT):
                if t + 1 < NT:
                    turn(t + 1)
                pe.wait_ge(lo_s, t + 1)
                if t >= 2:
                    pe.wait_ge(pp_copied, t - 1)
                for c in range(2):
                    mm = pe_token_tile(pe, zp[t % 2][:, c * 512:(c + 1) * 512], p_hi, p_lo, t, w, c, kt)
                mm.then_inc(pp_done, 1)

        @block.gpsimd
        def _(pool):
            pool.wait_ge(zero_set, 1)
            pool.dma_start(d["slots"].rearrange("(p n) o -> p (n o)", p=P), zero[:, :]).then_inc(table_zero, 16)
            pool.wait_ge(table_zero, 16)
            pool.wait_ge(slots_ready, 1)
            for n in range(2):
                for t in range(NT):
                    pool.indirect_dma_start(
                        out=d["slots"], out_offset=bass.IndirectOffsetOnAxis(ap=r.slot[:, n, t:t + 1].bitcast(U32), axis=0),
                        in_=r.ids[:, t:t + 1], in_offset=None).then_inc(scattered[n], 16)
            pool.wait_ge(scattered[0], 16 * NT)
            pool.wait_ge(scattered[1], 16 * NT)



def stage_experts(k, r):
    nc, d = k.nc, k.d
    with ExitStack() as ctx:
        raw = [k.at(f"ex_raw{s}", [P, 6, 1024], F32, O_W + 6 * 4096 * s) for s in range(2)]
        wlo = [k.at(f"ex_wlo{s}", [P, 6, 1024], F32R, O_W + 6 * 4096 * s) for s in range(2)]
        whi = [k.at(f"ex_whi{s}", [P, 6, 1024], F32R, O_W + 6 * 4096 * (s + 2)) for s in range(2)]
        o = O_W + 24 * 4096
        idx = [k.at(f"ex_idx{s}", [P, 1], I32, o + 32 * s) for s in range(2)]
        xg = [k.at(f"ex_x{s}", [P, D], F32, o + 64 + 4096 * s) for s in range(2)]
        xh = k.at("ex_xh", [P, KT, P], F32R, o + 64 + 8192)
        xl = k.at("ex_xl", [P, KT, P], F32R, o + 64 + 12288)
        act_t = k.at("ex_silu", [P, F], F32, o + 64 + 16384)
        hid = k.at("ex_hid", [P, F], F32, o + 64 + 17408)
        ah = k.at("ex_ah", [P, 2, P], F32R, o + 64 + 18432)
        al = k.at("ex_al", [P, 2, P], F32R, o + 64 + 19456)
        ys = [k.at(f"ex_y{s}", [P, D], F32, o + 64 + 20480 + 4096 * s) for s in range(2)]
        tx = ctx.enter_context(nc.psum_tensor("ex_tx", [P, KT, P], F32))
        gu = [ctx.enter_context(nc.psum_tensor(f"ex_gu{s}", [P, 2 * F], F32)) for s in range(2)]
        ta = ctx.enter_context(nc.psum_tensor("ex_ta", [P, 2, P], F32))
        yp = ctx.enter_context(nc.psum_tensor("ex_yp", [P, D], F32))
        w_in = [k.sems(ctx, *(f"ex_w_in{s}{n}" for n in range(6))) for s in range(2)]
        w_hi = k.sems(ctx, *(f"ex_w_hi{n}" for n in range(6)))
        w_lo = k.sems(ctx, *(f"ex_w_lo{n}" for n in range(6)))
        w_used = k.sems(ctx, *(f"ex_w_used{n}" for n in range(6)))
        idx_in = k.sems(ctx, "ex_idx_in0", "ex_idx_in1")
        x_in = k.sems(ctx, "ex_x_in0", "ex_x_in1")
        stored = k.sems(ctx, "ex_stored0", "ex_stored1")
        names = ("x_turned", "x_hi", "x_lo", "silu", "hid", "a_turned", "a_hi", "a_lo", "y_copied")
        (x_turned, x_hi, x_lo, silu, hid_done, a_turned, a_hi, a_lo, y_copied) = k.sems(
            ctx, *(f"ex_{n}" for n in names))
        ident = k.const[:, C_ID:C_ID + P]
        block = ctx.enter_context(nc.Block())

        def blocks(eng, body):
            body(0, 0, NBLK - 1)
            with eng.Fori(0, (NBLK - 3) // 2) as i:
                body(2 * i + 1, 1, 2)
                body(2 * i + 2, 0, 2)
            body(NBLK - 2, 1, 1)
            body(NBLK - 1, 0, 0)

        @block.sync
        def _(sp):
            sp.sem_inc(stored[0], 16)
            sp.sem_inc(stored[1], 16)

            def weights(b, s, units):
                e = sp.value_load(r.expert[0:1, ds(b, 1)], min_val=0, max_val=N_EXP - 1)
                for n in units:
                    sp.wait_ge(w_used[n], b + 1)
                    sp.dma_start(raw[s][:, n, :], d["experts"][ds(e * (6 * P) + n * P, P), :]).then_inc(w_in[s][n], 16)

            def index(b, s):
                sp.wait_ge(x_turned, b + 1)
                sp.dma_start(idx[s][:, :], d["slots"][ds(b * P, P), :]).then_inc(idx_in[s], 16)

            def store(b, s):
                sp.wait_ge(y_copied, b + 2)
                sp.dma_start(d["y_slots"][ds(b * P, P), :], ys[s][:, :]).then_inc(stored[s], 16)

            def body(b, s, more):
                if more > 1:
                    index(b + 2, s)
                    weights(b + 2, s, range(4))
                if more:
                    weights(b + 1, 1 - s, (4, 5))

            index(0, 0)
            index(1, 1)
            weights(0, 0, range(6))
            weights(1, 1, range(4))
            body(0, 0, NBLK - 1)
            with sp.Fori(0, (NBLK - 3) // 2) as i:
                for s, b in ((1, 2 * i + 1), (0, 2 * i + 2)):
                    body(b, s, 2)
                    store(b - 1, 1 - s)
            body(NBLK - 2, 1, 1)
            store(NBLK - 3, 0)
            store(NBLK - 2, 1)
            store(NBLK - 1, 0)
            sp.wait_ge(stored[0], 8 * (NBLK + 1) + 16)
            sp.wait_ge(stored[1], 8 * (NBLK - 1) + 16)

        def split_hi(eng, b, s, n):
            eng.wait_ge(w_in[s][n], 8 * (b - s) + 16)
            if eng is nc.scalar:
                eng.activation(whi[s][:, n, :], raw[s][:, n, :], ACT.Copy).then_inc(w_hi[n], 1)
            else:
                eng.tensor_copy(whi[s][:, n, :], raw[s][:, n, :]).then_inc(w_hi[n], 1)

        def split_lo(eng, b, s, n):
            eng.wait_ge(w_hi[n], b + 1)
            eng.tensor_tensor(wlo[s][:, n, :], raw[s][:, n, :], whi[s][:, n, :].bitcast(F32), ALU.subtract
                              ).then_inc(w_lo[n], 1)

        @block.gpsimd
        def _(pool):
            def may_gather(b, s):
                pool.wait_ge(idx_in[s], 8 * (b - s) + 16)
                pool.wait_ge(x_turned, b + 1)

            def gather(b, s):
                pool.indirect_dma_start(out=xg[s][:, :], out_offset=None, in_=d["h2"],
                                        in_offset=bass.IndirectOffsetOnAxis(ap=idx[s][:, 0:1].bitcast(U32), axis=0)
                                        ).then_inc(x_in[s], 16)

            for b in range(2):
                may_gather(b, b)
                gather(b, b)
            split_lo(pool, 0, 0, 1)
            split_lo(pool, 0, 0, 3)

            def body(b, s, more):
                if more:
                    split_lo(pool, b + 1, 1 - s, 1)
                    if more > 1:
                        may_gather(b + 2, s)
                    split_lo(pool, b + 1, 1 - s, 3)
                    if more > 1:
                        gather(b + 2, s)
                split_lo(pool, b, s, 5)

            blocks(pool, body)

        @block.tensor
        def _(pe):
            def turn_x(b, s):
                pe.wait_ge(x_in[s], 8 * (b - s) + 16)
                pe.wait_ge(x_lo, b + 1)
                for c in range(KT):
                    mm = pe.transpose(tx[:, c, :], xg[s][:, c * P:(c + 1) * P], ident)
                mm.then_inc(x_turned, 1)

            def gate_up(b, s):
                pe.wait_ge(x_lo, b + 2)
                pe.wait_ge(hid_done, b + 1)
                for n in range(4):
                    pe.wait_ge(w_lo[n], b + 1)
                    for j in range(2):
                        kk, c = 2 * n + j, slice(512 * j, 512 * j + 512)
                        pe.matmul(gu[s][:, :], xh[:, kk, :], whi[s][:, n, c], start=(kk == 0), stop=False)
                        pe.matmul(gu[s][:, :], xh[:, kk, :], wlo[s][:, n, c], start=False, stop=False)
                        mm = pe.matmul(gu[s][:, :], xl[:, kk, :], whi[s][:, n, c], start=False, stop=(kk == KT - 1))
                    mm.then_inc(w_used[n], 1)

            def down(b, s):
                pe.wait_ge(a_lo, b + 2)
                pe.wait_ge(y_copied, b + 1)
                for n in range(2):
                    pe.wait_ge(w_lo[4 + n], b + 1)
                    for h in range(2):
                        c = slice(512 * h, 512 * h + 512)
                        pe.matmul(yp[:, c], ah[:, n, :], whi[s][:, 4 + n, c], start=(n == 0), stop=False)
                        pe.matmul(yp[:, c], ah[:, n, :], wlo[s][:, 4 + n, c], start=False, stop=False)
                        mm = pe.matmul(yp[:, c], al[:, n, :], whi[s][:, 4 + n, c], start=False, stop=(n == 1))
                    mm.then_inc(w_used[4 + n], 1)

            def turn_a(b):
                pe.wait_ge(hid_done, b + 3)
                pe.wait_ge(a_lo, b + 1)
                for c in range(2):
                    mm = pe.transpose(ta[:, c, :], hid[:, c * P:(c + 1) * P], ident)
                mm.then_inc(a_turned, 1)

            def body(b, s, more):
                gate_up(b, s)
                if more:
                    turn_x(b + 1, 1 - s)
                if more < NBLK - 1:
                    down(b - 1, 1 - s)
                turn_a(b)

            for n in range(6):
                pe.sem_inc(w_used[n], 2)
            pe.sem_inc(x_turned, 2)
            turn_x(0, 0)
            blocks(pe, body)
            down(NBLK - 1, 0)

        @block.scalar
        def _(act):
            act.preload_act_table(ACT.Silu)
            act.sem_inc(y_copied, 1)

            def x_split(b):
                act.wait_ge(x_turned, b + 3)
                act.wait_ge(w_used[3], b + 2)
                act.activation(xh[:, :, :], tx[:, :, :], ACT.Copy).then_inc(x_hi, 1)

            def gate(b, s):
                act.wait_ge(w_used[3], b + 3)
                act.activation(act_t[:, :], gu[s][:, 0:F], ACT.Silu).then_inc(silu, 1)

            def y_copy(b, s):
                act.wait_ge(w_used[5], b + 3)
                act.wait_ge(stored[s], 8 * (b - s) + 16)
                act.activation(ys[s][:, :], yp[:, :], ACT.Copy).then_inc(y_copied, 1)

            def a_split(b):
                act.wait_ge(a_turned, b + 1)
                act.wait_ge(w_used[5], b + 2)
                act.activation(ah[:, :, :], ta[:, :, :], ACT.Copy).then_inc(a_hi, 1)

            def body(b, s, more):
                if more:
                    for n in range(4):
                        split_hi(act, b + 1, 1 - s, n)
                gate(b, s)
                if more:
                    x_split(b + 1)
                if more < NBLK - 1:
                    y_copy(b - 1, 1 - s)
                a_split(b)

            for n in range(4):
                split_hi(act, 0, 0, n)
            x_split(0)
            blocks(act, body)
            y_copy(NBLK - 1, 0)

        @block.vector
        def _(dve):
            dve.sem_inc(x_lo, 1)
            dve.sem_inc(a_lo, 1)
            dve.sem_inc(hid_done, 2)

            def x_rest(b):
                dve.wait_ge(x_hi, b + 1)
                dve.tensor_tensor(xl[:, :, :], tx[:, :, :], xh[:, :, :].bitcast(F32), ALU.subtract).then_inc(x_lo, 1)

            def hidden(b, s):
                dve.wait_ge(silu, b + 1)
                dve.wait_ge(a_lo, b + 1)
                dve.tensor_tensor(hid[:, :], gu[s][:, F:2 * F], act_t[:, :], ALU.mult).then_inc(hid_done, 1)

            def a_rest(b):
                dve.wait_ge(a_hi, b + 1)
                dve.tensor_tensor(al[:, :, :], ta[:, :, :], ah[:, :, :].bitcast(F32), ALU.subtract).then_inc(a_lo, 1)

            def body(b, s, more):
                if more:
                    split_lo(dve, b + 1, 1 - s, 0)
                    split_lo(dve, b + 1, 1 - s, 2)
                hidden(b, s)
                if more:
                    x_rest(b + 1)
                a_rest(b)
                split_hi(dve, b, s, 4)
                split_hi(dve, b, s, 5)
                split_lo(dve, b, s, 4)

            split_lo(dve, 0, 0, 0)
            split_lo(dve, 0, 0, 2)
            x_rest(0)
            blocks(dve, body)


def stage_combine_norm(k, r, x1, hi, lo):
    nc, d = k.nc, k.d
    with ExitStack() as ctx:
        yg = [[k.at(f"cm_y{n}{s}", [P, D], F32, O_W + (2 * n + s) * 4096) for s in range(2)] for n in range(2)]
        xn = [k.at(f"cm_xn{s}", [P, D], F32, O_W + (4 + s) * 4096) for s in range(2)]
        junk = [k.at(f"cm_j{s}", [P, D], F32, O_W + (6 + s) * 4096) for s in range(2)]
        norm = TileNorm(k, "cn", d["g_ple"], O_W + 8 * 4096, O_W + 9 * 4096)
        tp = [ctx.enter_context(nc.psum_tensor(f"cm_tp{s}", [P, KT, P], F32)) for s in range(2)]
        y_in = [k.sems(ctx, f"cm_in{n}0", f"cm_in{n}1") for n in range(2)]
        added, part, turned, hi_s, lo_s = k.sems(ctx, *(f"cm_{n}" for n in ("added", "part", "turned", "hi", "lo")))
        ident = k.const[:, C_ID:C_ID + P]
        block = ctx.enter_context(nc.Block())

        @block.sync
        def _(sp):
            norm.load(sp)

        @block.gpsimd
        def _(pool):
            def gather(t):
                if t >= 2:
                    pool.wait_ge(added, t - 1)
                for n in range(2):
                    pool.indirect_dma_start(out=yg[n][t % 2][:, :], out_offset=None, in_=d["y_slots"],
                                            in_offset=bass.IndirectOffsetOnAxis(ap=r.slot[:, n, t:t + 1].bitcast(U32), axis=0)
                                            ).then_inc(y_in[n][t % 2], 16)

            pool.memset(norm.nh[:, :], -0.5).then_inc(norm.half_set, 1)
            pool.wait_ge(norm.half_set, 1)
            gather(0)
            gather(1)
            for t in range(NT):
                pool.wait_ge(norm.scaled, t + 1)
                pool.tensor_tensor(norm.st[:, t, 2:3], norm.st[:, t, 1:2], norm.nh[:, :], ALU.pow).then_inc(norm.rstd, 1)
                if t + 2 < NT:
                    gather(t + 2)

        @block.vector
        def _(dve):
            def combine(t):
                for n in range(2):
                    dve.wait_ge(y_in[n][t % 2], 16 * (t // 2 + 1))
                    if n:
                        dve.wait_ge(part, t + 1)
                    dve.scalar_tensor_tensor(out=x1[:, t, :], in0=yg[n][t % 2][:, :], scalar=r.weight[:, n, t:t + 1],
                                             in1=x1[:, t, :], op0=ALU.mult, op1=ALU.add).then_inc(added if n else part, 1)

            def rest(t):
                dve.wait_ge(hi_s, t + 1)
                dve.tensor_tensor(of_tile(lo, t), tp[t % 2][:, :, :], of_tile(hi, t).bitcast(F32), ALU.subtract
                                  ).then_inc(lo_s, 1)

            combine(0)
            for t in range(NT):
                if t + 1 < NT:
                    combine(t + 1)
                if t >= 2:
                    dve.wait_ge(turned, t - 1)
                norm.norm(dve, t, x1[:, t, :], xn[t % 2][:, :])
                if t:
                    rest(t - 1)
            rest(NT - 1)

        @block.scalar
        def _(act):
            def split(t):
                act.wait_ge(turned, t + 1)
                act.activation(of_tile(hi, t), tp[t % 2][:, :, :], ACT.Copy).then_inc(hi_s, 1)

            for t in range(NT):
                act.wait_ge(added, t + 1)
                if t >= 2:
                    act.wait_ge(norm.squared, t - 1)
                norm.square(act, t, x1[:, t, :], junk[t % 2][:, :])
                if t:
                    split(t - 1)
            split(NT - 1)

        @block.tensor
        def _(pe):
            for t in range(NT):
                pe.wait_ge(norm.normed, t + 1)
                if t >= 2:
                    pe.wait_ge(lo_s, t - 1)
                for c in range(KT):
                    mm = pe.transpose(tp[t % 2][:, c, :], xn[t % 2][:, c * P:(c + 1) * P], ident)
                mm.then_inc(turned, 1)



def stage_ple(k, hi, lo, x2):
    nc, d = k.nc, k.d
    with ExitStack() as ctx:
        w = ResidentUnits(k, "pg", U_PG, [O_ST + 4096 * j for j in range(4)])
        pin = [k.at(f"pg_p{s}", [P, D], F32, O_ST + 4096 * (4 + s)) for s in range(2)]
        norm = TileNorm(k, "fn", d["g_final"], O_R2 + 10 * 4096, O_ST + 6 * 4096 + 736)
        sg, y = tile_views(k, "pg", O_R1)
        zp = [ctx.enter_context(nc.psum_tensor(f"pg_z{b}", [P, D], F32)) for b in range(2)]
        p_in = k.sems(ctx, "pg_p_in0", "pg_p_in1")
        tile_done, sig, part, added, stored = k.sems(ctx, "pg_tile", "pg_sig", "pg_part", "pg_added", "pg_stored")
        block = ctx.enter_context(nc.Block())

        @block.sync
        def _(sp):
            def store(t):
                out = d["y_prompt"][0, t * P:(t + 1) * P, :] if t < QB else d["y_sample"][0, (t - QB) * P:(t - QB + 1) * P, :]
                sp.wait_ge(norm.normed, t + 1)
                sp.dma_start(by_ktile(out), of_tile(y, t)).then_inc(stored, 16)

            w.load(sp)
            norm.load(sp)
            for t in range(NT):
                if t >= 2:
                    sp.wait_ge(part, t - 1)
                sp.dma_start(pin[t % 2][:, :], d["pp"][t * P:(t + 1) * P, :]).then_inc(p_in[t % 2], 16)
                if t >= 2:
                    store(t - 2)
            store(NT - 2)
            store(NT - 1)
            sp.wait_ge(stored, 16 * NT)

        @block.scalar
        def _(act):
            act.preload_act_table(ACT.Sigmoid)
            for n in range(8):
                w.split_hi(act, n)
            for t in range(NT):
                act.wait_ge(tile_done, t + 1)
                act.activation(of_tile(sg, t), by_ktile(zp[t % 2][:, :]), ACT.Sigmoid).then_inc(sig, 1)
                act.wait_ge(added, t + 1)
                norm.square(act, t, by_ktile(x2[:, t, :]), of_tile(sg, t))

        @block.gpsimd
        def _(pool):
            for n in range(1, 8, 2):
                w.split_lo(pool, n)
            norm.root(pool)

        @block.tensor
        def _(pe):
            for t in range(NT):
                if t >= 2:
                    pe.wait_ge(sig, t - 1)
                for c in range(2):
                    mm = pe_token_tile(pe, zp[t % 2][:, c * 512:(c + 1) * 512], hi, lo, t, w, c)
                mm.then_inc(tile_done, 1)

        @block.vector
        def _(dve):
            for n in range(0, 8, 2):
                w.split_lo(dve, n)
            for t in range(NT):
                dve.wait_ge(p_in[t % 2], 16 * (t // 2 + 1))
                dve.wait_ge(sig, t + 1)
                gated = of_tile(sg, t)
                dve.tensor_tensor(gated, gated, by_ktile(pin[t % 2][:, :]), ALU.mult).then_inc(part, 1)
                dve.wait_ge(part, t + 1)
                x = by_ktile(x2[:, t, :])
                dve.tensor_tensor(x, x, gated, ALU.add).then_inc(added, 1)
                norm.norm(dve, t, x, of_tile(y, t))


def build(nc, dram, upto=99):
    scratch = {
        "bc": ([2 * P, T], F32), "xtok": ([T, D + 256], F32), "rest": ([22 * P, T], F32),
        "ztok": ([T, D], F32), "mix_a": ([D, T], F32), "bias_line": ([N_HEADS, 512], F32),
        "h2": ([T, D], F32), "slots": ([NBLK * P, 1], I32), "y_slots": ([NBLK * P, D], F32),
        "pp": ([T, D], F32),
    }
    for name, (shape, dtype) in scratch.items():
        dram[name] = nc.dram_tensor(name, shape, dtype, kind="Internal").ap()
    k = Core(nc, dram)
    k.dt_raw = k.at("dt_raw", [P, NT, 32], F32, O_KEEP + 256)
    k.bias = k.at("bias", [P, 3, N_HEADS, BAND], F32, O_BIAS)
    stage_load_constants(k)
    hi, lo = split_pair(k, "h")
    stage_norm_transpose(k, "norm_in", dram["g_mix"], hi, lo, x_dram=dram["x"])
    stage_project_conv(k, hi, lo)
    stage_project_rest(k, hi, lo)
    stage_project_z(k, hi, lo)
    stage_bias_tables(k)
    att_hi, att_lo = split_pair(k, "att", 4)
    stage_attention(k, att_hi, att_lo)
    stage_gated(k, "ao", att_hi, att_lo, 4, U_AO, 6, add=False)
    k.clear_semaphores()
    q = SsdTiles(k)
    stage_ssd_decays(k, q)
    stage_ssd_states(k, q)
    y_hi, y_lo = split_pair(k, "y")
    stage_ssd_scan(k, q, y_hi, y_lo)
    mixed = k.at("mixed", [P, KT, T], F32, O_R2)
    stage_gated(k, "so", y_hi, y_lo, KT, U_SO, 14, add=True, out_sbuf=mixed)
    k.clear_semaphores()
    m_hi, m_lo = split_pair(k, "m")
    x1 = k.at("x1", [P, NT, D], F32, O_R2)
    r = Routing(k)
    stage_out_route(k, mixed, m_hi, m_lo, x1, r)
    stage_route(k, r)
    stage_experts(k, r)
    k.clear_semaphores()
    g_hi, g_lo = split_pair(k, "g")
    stage_combine_norm(k, r, x1, g_hi, g_lo)
    stage_ple(k, g_hi, g_lo, x1)



def _units(w_in, w_attn_out, w_ssd_out, w_out, w_ple_gate, w_ple_proj):
    def by_channel(w):
        kt, cols = w.shape[0] // P, w.shape[1]
        return w.reshape(kt, P, cols // P, P).transpose(2, 1, 0, 3).reshape(cols // P, P, kt * P)

    def by_token(w):
        kt, cols = w.shape[0] // P, w.shape[1]
        return w.reshape(kt // 2, 2, P, cols // 512, 512).transpose(3, 0, 2, 1, 4).reshape(-1, P, 1024)

    q, kk, v, z, xbc, dt, ga, gs = np.split(w_in, np.cumsum([512, 128, 128, 1024, 1280, 32, 1024]), axis=1)
    q = q.reshape(D, N_KV, GQ, HEAD).transpose(0, 2, 1, 3).reshape(D, N_HEADS * HEAD)
    ao = by_channel(w_attn_out).reshape(4, 2, P, 512).transpose(0, 2, 1, 3).reshape(4, P, 1024)
    units = [by_channel(xbc), by_channel(q), by_channel(kk), by_channel(v), by_channel(ga), by_channel(gs),
             by_token(z), ao, by_channel(w_ssd_out), by_token(w_out), by_token(w_ple_gate), by_token(w_ple_proj)]
    return np.ascontiguousarray(np.concatenate(units)), dt.reshape(KT, P, 32).transpose(1, 0, 2)


def kernel(**inputs):
    import concourse.bacc as _bacc
    from concourse.bass_utils import run_bass_kernel_spmd as _run

    a = {n: np.asarray(v) for n, v in inputs.items()}
    consts, ids, hot = host_constants()
    units, w_dt = _units(a["w_in"][0], a["w_attn_out"][0], a["w_ssd_out"][0], a["w_out"][0], a["w_ple_gate"][0],
                         a["w_ple_proj"][0])
    conv = np.concatenate([a["conv_w"][0], a["conv_b"]]).reshape(CONV + 1, 10, P).transpose(2, 1, 0)
    gu = a["w_gate_up"][0].reshape(N_EXP, 4, 2, P, 512).transpose(0, 1, 3, 2, 4).reshape(N_EXP, 4, P, 1024)
    down = a["w_down"][0].reshape(N_EXP, 2, P, D)
    arrays = {
        "x": np.concatenate([a["x_prompt"][0], a["x_sample"][0]]),
        "p": np.concatenate([a["p_prompt"][0, 0], a["p_sample"][0, 0]]),
        "units": units, "w_dt": w_dt, "conv": conv, "consts": consts, "ids": ids, "hot": hot,
        "experts": np.concatenate([gu, down], axis=1).reshape(N_EXP * 6 * P, 1024),
        "g_mix": a["g_mix"][0], "g_ffn": a["g_ffn"][0], "g_ple": a["g_ple"][0], "g_final": a["g_final"],
        "norm_g": a["ssd_norm_g"][0], "rel_bias": a["rel_bias"], "sink": a["attn_sink"][0],
        "dt_bias": np.concatenate([a["dt_bias_f"][0], a["dt_bias_b"][0]]),
        "a_log": np.concatenate([a["a_log_f"][0], a["a_log_b"][0]]), "d_skip": a["d_skip"][0],
        "router": np.concatenate([a["router_g"][0], a["router_e"][0]], axis=1).reshape(KT, P, 20).transpose(1, 0, 2),
        "router_b": np.concatenate([a["router_g_b"][0], a["router_e_b"][0]]),
    }
    arrays = {n: np.ascontiguousarray(v) for n, v in arrays.items()}
    nc = _bacc.Bacc("TRN2", target_bir_lowering=False, num_devices=1)
    dram = {n: nc.dram_tensor(n, v.shape, mybir.dt.from_np(v.dtype), kind="ExternalInput").ap() for n, v in arrays.items()}
    outs = [((1, s, D), "y_prompt" if n == 0 else "y_sample") for n, s in enumerate(SEQS)]
    for shape, name in outs:
        dram[name] = nc.dram_tensor(name, shape, F32, kind="ExternalOutput").ap()
    build(nc, dram)
    r = _run(nc, [arrays], core_ids=[0])
    return tuple(r.results[0][name] for _, name in outs)
```
